# Optimizing a Trainium2 kernel written in Bass

```python
import jax, jax.numpy as jnp
from jax import lax
import numpy as np
import math

D_MODEL = 1024
BATCH = 1
SEQ = 512
DEPTH = 1

CHUNK = 64
Q_BLOCK = 128
MIX_WIDTH = D_MODEL
POOL_WIDTH = MIX_WIDTH // 2
POOL_WINDOWS = (2, 4, 8, 16)
POOL_GROUPS = len(POOL_WINDOWS)
POOL_GROUP_DIM = POOL_WIDTH // POOL_GROUPS
ATTN_WIDTH = MIX_WIDTH - POOL_WIDTH
DIFF_HEAD_DIM = 64
V_HEAD_DIM = 2 * DIFF_HEAD_DIM
N_DIFF_HEADS = ATTN_WIDTH // V_HEAD_DIM
IN_WIDTH = POOL_WIDTH + 3 * ATTN_WIDTH
D_FF = 2816
CONV_WIDTH = 3
ROPE_THETA = 10000.0
EPS = 1e-6


def rmsnorm(x, g):
    xf = x.astype(jnp.float32)
    y = xf * lax.rsqrt(jnp.mean(xf * xf, axis=-1, keepdims=True) + EPS)
    return (y * g.astype(jnp.float32)).astype(x.dtype)

def rope_tables(positions, dtype):
    inv_freq = ROPE_THETA ** (-jnp.arange(0, DIFF_HEAD_DIM, 2, dtype=jnp.float32) / DIFF_HEAD_DIM)
    ang = positions.astype(jnp.float32)[..., None] * inv_freq
    return (jnp.cos(ang)[:, :, None, None, :].astype(dtype),
            jnp.sin(ang)[:, :, None, None, :].astype(dtype))

def apply_rope(t, cos, sin):
    t1, t2 = jnp.split(t, 2, axis=-1)
    return jnp.concatenate([t1 * cos - t2 * sin, t1 * sin + t2 * cos], axis=-1)

def multiscale_pool(p, pool_w, pool_scale):
    s = p.shape[1]
    pf = p.astype(jnp.float32)
    csum = jnp.pad(jnp.cumsum(pf, axis=1), ((0, 0), (1, 0), (0, 0)))
    t = jnp.arange(s)
    pooled = []
    for g, w in enumerate(POOL_WINDOWS):
        cs = csum[..., g * POOL_GROUP_DIM:(g + 1) * POOL_GROUP_DIM]
        upper = cs[:, 1:]
        lower = jnp.pad(cs[:, :s + 1 - w], ((0, 0), (w - 1, 0), (0, 0)))
        count = jnp.minimum(t + 1, w).astype(jnp.float32)[None, :, None]
        pooled.append((upper - lower) / count)
    d = (jnp.concatenate(pooled, axis=-1) - pf).astype(p.dtype)
    d = d.reshape(p.shape[0], s, POOL_GROUPS, POOL_GROUP_DIM)
    y = jnp.einsum('bsgc,gcd->bsgd', d, pool_w).reshape(p.shape[0], s, POOL_WIDTH)
    return y * pool_scale

def diff_attention(q, k, v, lam, lam_init, head_g):
    b, h, _, s, _ = q.shape
    scale = DIFF_HEAD_DIM ** -0.5
    outs = []
    for i in range(s // Q_BLOCK):
        q0 = i * Q_BLOCK
        end = q0 + Q_BLOCK
        qb = q[:, :, :, q0:end]
        kb = k[:, :, :, :end]
        vb = v[:, :, :end]
        scores = jnp.einsum('bhnqd,bhnkd->bhnqk', qb, kb).astype(jnp.float32) * scale
        q_chunk = (q0 + jnp.arange(Q_BLOCK)) // CHUNK
        k_chunk = jnp.arange(end) // CHUNK
        mask = k_chunk[None, :] <= q_chunk[:, None]
        probs = jax.nn.softmax(jnp.where(mask, scores, -jnp.inf), axis=-1)
        attn = probs[:, :, 0] - lam * probs[:, :, 1]
        outs.append(jnp.einsum('bhqk,bhkd->bhqd', attn.astype(v.dtype), vb))
    o = jnp.concatenate(outs, axis=2)
    o = rmsnorm(o, head_g[None, :, None, :]) * (1.0 - lam_init)
    return o.transpose(0, 2, 1, 3).reshape(b, s, ATTN_WIDTH)

def causal_dwconv(u, w, bias):
    s = u.shape[1]
    upad = jnp.pad(u, ((0, 0), (CONV_WIDTH - 1, 0), (0, 0)))
    out = bias
    for j in range(CONV_WIDTH):
        out = out + w[j] * upad[:, j:j + s]
    return out

def first_inputs(seed: int = 0) -> dict:
    key = jax.random.key(seed)
    ks = jax.random.split(key, 20)
    nrm = lambda k, shape, s: jax.random.normal(k, shape, jnp.float32) * s
    x = jax.random.normal(ks[0], (BATCH, SEQ, D_MODEL), jnp.float32)
    offset = jax.random.randint(ks[1], (BATCH,), 0, 10000, dtype=jnp.int32)
    positions = offset[:, None] + jnp.arange(SEQ, dtype=jnp.int32)[None, :]
    return {
        "x": x,
        "positions": positions,
        "norm_mix_g": 1.0 + nrm(ks[2], (DEPTH, D_MODEL), 0.05),
        "w_in": nrm(ks[3], (DEPTH, D_MODEL, IN_WIDTH), D_MODEL ** -0.5),
        "pool_w": nrm(ks[4], (DEPTH, POOL_GROUPS, POOL_GROUP_DIM, POOL_GROUP_DIM), POOL_GROUP_DIM ** -0.5),
        "pool_scale": 1.0 + nrm(ks[5], (DEPTH, POOL_WIDTH), 0.05),
        "lambda_q1": nrm(ks[6], (DEPTH, DIFF_HEAD_DIM), 0.1),
        "lambda_k1": nrm(ks[7], (DEPTH, DIFF_HEAD_DIM), 0.1),
        "lambda_q2": nrm(ks[8], (DEPTH, DIFF_HEAD_DIM), 0.1),
        "lambda_k2": nrm(ks[9], (DEPTH, DIFF_HEAD_DIM), 0.1),
        "attn_norm_g": 1.0 + nrm(ks[10], (DEPTH, N_DIFF_HEADS, V_HEAD_DIM), 0.05),
        "w_o": nrm(ks[11], (DEPTH, MIX_WIDTH, D_MODEL), MIX_WIDTH ** -0.5),
        "norm_ffn_g": 1.0 + nrm(ks[12], (DEPTH, D_MODEL), 0.05),
        "w_up": nrm(ks[13], (DEPTH, D_MODEL, 2 * D_FF), D_MODEL ** -0.5),
        "conv_w": nrm(ks[14], (DEPTH, CONV_WIDTH, 2 * D_FF), CONV_WIDTH ** -0.5),
        "conv_b": nrm(ks[15], (DEPTH, 2 * D_FF), 0.02),
        "w_down": nrm(ks[16], (DEPTH, D_FF, D_MODEL), D_FF ** -0.5),
        "norm_final_g": 1.0 + nrm(ks[17], (D_MODEL,), 0.05),
    }

def first_block(x, positions, norm_mix_g, w_in, pool_w, pool_scale, lambda_q1, lambda_k1,
              lambda_q2, lambda_k2, attn_norm_g, w_o, norm_ffn_g, w_up, conv_w, conv_b,
              w_down, norm_final_g):
    b, s, _ = x.shape
    cos, sin = rope_tables(positions, x.dtype)
    for l in range(DEPTH):
        h = rmsnorm(x, norm_mix_g[l])
        proj = h @ w_in[l]
        p, q, k, v = jnp.split(
            proj, [POOL_WIDTH, POOL_WIDTH + ATTN_WIDTH, POOL_WIDTH + 2 * ATTN_WIDTH], axis=-1)
        pool_out = multiscale_pool(p, pool_w[l], pool_scale[l])
        q = apply_rope(q.reshape(b, s, N_DIFF_HEADS, 2, DIFF_HEAD_DIM), cos, sin)
        k = apply_rope(k.reshape(b, s, N_DIFF_HEADS, 2, DIFF_HEAD_DIM), cos, sin)
        q = q.transpose(0, 2, 3, 1, 4)
        k = k.transpose(0, 2, 3, 1, 4)
        v = v.reshape(b, s, N_DIFF_HEADS, V_HEAD_DIM).transpose(0, 2, 1, 3)
        lam_init = 0.8 - 0.6 * float(np.exp(-0.3 * l))
        lam = (jnp.exp(jnp.sum(lambda_q1[l].astype(jnp.float32) * lambda_k1[l].astype(jnp.float32)))
               - jnp.exp(jnp.sum(lambda_q2[l].astype(jnp.float32) * lambda_k2[l].astype(jnp.float32)))
               + lam_init)
        attn_out = diff_attention(q, k, v, lam, lam_init, attn_norm_g[l])
        mix = jnp.concatenate([pool_out, attn_out], axis=-1) @ w_o[l]
        x = x + mix
        h = rmsnorm(x, norm_ffn_g[l])
        u = causal_dwconv(h @ w_up[l], conv_w[l], conv_b[l])
        gate, val = jnp.split(u, 2, axis=-1)
        x = x + (jax.nn.silu(gate) * val) @ w_down[l]
    return rmsnorm(x, norm_final_g)


PLE_DIM = 256
ATT_HEADS = 8
ATT_HEAD_DIM = 64
KV_LATENT = 128
IDX_HEADS = 8
IDX_HEAD_DIM = 64
TOPK_MAX = 256
ATT_SCALE = ATT_HEAD_DIM ** -0.5
IDX_W_SCALE = (IDX_HEADS ** -0.5) * (IDX_HEAD_DIM ** -0.5)
REL_BUCKETS = 32
REL_MAX_DIST = 128
HG_HEADS = 4
HG_KEY_DIM = 128
HG_VAL_DIM = 128
ATT_WIDTH = ATT_HEADS * ATT_HEAD_DIM
IDX_Q_WIDTH = IDX_HEADS * IDX_HEAD_DIM
HG_KW = HG_HEADS * HG_KEY_DIM
HG_VW = HG_HEADS * HG_VAL_DIM
IN_SPLITS = (ATT_WIDTH, KV_LATENT, IDX_Q_WIDTH, IDX_HEAD_DIM, IDX_HEADS, HG_KW, HG_KW, HG_VW, HG_VW, D_MODEL, D_MODEL)
N_IN = sum(IN_SPLITS)


def rms_norm(x, g):
    xf = x.astype(jnp.float32)
    y = xf * lax.rsqrt(jnp.mean(xf * xf, axis=-1, keepdims=True) + EPS)
    return (y * g.astype(jnp.float32)).astype(x.dtype)

def swiglu(x, w_gate, w_up, w_down):
    return (jax.nn.silu(x @ w_gate) * (x @ w_up)) @ w_down

def split_cols(a):
    outs = []
    off = 0
    for w in IN_SPLITS:
        outs.append(a[..., off:off + w])
        off += w
    return outs

def rel_bucket(dist):
    max_exact = REL_BUCKETS // 2
    d_f = jnp.maximum(dist, 1).astype(jnp.float32)
    log_b = max_exact + (jnp.log(d_f / max_exact) / math.log(REL_MAX_DIST / max_exact)
                         * (REL_BUCKETS - max_exact)).astype(jnp.int32)
    return jnp.where(dist < max_exact, dist, jnp.minimum(log_b, REL_BUCKETS - 1))

def dsa_branch(q, c_kv, q_idx, k_idx, w_idx, w_uk, w_uv, rel_bias):
    B_, S_ = q.shape[0], q.shape[1]
    topk = min(TOPK_MAX, S_ // 4)
    nblk = S_ // Q_BLOCK
    q_lat = jnp.einsum('bshd,hcd->bshc', q, w_uk)
    key_pos = jnp.arange(S_, dtype=jnp.int32)

    def to_blocks(a):
        return jnp.moveaxis(a.reshape((B_, nblk, Q_BLOCK) + a.shape[2:]), 1, 0)

    def block(args):
        ql, qi, wi, t_pos = args
        dots = jnp.einsum('bqhd,bsd->bqhs', qi, k_idx)
        score = jnp.einsum('bqh,bqhs->bqs', wi, jax.nn.relu(dots)).astype(jnp.float32)
        causal = key_pos[None, :] <= t_pos[:, None]
        score = jnp.where(causal[None], score, -jnp.inf)
        _, idx = lax.top_k(score, topk)
        valid = idx <= t_pos[None, :, None]
        c_sel = jax.vmap(lambda c, i: c[i])(c_kv, idx)
        dist = jnp.maximum(t_pos[None, :, None] - idx, 0)
        bias = jnp.moveaxis(rel_bias[rel_bucket(dist)], -1, 2)
        logits = (jnp.einsum('bqhc,bqkc->bqhk', ql.astype(jnp.float32), c_sel.astype(jnp.float32)) * ATT_SCALE
                  + bias.astype(jnp.float32))
        logits = jnp.where(valid[:, :, None, :], logits, -jnp.inf)
        probs = jax.nn.softmax(logits, axis=-1).astype(c_kv.dtype)
        return jnp.einsum('bqhk,bqkc->bqhc', probs, c_sel)

    t_blocks = jnp.arange(S_, dtype=jnp.int32).reshape(nblk, Q_BLOCK)
    o_lat = lax.map(block, (to_blocks(q_lat), to_blocks(q_idx), to_blocks(w_idx), t_blocks))
    o_lat = jnp.moveaxis(o_lat, 0, 1).reshape(B_, S_, ATT_HEADS, KV_LATENT)
    o = jnp.einsum('bshc,hcd->bshd', o_lat, w_uv)
    return o.reshape(B_, S_, ATT_WIDTH)

def hgrn2_chunkwise(q, k, v, log_f):
    B_, S_, H_, DK_ = q.shape
    DV_ = v.shape[-1]
    n = S_ // CHUNK

    def chunks(a):
        return jnp.moveaxis(a.astype(jnp.float32).reshape(B_, n, CHUNK, H_, a.shape[-1]), 1, 0)

    tri = jnp.tril(jnp.ones((CHUNK, CHUNK), dtype=bool))

    def step(state, inp):
        qc, kc, vc, gc = inp
        G = jnp.cumsum(gc, axis=1)
        o_inter = jnp.einsum('bthk,bhkv->bthv', qc * jnp.exp(G), state)
        diff = G[:, :, None] - G[:, None, :]
        decay = jnp.exp(jnp.where(tri[None, :, :, None, None], diff, -jnp.inf))
        A = jnp.einsum('bthk,bshk,btshk->bhts', qc, kc, decay)
        o_intra = jnp.einsum('bhts,bshv->bthv', A, vc)
        G_last = G[:, -1]
        k_dec = kc * jnp.exp(G_last[:, None] - G)
        new_state = jnp.exp(G_last)[..., None] * state + jnp.einsum('bshk,bshv->bhkv', k_dec, vc)
        return new_state, o_inter + o_intra

    s0 = jnp.zeros((B_, H_, DK_, DV_), jnp.float32)
    _, o = lax.scan(step, s0, (chunks(q), chunks(k), chunks(v), chunks(log_f)))
    return jnp.moveaxis(o, 0, 1).reshape(B_, S_, H_, DV_)

def second_inputs(seed: int = 0) -> dict:
    key = jax.random.key(seed)
    ks = jax.random.split(key, 40)

    def nrm(k, shape, scale):
        return jax.random.normal(k, shape, jnp.float32) * scale

    def gain(k, shape):
        return 1.0 + 0.05 * jax.random.normal(k, shape, jnp.float32)

    L = DEPTH
    D = D_MODEL
    return {
        'x': nrm(ks[0], (BATCH, SEQ, D), 1.0),
        'p': nrm(ks[1], (DEPTH, BATCH, SEQ, PLE_DIM), 1.0),
        'rel_bias': nrm(ks[2], (REL_BUCKETS, ATT_HEADS), 0.1),
        'hgrn_lb': nrm(ks[3], (DEPTH + 1, HG_KW), 1.0),
        'ffn1_pre_g': gain(ks[4], (L, D)),
        'ffn1_post_g': gain(ks[5], (L, D)),
        'ffn1_w_gate': nrm(ks[6], (L, D, D_FF), D ** -0.5),
        'ffn1_w_up': nrm(ks[7], (L, D, D_FF), D ** -0.5),
        'ffn1_w_down': nrm(ks[8], (L, D_FF, D), D_FF ** -0.5),
        'mix_pre_g': gain(ks[9], (L, D)),
        'mix_post_g': gain(ks[10], (L, D)),
        'w_in': nrm(ks[11], (L, D, N_IN), D ** -0.5),
        'kv_norm_g': gain(ks[12], (L, KV_LATENT)),
        'kidx_norm_g': gain(ks[13], (L, IDX_HEAD_DIM)),
        'w_uk': nrm(ks[14], (L, ATT_HEADS, KV_LATENT, ATT_HEAD_DIM), KV_LATENT ** -0.5),
        'w_uv': nrm(ks[15], (L, ATT_HEADS, KV_LATENT, ATT_HEAD_DIM), KV_LATENT ** -0.5),
        'hgrn_norm_g': gain(ks[16], (L, HG_VAL_DIM)),
        'w_br_a': nrm(ks[17], (L, ATT_WIDTH, D), ATT_WIDTH ** -0.5),
        'w_br_b': nrm(ks[18], (L, HG_VW, D), HG_VW ** -0.5),
        'b_gate': nrm(ks[19], (L, 2 * D), 0.02),
        'w_out': nrm(ks[20], (L, D, D), D ** -0.5),
        'ffn2_pre_g': gain(ks[21], (L, D)),
        'ffn2_post_g': gain(ks[22], (L, D)),
        'ffn2_w_gate': nrm(ks[23], (L, D, D_FF), D ** -0.5),
        'ffn2_w_up': nrm(ks[24], (L, D, D_FF), D ** -0.5),
        'ffn2_w_down': nrm(ks[25], (L, D_FF, D), D_FF ** -0.5),
        'ple_pre_g': gain(ks[26], (L, D)),
        'ple_post_g': gain(ks[27], (L, D)),
        'w_ple_gate': nrm(ks[28], (L, D, D), D ** -0.5),
        'w_ple_proj': nrm(ks[29], (L, PLE_DIM, D), PLE_DIM ** -0.5),
    }

def second_block(x, p, rel_bias, hgrn_lb, ffn1_pre_g, ffn1_post_g, ffn1_w_gate, ffn1_w_up, ffn1_w_down,
              mix_pre_g, mix_post_g, w_in, kv_norm_g, kidx_norm_g, w_uk, w_uv, hgrn_norm_g,
              w_br_a, w_br_b, b_gate, w_out, ffn2_pre_g, ffn2_post_g, ffn2_w_gate, ffn2_w_up, ffn2_w_down,
              ple_pre_g, ple_post_g, w_ple_gate, w_ple_proj):
    B_, S_, D = x.shape
    lower_bounds = jnp.cumsum(jax.nn.softmax(hgrn_lb.astype(jnp.float32), axis=0), axis=0)
    h = x
    for i in range(DEPTH):
        h = h + 0.5 * rms_norm(swiglu(rms_norm(h, ffn1_pre_g[i]), ffn1_w_gate[i], ffn1_w_up[i], ffn1_w_down[i]),
                               ffn1_post_g[i])
        u = rms_norm(h, mix_pre_g[i])
        proj = u @ w_in[i]
        (q_a, c_kv, q_idx, k_idx, w_idx, q_h, f_h, i_h, g_h, gate_a, gate_b) = split_cols(proj)
        c_kv = rms_norm(c_kv, kv_norm_g[i])
        k_idx = rms_norm(k_idx, kidx_norm_g[i])
        y_a = dsa_branch(q_a.reshape(B_, S_, ATT_HEADS, ATT_HEAD_DIM), c_kv,
                         q_idx.reshape(B_, S_, IDX_HEADS, IDX_HEAD_DIM), k_idx, w_idx * IDX_W_SCALE,
                         w_uk[i], w_uv[i], rel_bias)
        lb = lower_bounds[i]
        f = (lb + (1.0 - lb) * jax.nn.sigmoid(f_h.astype(jnp.float32))).reshape(B_, S_, HG_HEADS, HG_KEY_DIM)
        o_h = hgrn2_chunkwise(jax.nn.silu(q_h).reshape(B_, S_, HG_HEADS, HG_KEY_DIM), 1.0 - f,
                              i_h.reshape(B_, S_, HG_HEADS, HG_VAL_DIM), jnp.log(f))
        o_h = rms_norm(o_h, hgrn_norm_g[i]) * jax.nn.silu(g_h.astype(jnp.float32).reshape(B_, S_, HG_HEADS, HG_VAL_DIM))
        y_b = o_h.reshape(B_, S_, HG_VW).astype(x.dtype)
        merged = (jax.nn.sigmoid(gate_a + b_gate[i, :D]) * (y_a @ w_br_a[i])
                  + jax.nn.sigmoid(gate_b + b_gate[i, D:]) * (y_b @ w_br_b[i]))
        h = h + rms_norm(merged @ w_out[i], mix_post_g[i])
        h = h + 0.5 * rms_norm(swiglu(rms_norm(h, ffn2_pre_g[i]), ffn2_w_gate[i], ffn2_w_up[i], ffn2_w_down[i]),
                               ffn2_post_g[i])
        ple_gate = jax.nn.sigmoid(rms_norm(h, ple_pre_g[i]) @ w_ple_gate[i])
        h = h + rms_norm(ple_gate * (p[i] @ w_ple_proj[i]), ple_post_g[i])
    return h


def setup_inputs(seed=0):
    out = dict(first_inputs(seed))
    for name, value in second_inputs(seed + 1).items():
        if name != "x":
            out[name + "_2"] = value
    return out


def reference(
    x, positions, norm_mix_g, w_in, pool_w, pool_scale, lambda_q1, lambda_k1, lambda_q2,
    lambda_k2, attn_norm_g, w_o, norm_ffn_g, w_up, conv_w, conv_b, w_down, norm_final_g, p_2,
    rel_bias_2, hgrn_lb_2, ffn1_pre_g_2, ffn1_post_g_2, ffn1_w_gate_2, ffn1_w_up_2,
    ffn1_w_down_2, mix_pre_g_2, mix_post_g_2, w_in_2, kv_norm_g_2, kidx_norm_g_2, w_uk_2,
    w_uv_2, hgrn_norm_g_2, w_br_a_2, w_br_b_2, b_gate_2, w_out_2, ffn2_pre_g_2, ffn2_post_g_2,
    ffn2_w_gate_2, ffn2_w_up_2, ffn2_w_down_2, ple_pre_g_2, ple_post_g_2, w_ple_gate_2,
    w_ple_proj_2,
):
    x = first_block(
        x, positions, norm_mix_g, w_in, pool_w, pool_scale, lambda_q1, lambda_k1, lambda_q2,
        lambda_k2, attn_norm_g, w_o, norm_ffn_g, w_up, conv_w, conv_b, w_down, norm_final_g,
    )
    return second_block(
        x, p_2, rel_bias_2, hgrn_lb_2, ffn1_pre_g_2, ffn1_post_g_2, ffn1_w_gate_2, ffn1_w_up_2,
        ffn1_w_down_2, mix_pre_g_2, mix_post_g_2, w_in_2, kv_norm_g_2, kidx_norm_g_2, w_uk_2,
        w_uv_2, hgrn_norm_g_2, w_br_a_2, w_br_b_2, b_gate_2, w_out_2, ffn2_pre_g_2,
        ffn2_post_g_2, ffn2_w_gate_2, ffn2_w_up_2, ffn2_w_down_2, ple_pre_g_2, ple_post_g_2,
        w_ple_gate_2, w_ple_proj_2,
    )


_drawn_inputs = setup_inputs


def setup_inputs(seed=0):
    import zlib

    import numpy as np

    out = dict(_drawn_inputs(seed))
    spreads = {}
    factors = {'lambda_k2': 6.949,
     'conv_b': 2.762,
     'rel_bias_2': 4.572,
     'kv_norm_g_2': 3.614,
     'kidx_norm_g_2': 3.128,
     'b_gate_2': 8.0,
     'ffn2_pre_g_2': 2.889,
     'ffn2_post_g_2': 4.305,
     'ple_pre_g_2': 18.262,
     'hgrn_lb_2': 3.087,
     'hgrn_norm_g_2': 4.877,
     'ple_post_g_2': 3.143}
    for name, (base, spread) in spreads.items():
        noise = np.random.default_rng([zlib.crc32(name.encode()), seed]).standard_normal(out[name].shape)
        drawn = base * np.exp(spread * noise) if base else spread * noise
        out[name] = __import__('jax').numpy.asarray(drawn.astype(out[name].dtype))
    for name, factor in factors.items():
        out[name] = (out[name] * factor).astype(out[name].dtype)
    return out
```

```python
from contextlib import ExitStack

import numpy as np

import concourse.bass as bass
from concourse import mybir

F32 = mybir.dt.float32
F32R = mybir.dt.float32r
I32 = mybir.dt.int32
ALU = mybir.AluOpType
ACT = mybir.ActivationFunctionType
AX_X = mybir.AxisListType.X

P = 128
T = 512
D = 1024
DC = D // P
FF = 2816
FC = FF // P
QB = T // P
EPS = 1e-6
HEADS = 4
DSA_HEADS = 8
DIFF_SCALE = 64 ** -0.5
ATT_SCALE = 64 ** -0.5
IDX_W_SCALE = (8 ** -0.5) * (64 ** -0.5)
TOPK = 128
LAM_INIT = 0.2
WINDOWS = (2, 4, 8, 16)
PAD = max(WINDOWS)
NEG = -1e30
TAKEN = -3e38
LEVELS = (1, 2, 4, 8, 16, 32, 64, 128, 256)
DOWN_CHUNKS = FC // 2
SLOT = DOWN_CHUNKS * P
RAW_SLOTS = 4
SPLIT_SLOTS = 2
BANKS = 4
AUX_BANKS = 3
BIAS_COLS = 640

PARAMS = {}
_at = 0
for _name, _n in (("norm_mix_g", 8), ("norm_ffn_g", 8), ("norm_final_g", 8), ("pool_scale", 4),
                  ("attn_norm_g", 4), ("conv_w0", 44), ("conv_w1", 44), ("conv_w2", 44), ("conv_b", 44),
                  ("ffn1_pre_g", 8), ("ffn1_post_g", 8), ("mix_pre_g", 8), ("mix_post_g", 8),
                  ("kv_norm_g", 1), ("kidx_norm_g", 1), ("hgrn_norm_g", 1), ("b_gate", 16),
                  ("ffn2_pre_g", 8), ("ffn2_post_g", 8), ("ple_pre_g", 8), ("ple_post_g", 8),
                  ("hgrn_lb0", 4), ("hgrn_lb1", 4), ("inv_freq", 1), ("eps", 1)):
    PARAMS[_name] = (_at, _n)
    _at += _n
N_PARAMS = _at

TILES2 = (["ckv", "kidx", "widx"] + [f"qi{t}" for t in range(4)] + [f"qa{t}" for t in range(4)]
          + [f"i{t}" for t in range(4)] + [f"qh{t}" for t in range(4)] + [f"gh{t}" for t in range(4)]
          + [f"fh{t}" for t in range(4)] + [f"gate{t}" for t in range(16)])
STAGES = (("proj1", 16, DC), ("wo", DC, DC), ("up1", 2 * FC, DC), ("down1", 2 * DC, DOWN_CHUNKS),
          ("up2", 2 * FC, DC), ("down2", 2 * DC, DOWN_CHUNKS), ("proj2", len(TILES2), DC),
          ("branch", 2 * DC, 4), ("out", DC, DC),
          ("up3", 2 * FC, DC), ("down3", 2 * DC, DOWN_CHUNKS), ("pproj", 2, DC), ("ple", DC, DC))
UNIT = {}
_at = 0
for _name, _n, _c in STAGES:
    UNIT[_name] = (_at, _n, _c)
    _at += _n

BLOCKS_OF = [c for _, n, c in STAGES for _i in range(n)]

TILE = {}


def _tiles(name, n):
    for i in range(n):
        TILE[name, i] = len(TILE)


_tiles("proj1", 16)
_tiles("attn", HEADS)
_tiles("wo", DC)
_tiles("up1", 2 * FC)
_tiles("down1", DC)
_tiles("up2", 2 * FC)
_tiles("down2", DC)
_tiles("proj2", len(TILES2))
_tiles("olat", DSA_HEADS)
_tiles("hgrn", HEADS)
_tiles("branch", 2 * DC)
_tiles("out", DC)
_tiles("up3", 2 * FC)
_tiles("down3", DC)
_tiles("pproj", DC)
_tiles("ple", DC)

AUX = {}


def _aux(*name):
    AUX[name] = len(AUX)


def aux_of_proj1(t):
    return ("rope", t) if t < 8 else ("vtok", t - 8) if t < 12 else ("pool", t - 12)


for _t in range(16):
    if _t:
        _aux(*aux_of_proj1(_t - 1))
_aux(*aux_of_proj1(15))
for _a in range(17):
    if _a < 16:
        _aux("score", _a, 0)
        _aux("score", _a, 1)
        _aux("bias", _a)
    if _a:
        _aux("turn", _a - 1)
IDX_STEPS = [(i, h) for i in (3, 2, 1) for h in range(DSA_HEADS)]
AFTER2 = {n: [] for n in range(len(TILES2))}
AFTER2[1].append(("stat", "ckv"))
AFTER2[2].append(("stat", "kidx"))
AFTER2[3].append(("wturn", 0))
AFTER2[4].append(("ckvtok", 0))
for _t in range(4):
    AFTER2[8 + _t] += [("qlat", 2 * _t), ("qlat", 2 * _t + 1)]
    AFTER2[12 + _t].append(("vturn", _t))
for _s in range(len(IDX_STEPS)):
    AFTER2[7 + _s].append(("idx", _s))
for _n in AFTER2:
    for _ev in AFTER2[_n]:
        if _ev[0] != "stat":
            _aux(*_ev)
for _a in range(35):
    if _a < 32:
        _aux("logit", _a)
    if 1 <= _a <= 32:
        _aux("turn2", _a - 1)
    if _a >= 10 and _a % 8 == 2:
        _aux("ya", (_a - 10) // 8)
for _h in range(HEADS):
    _aux("pair0", _h)
    for _l in range(len(LEVELS)):
        _aux("pair", _h, _l)

STAT = {n: i for i, n in enumerate(
    ["norm1"] + [f"head{h}" for h in range(4)] + ["norm2", "final1", "pre1", "post1", "mixpre", "ckv", "kidx"]
    + [f"hgrn{h}" for h in range(4)] + ["postmix", "pre2", "post2", "plepre", "plepost"])}
SQUARE = {n: 8 * i for i, n in enumerate(
    ["norm1", "norm2", "final1", "pre1", "post1", "mixpre", "postmix", "pre2", "post2", "plepre", "plepost"])}
SPLIT = {}
_at = 0
for _name, _n in (("norm1", 8), ("mix1", 8), ("norm2", 8), ("pre1", 8), ("mixpre", 8), ("y", 8), ("merged", 8),
                  ("pre2", 8), ("p", 2), ("plepre", 8)):
    SPLIT[_name] = _at
    _at += _n


def bucket(dist):
    d_f = np.maximum(dist, 1).astype(np.float32)
    log_b = 16 + (np.log(d_f / np.float32(16)) / np.float32(np.log(8.0)) * np.float32(16)).astype(np.int32)
    return np.where(dist < 16, dist, np.minimum(log_b, 31))


def constants():
    i = np.arange(P)
    ident = np.eye(P, dtype=np.float32)
    rot = np.zeros((P, P), np.float32)
    for g in (0, 64):
        for j in range(32):
            rot[g + j + 32, g + j] = -1.0
            rot[g + j, g + j + 32] = 1.0
    onehot = np.zeros((P, BIAS_COLS), np.float32)
    onehot[bucket(np.maximum(T - 1 - np.arange(BIAS_COLS), 0)), np.arange(BIAS_COLS)] = 1.0
    count = np.ones((P, len(WINDOWS), PAD), np.float32)
    for g, w in enumerate(WINDOWS):
        count[:, g, :] = (1.0 / np.minimum(np.arange(PAD) + 1, w)).astype(np.float32)
    tri = np.where(i[None, :] > i[:, None], np.float32(-1e38), np.float32(0)).astype(np.float32)
    masks = np.zeros((P, 8, P), np.int32)
    masks[:, 0, :] = np.eye(P, dtype=np.int32)
    for l in range(7):
        b = LEVELS[l]
        s, t = i[:, None], i[None, :]
        masks[:, l + 1, :] = (s // (2 * b) == t // (2 * b)) & (s % (2 * b) < b) & (t % (2 * b) >= b)
    resets = np.ones((P, 3, T), np.float32)
    for n, seg in enumerate((64, 128, 256)):
        resets[:, n, ::seg] = 0.0
    return {"c_ident": ident, "c_ones": np.ones((P, P), np.float32), "c_rot": rot, "c_onehot": onehot[:32],
            "c_count": count.reshape(P, -1), "c_tri": tri, "c_masks": masks.reshape(P, -1),
            "c_resets": resets.reshape(P, -1)}

ROUND = 12582912.0
PI_BELOW = 3.1415925
TURN_PARTS = (6.28125, 8117 / 2 ** 22, float(2 * np.pi - 6.28125 - 8117 / 2 ** 22))


def decays(h, l):
    return 12 * h + (l + 1 if l < 6 else 6 + 2 * (l - 5))


LAST_UNIT = sum(n for _, n, _ in STAGES)


def two_blocks(nc, ins, spill, bias_rows, out):
    with ExitStack() as ctx:
        base = (nc.sbuf_base + 31) // 32 * 32
        arena_bytes = (nc.sbuf_usable_end - base) // 32 * 32 - 64
        ctx.enter_context(nc.sbuf_tensor("arena", [P, arena_bytes // 4], F32))
        limit = base + arena_bytes

        def placer(start, end):
            at = [start]

            def put(name, shape, dtype=F32):
                size = (int(np.prod(shape[1:])) * 4 + 31) // 32 * 32
                tensor = nc.alloc_sbuf_tensor_at(name, shape, dtype, offset=at[0])
                at[0] += size
                assert at[0] <= end, (name, at[0] - end)
                return tensor

            put.at = at
            return put

        keep = placer(base, limit)
        raw = keep("raw", [P, RAW_SLOTS, SLOT])
        w_hi = keep("w_hi", [P, SPLIT_SLOTS, SLOT], F32R)
        w_lo = keep("w_lo", [P, SPLIT_SLOTS, SLOT], F32R)
        x = keep("x", [P, DC, T])
        a_hi = keep("a_hi", [P, DC, T], F32R)
        y_at = keep.at[0]
        a_lo = keep("a_lo", [P, DC, T], F32R)
        room_at = keep.at[0]
        h_hi = keep("h_hi", [P, FC, T], F32R)
        h_lo = keep("h_lo", [P, FC, T], F32R)
        room_end = keep.at[0]
        par = keep("par", [P, N_PARAMS])
        ident = keep("ident", [P, P])
        ones = keep("ones", [P, P])
        sum_sq = keep("sum_sq", [P, T])
        sq = keep("sq", [P, 2, T])
        chunk = keep("chunk", [P, 2, T])
        root = keep("root", [P, T])
        rstd = keep("rstd", [P, T])
        gate = keep("gate", [P, T])
        val = keep("val", [P, T])
        silu = keep("silu", [P, T])
        small = keep("small", [P, 64])
        y = placer(y_at, room_at)("y", [P, DC, T])
        spill_slot = [gate, val, silu]

        r1 = placer(room_at, room_end)
        rot = r1("rot", [P, P])
        pool_w = r1("pool_w", [P, 4, P])
        count = r1("count", [P, 4, PAD])
        lam_in = r1("lam_in", [P, 4, 64])
        cos = r1("cos", [P, T])
        sin = r1("sin", [P, T])
        q1 = r1("q1", [P, HEADS, T])
        k1 = r1("k1", [P, HEADS, T])
        v1 = r1("v1", [P, QB, HEADS, P])
        o1 = r1("o1", [P, HEADS, T])
        neg_row = r1("neg_row", [1, P])
        one_row = r1("one_row", [1, 64])
        onehot = r1("onehot", [32, BIAS_COLS])
        rel = r1("rel", [32, DSA_HEADS])
        rel_wide = r1("rel_wide", [32, DSA_HEADS, P])
        bias_slot = r1("bias_slot", [P, 2, BIAS_COLS])
        before_softmax = r1.at[0]
        pos_i = r1("pos_i", [P, T], I32)
        angle = r1("angle", [P, T])
        turns = r1("turns", [P, T])
        unrot = r1("unrot", [P, 2, T])
        rope_a = r1("rope_a", [P, T])
        v1t = r1("v1t", [P, 2, T])
        pool_in = r1("pool_in", [P, 2, PAD + T])
        pool_s = r1("pool_s", [P, 2, PAD + T])
        pool_d = r1("pool_d", [P, 2, T])
        r1 = placer(before_softmax, room_end)
        prob = r1("prob", [P, 2, 2, T])
        attn = r1("attn", [P, 2, T])
        attn_t = r1("attn_t", [P, 2, T])

        r2 = placer(room_at, room_end)
        v2 = r2("v2", [P, QB, HEADS, P])
        r2_split = r2.at[0]
        ckv_raw = r2("ckv_raw", [P, T])
        ckv = r2("ckv", [P, T])
        ckv_tok = r2("ckv_tok", [P, QB, P])
        kidx_raw = r2("kidx_raw", [P, T])
        kidx = r2("kidx", [P, T])
        widx_t = r2("widx_t", [P, T])
        widx = r2("widx", [P, QB, DSA_HEADS])
        wuk = r2("wuk", [P, 4, P])
        wuv = r2("wuv", [P, DSA_HEADS, 64])
        tri = r2("tri", [P, P])
        qlat = r2("qlat", [P, DSA_HEADS, T])
        score = [tri] + [r2(f"score{i}", [P, (i + 1) * P]) for i in range(1, QB)]
        best = r2("best", [P, 8])
        t_bias = r2("t_bias", [P, 2, T])
        r2_under = placer(r2.at[0], room_end)
        qa = r2_under("qa", [P, 2, T])
        relu = r2_under("relu", [P, 2, T])
        i_t = r2_under("i_t", [P, 2, T])
        logit = r2("logit", [P, 2, T])
        prob2 = r2("prob2", [P, 2, T])
        attn2 = r2("attn2", [P, 2, T])
        attn2_t = r2("attn2_t", [P, 2, T])
        olat = r2("olat", [P, 2, T])
        qidx = r2("qidx", [P, 4, T])
        r3 = placer(r2_split, room_end)
        masks = r3("masks", [P, 8, P], I32)
        resets = r3("resets", [P, 3, T])
        hq = r3("hq", [P, 2, T])
        hf = r3("hf", [P, 2, T])
        hk = r3("hk", [P, 2, T])
        logf = r3("logf", [P, T])
        run = r3("run", [P, 2, 3, T])
        diff = r3("diff", [P, 2, T])
        decay = r3("decay", [P, 2, T])
        qk = r3("qk", [P, 2, T])
        pair_d = r3("pair_d", [P, 2, T])
        pair_1 = r3("pair_1", [P, 2, 2, P])
        pair_2 = r3("pair_2", [P, 2, 2, 2 * P])
        oh = r3("oh", [P, HEADS, T])
        hg = r3("hg", [P, HEADS, T])
        r4 = placer(room_at + 8 * T * 4, room_at + FC * T * 4)
        gates_in = r4("gates_in", [P, 4, T])
        gated = r4("gated", [P, 2, T])
        pe_in = placer(y_at - 4 * T * 4, y_at)("pe_in", [P, 2, T])
        p_proj = placer(room_at, room_end)("p_proj", [P, DC, T])

        bank = [ctx.enter_context(nc.psum_tensor(f"bank{i}", [P, T], F32)) for i in range(8)]
        stat_bank = bank[7]

        def tile_bank(stage, i):
            return bank[TILE[stage, i] % BANKS]

        def aux_bank(*name):
            return bank[BANKS + AUX[name] % AUX_BANKS]

        def tile_sem(stage, i):
            return bank_free[TILE[stage, i] % BANKS]

        def tile_read(stage, i):
            return tile_sem(stage, i), TILE[stage, i] // BANKS + 1

        def tile_done(stage, i):
            per_tile = 2 if stage.startswith("down") else 1
            return unit_done, UNIT[stage][0] + per_tile * (i + 1)

        def aux_sem(*name):
            return aux_free[AUX[name] % AUX_BANKS]

        def aux_read(*name):
            return aux_sem(*name), AUX[name] // AUX_BANKS + 1

        def prm(name, i=0, rows=P):
            return par[0:rows, PARAMS[name][0] + i:PARAMS[name][0] + i + 1]

        def sem(name):
            return ctx.enter_context(nc.semaphore(name))

        raw_loaded = [sem(f"raw_loaded{i}") for i in range(RAW_SLOTS)]
        unit_high = sem("unit_high")
        unit_split = sem("unit_split")
        unit_done = sem("unit_done")
        bank_free = [sem(f"bank_free{i}") for i in range(BANKS)]
        aux_ready = sem("aux_ready")
        aux_free = [sem(f"aux_free{i}") for i in range(AUX_BANKS)]
        head_ready = sem("head_ready")
        total_ready = sem("total_ready")
        root_ready = sem("root_ready")
        rstd_ready = sem("rstd_ready")
        sq_ready = sem("sq_ready")
        sum_added = sem("sum_added")
        head_sq = sem("head_sq")
        chunk_ready = sem("chunk_ready")
        hi_ready = sem("hi_ready")
        act_ready = sem("act_ready")
        x_ready = sem("x_ready")
        y_ready = sem("y_ready")
        x_loaded = sem("x_loaded")
        const_loaded = sem("const_loaded")
        const1_loaded = sem("const1_loaded")
        const2_loaded = sem("const2_loaded")
        const3_loaded = sem("const3_loaded")
        p_loaded = sem("p_loaded")
        dve_step = sem("dve_step")
        act_step = sem("act_step")
        trig_in = sem("trig_in")
        trig = sem("trig")
        lam_sum = sem("lam_sum")
        lam_exp = sem("lam_exp")
        rel_set = sem("rel_set")
        rope_done = sem("rope_done")
        pool_ready = sem("pool_ready")
        neg_max = sem("neg_max")
        attn_ready = sem("attn_ready")
        bias_out = [sem(f"bias_out{i}") for i in range(2)]
        high_done = sem("high_done")
        silu_ready = sem("silu_ready")
        gate_ready = sem("gate_ready")
        hidden_ready = sem("hidden_ready")
        norm_ready = sem("norm_ready")
        relu_used = sem("relu_used")
        spill_out = [sem(f"spill_out{i}") for i in range(3)]
        bias_in = [sem(f"bias_in{i}") for i in range(2)]
        logit_max = sem("logit_max")
        exp2_done = sem("exp2_done")
        attn2_ready = sem("attn2_ready")
        h_loaded = [sem(f"h_loaded{i}") for i in range(2)]
        hg_loaded = sem("hg_loaded")
        f_ready = sem("f_ready")
        logf_ready = sem("logf_ready")
        k_ready = sem("k_ready")
        diff_ready = sem("diff_ready")
        decay_ready = sem("decay_ready")
        qk_ready = sem("qk_ready")
        gates_loaded = [sem(f"gates_loaded{i}") for i in range(2)]
        out_ready = sem("out_ready")
        stored = sem("stored")

        block = ctx.enter_context(nc.Block())

        @block.sync
        def _(sp):
            def load_unit(src, u, slot, size):
                sp.dma_start(raw[:, slot, 0:size], src).then_inc(raw_loaded[slot], 16)

            def load_stage(name):
                first, n, blocks = UNIT[name]
                src = ins["w_" + name]
                size = blocks * P
                straight = max(0, RAW_SLOTS - first)
                for i in range(straight):
                    load_unit(src[i], first + i, (first + i) % RAW_SLOTS, size)
                loops = (n - straight) // RAW_SLOTS
                if loops:
                    with sp.Fori(0, loops) as it:
                        for j in range(RAW_SLOTS):
                            u = first + straight + j
                            sp.wait_ge(unit_split, u - RAW_SLOTS + 1 + it * RAW_SLOTS)
                            unit = src[bass.ds(it * RAW_SLOTS + (straight + j), 1), :, :]
                            load_unit(unit.rearrange("u p m -> (u p) m"), u, u % RAW_SLOTS, size)
                for i in range(straight + loops * RAW_SLOTS, n):
                    u = first + i
                    sp.wait_ge(unit_split, u - RAW_SLOTS + 1)
                    load_unit(src[i], u, u % RAW_SLOTS, size)

            for k in range(DC):
                sp.dma_start(x[:, k, :], ins["xt"][k]).then_inc(x_loaded, 16)
            sp.dma_start(par[:, :], ins["par"]).then_inc(const_loaded, 16)
            sp.dma_start(ident[:, :], ins["c_ident"]).then_inc(const_loaded, 16)
            sp.dma_start(ones[:, :], ins["c_ones"]).then_inc(const_loaded, 16)
            for name, n, _ in STAGES:
                load_stage(name)
            for k in range(DC):
                sp.wait_ge(out_ready, k + 1)
                sp.dma_start(out[k], x[:, k, :]).then_inc(stored, 16)
            sp.wait_ge(stored, 16 * DC)

        @block.gpsimd
        def _(pool):
            def split_unit(u, size, it=0, per_loop=0):
                slot, half = u % RAW_SLOTS, u % SPLIT_SLOTS
                hi, lo, src = w_hi[:, half, 0:size], w_lo[:, half, 0:size], raw[:, slot, 0:size]
                pool.wait_ge(unit_high, u + 1 + it * per_loop)
                pool.tensor_tensor(lo, src, hi.bitcast(F32), ALU.subtract).then_inc(unit_split, 1)

            for name, n, blocks in STAGES:
                first = UNIT[name][0]
                loops = n // RAW_SLOTS
                if loops:
                    with pool.Fori(0, loops) as it:
                        for j in range(RAW_SLOTS):
                            split_unit(first + j, blocks * P, it, RAW_SLOTS)
                for i in range(loops * RAW_SLOTS, n):
                    split_unit(first + i, blocks * P)

        @block.tensor
        def _(pe):
            mm = nc.tensor.matmul

            def wait(pair):
                pe.wait_ge(pair[0], pair[1])

            def wait_bank(t, it=0, per_loop=0):
                if t >= BANKS:
                    pe.wait_ge(bank_free[t % BANKS], t // BANKS + it * (per_loop // BANKS))

            def unit_blocks(u, n, dst, chunk_at, hi, lo, first, last, it=0, per_loop=0, ready=None):
                half = u % SPLIT_SLOTS
                pe.wait_ge(unit_split, u + 1 + it * per_loop)
                for c in range(n):
                    if ready is not None:
                        pe.wait_ge(ready[0], ready[1] + c + 1)
                    k = chunk_at + c
                    wh, wl = w_hi[:, half, c * P:(c + 1) * P], w_lo[:, half, c * P:(c + 1) * P]
                    mm(dst[:, :], wh, hi[:, k, :], start=(first and c == 0), stop=False)
                    mm(dst[:, :], wh, lo[:, k, :], start=False, stop=False)
                    step = mm(dst[:, :], wl, hi[:, k, :], start=False, stop=(last and c == n - 1))
                step.then_inc(unit_done, 1)

            def project(stage, i, ready=None, hi=a_hi, lo=a_lo):
                t, (first, _, blocks) = TILE[stage, i], UNIT[stage]
                wait_bank(t)
                unit_blocks(first + i, blocks, bank[t % BANKS], 0, hi, lo, True, True, ready=ready)

            def aux_wait(*name):
                n = AUX[name]
                if n >= AUX_BANKS:
                    pe.wait_ge(aux_free[n % AUX_BANKS], n // AUX_BANKS)
                return bank[BANKS + n % AUX_BANKS]

            def total(name, source, waits):
                n = STAT[name]
                for s, v in waits:
                    pe.wait_ge(s, v)
                if n:
                    pe.wait_ge(root_ready, n)
                mm(stat_bank[:, :], ones[:, :], source, start=True, stop=True).then_inc(total_ready, 1)

            def total_x(name):
                total(name, sum_sq[:, :], [(sum_added, SQUARE[name] + DC)])

            def hidden(stage, split=None):
                first, n, blocks = UNIT[stage]
                t = TILE[stage, 0]
                ready = (act_ready, SPLIT[split])
                project(stage, 0, ready)
                for j in range(1, 4):
                    project(stage, j)
                with pe.Fori(0, n // 4 - 1) as it:
                    for j in range(4, 8):
                        wait_bank(t + j, it, 4)
                        unit_blocks(first + j, blocks, bank[(t + j) % BANKS], 0, a_hi, a_lo, True, True, it, 4)

            def down(stage, turn):
                first = UNIT[stage][0]
                t = TILE[stage, 0]
                pe.wait_ge(hidden_ready, FC * (turn + 1))
                with pe.Fori(0, DC // 4) as it:
                    for j in range(4):
                        wait_bank(t + j, it, 4)
                        for half in range(2):
                            unit_blocks(first + 2 * j + half, DOWN_CHUNKS, bank[(t + j) % BANKS],
                                        half * DOWN_CHUNKS, h_hi, h_lo, half == 0, half == 1, it, 8)

            pe.wait_ge(const_loaded, 48)
            total_x("norm1")
            pe.wait_ge(const1_loaded, 16 * 7)

            def aux1(t):
                name = aux_of_proj1(t)
                dst = aux_wait(*name)
                wait(tile_read("proj1", t))
                if name[0] == "rope":
                    mm(dst[:, :], rot[:, :], unrot[:, t % 2, :], start=True, stop=True).then_inc(aux_ready, 1)
                elif name[0] == "vtok":
                    for j in range(QB):
                        step = pe.transpose(dst[:, j * P:(j + 1) * P], v1t[:, t % 2, j * P:(j + 1) * P], ident[:, :])
                    step.then_inc(aux_ready, 1)
                else:
                    g = name[1]
                    pe.wait_ge(pool_ready, g + 1)
                    mm(dst[:, :], pool_w[:, g, :], pool_d[:, g % 2, :], start=True, stop=True).then_inc(aux_ready, 1)

            for t in range(16):
                project("proj1", t, (act_ready, SPLIT["norm1"]) if t == 0 else None)
                if t:
                    aux1(t - 1)
            aux1(15)

            for a in range(18):
                if a < 16:
                    h, i = a // QB, a % QB
                    end = (i + 1) * P
                    pe.wait_ge(rope_done, 8)
                    for n in range(2):
                        dst = aux_wait("score", a, n)
                        rows = slice(64 * n, 64 * n + 64)
                        mm(dst[:, 0:end], q1[rows, h, i * P:end], k1[rows, h, 0:end], start=True, stop=False)
                        mm(dst[:, end - 64:end], neg_row[0:1, :], one_row[0:1, :], start=False,
                           stop=True).then_inc(aux_ready, 1)
                    dst = aux_wait("bias", a)
                    pe.wait_ge(rel_set, 1)
                    cols = slice(0, T) if a % 2 == 0 else slice(T, BIAS_COLS)
                    mm(dst[:, 0:cols.stop - cols.start], rel_wide[:, a // 2, :], onehot[:, cols], start=True,
                       stop=True).then_inc(aux_ready, 1)
                if 1 <= a <= 16:
                    dst = aux_wait("turn", a - 1)
                    pe.wait_ge(attn_ready, a)
                    for j in range((a - 1) % QB + 1):
                        step = pe.transpose(dst[:, j * P:(j + 1) * P], attn[:, (a - 1) % 2, j * P:(j + 1) * P],
                                            ident[:, :])
                    step.then_inc(aux_ready, 1)
                if a >= 2:
                    b = a - 2
                    h, i = b // QB, b % QB
                    if i == 0:
                        wait_bank(TILE["attn", h])
                        wait(aux_read("vtok", h))
                    wait(aux_read("turn", b))
                    dst = tile_bank("attn", h)
                    for j in range(i + 1):
                        step = mm(dst[:, i * P:(i + 1) * P], v1[:, j, h, :], attn_t[:, b % 2, j * P:(j + 1) * P],
                                  start=(j == 0), stop=(j == i))
                    if i == QB - 1:
                        step.then_inc(head_ready, 1)
            for h in range(HEADS):
                total(f"head{h}", sq[:, h % 2, :], [(head_sq, h + 1)])
            for i in range(DC):
                project("wo", i, (act_ready, SPLIT["mix1"]) if i == 0 else None)
            total_x("norm2")
            hidden("up1", "norm2")
            down("down1", 0)
            total_x("final1")
            total_x("pre1")
            hidden("up2", "pre1")
            down("down2", 1)
            total_x("post1")
            total_x("mixpre")
            pe.wait_ge(const2_loaded, 16 * 3)
            for n in range(len(TILES2)):
                project("proj2", n, (act_ready, SPLIT["mixpre"]) if n == 0 else None)
                for kind, m in AFTER2[n]:
                    if kind == "stat":
                        total(m, sq[:, STAT[m] % 2, :], [(head_sq, 5 + (m == "kidx"))])
                    elif kind == "wturn":
                        dst = aux_wait(kind, m)
                        wait(tile_read("proj2", 2))
                        for j in range(QB):
                            step = pe.transpose(dst[:, j * 8:j * 8 + 8], widx_t[0:8, j * P:(j + 1) * P],
                                                ident[0:8, 0:8])
                        step.then_inc(aux_ready, 1)
                    elif kind == "ckvtok":
                        dst = aux_wait(kind, m)
                        pe.wait_ge(norm_ready, 1)
                        for j in range(QB):
                            step = pe.transpose(dst[:, j * P:(j + 1) * P], ckv[:, j * P:(j + 1) * P], ident[:, :])
                        step.then_inc(aux_ready, 1)
                    elif kind == "qlat":
                        dst = aux_wait(kind, m)
                        wait(tile_read("proj2", 7 + m // 2))
                        rows = slice(64 * (m % 2), 64 * (m % 2) + 64)
                        mm(dst[:, :], wuk[rows, m // 2, :], qa[rows, (m // 2) % 2, :], start=True,
                           stop=True).then_inc(aux_ready, 1)
                    elif kind == "vturn":
                        dst = aux_wait(kind, m)
                        wait(tile_read("proj2", 11 + m))
                        for j in range(QB):
                            step = pe.transpose(dst[:, j * P:(j + 1) * P], i_t[:, m % 2, j * P:(j + 1) * P],
                                                ident[:, :])
                        step.then_inc(aux_ready, 1)
                    else:
                        dst = aux_wait(kind, m)
                        i, h = IDX_STEPS[m]
                        pe.wait_ge(norm_ready, 2)
                        wait(tile_read("proj2", 3 + h // 2))
                        rows = slice(64 * (h % 2), 64 * (h % 2) + 64)
                        mm(dst[:, 0:(i + 1) * P], qidx[rows, h // 2, i * P:(i + 1) * P],
                           kidx[rows, 0:(i + 1) * P], start=True, stop=True).then_inc(aux_ready, 1)
            for a in range(35):
                if a < 32:
                    h, i = a // QB, a % QB
                    end = (i + 1) * P
                    dst = aux_wait("logit", a)
                    wait(aux_read("qlat", h))
                    mm(dst[:, 0:end], qlat[:, h, i * P:end], ckv[:, 0:end], start=True,
                       stop=True).then_inc(aux_ready, 1)
                if 1 <= a <= 32:
                    dst = aux_wait("turn2", a - 1)
                    pe.wait_ge(attn2_ready, a)
                    for j in range((a - 1) % QB + 1):
                        step = pe.transpose(dst[:, j * P:(j + 1) * P], attn2[:, (a - 1) % 2, j * P:(j + 1) * P],
                                            ident[:, :])
                    step.then_inc(aux_ready, 1)
                if 2 <= a <= 33:
                    b = a - 2
                    h, i = b // QB, b % QB
                    if i == 0:
                        wait_bank(TILE["olat", h])
                        wait(aux_read("ckvtok", 0))
                    wait(aux_read("turn2", b))
                    dst = tile_bank("olat", h)
                    for j in range(i + 1):
                        step = mm(dst[:, i * P:(i + 1) * P], ckv_tok[:, j, :],
                                  attn2_t[:, b % 2, j * P:(j + 1) * P], start=(j == 0), stop=(j == i))
                    if i == QB - 1:
                        step.then_inc(head_ready, 1)
                if a >= 10 and a % 8 == 2:
                    t = (a - 10) // 8
                    dst = aux_wait("ya", t)
                    wait(tile_read("olat", 2 * t))
                    wait(tile_read("olat", 2 * t + 1))
                    for n in range(2):
                        step = mm(dst[64 * n:64 * n + 64, :], wuv[:, 2 * t + n, :], olat[:, n, :], start=True,
                                  stop=True)
                    step.then_inc(aux_ready, 1)
            def hgrn_out(h):
                wait_bank(TILE["hgrn", h])
                for l in (6, 7, 8):
                    wait(aux_read("pair", h, l))
                wait(aux_read("vturn", h))
                s = h % 2
                dst = tile_bank("hgrn", h)
                for i in range(QB):
                    blocks = [(i, pair_d[:, s, i * P:(i + 1) * P])]
                    if i % 2:
                        blocks.append((i - 1, pair_1[:, s, i // 2, :]))
                    if i >= 2:
                        blocks += [(j, pair_2[:, s, j, (i - 2) * P:(i - 1) * P]) for j in range(2)]
                    for n, (j, pairs) in enumerate(blocks):
                        step = mm(dst[:, i * P:(i + 1) * P], v2[:, j, h, :], pairs, start=(n == 0),
                                  stop=(n == len(blocks) - 1))
                step.then_inc(head_ready, 1)

            for h in range(HEADS):
                s = h % 2
                dst = aux_wait("pair0", h)
                pe.wait_ge(k_ready, h + 1)
                for j in range(QB):
                    cols = slice(j * P, (j + 1) * P)
                    step = mm(dst[:, cols], hk[:, s, cols], hq[:, s, cols], start=True, stop=True)
                step.then_inc(aux_ready, 1)
                for l, b in enumerate(LEVELS):
                    e = h * len(LEVELS) + l
                    dst = aux_wait("pair", h, l)
                    pe.wait_ge(qk_ready, e + 1)
                    if b <= 64:
                        pieces = [(j, j * P, P, j * P) for j in range(QB)]
                    elif b == 128:
                        pieces = [(0, P, P, 0), (2, 3 * P, P, P)]
                    else:
                        pieces = [(0, 2 * P, 2 * P, 0), (1, 2 * P, 2 * P, 2 * P)]
                    for j, q0, n, col in pieces:
                        step = mm(dst[:, col:col + n], qk[:, e % 2, j * P:(j + 1) * P], qk[:, e % 2, q0:q0 + n],
                                  start=True, stop=True)
                    step.then_inc(aux_ready, 1)
                    if h and l == 2:
                        hgrn_out(h - 1)
            hgrn_out(HEADS - 1)
            for h in range(HEADS):
                total(f"hgrn{h}", sq[:, h % 2, :], [(head_sq, 7 + h)])
            for i in range(2 * DC):
                t, first = TILE["branch", i], UNIT["branch"][0]
                wait_bank(t)
                chunks = 4 * (i % 2)
                unit_blocks(first + i, 4, bank[t % BANKS], chunks, a_hi, a_lo, True, True,
                            ready=(act_ready, SPLIT["y"] + chunks) if i < 2 else None)
            for i in range(DC):
                project("out", i, (act_ready, SPLIT["merged"]) if i == 0 else None, h_hi, h_lo)
            total_x("postmix")
            total_x("pre2")
            hidden("up3", "pre2")
            down("down3", 2)
            for i in range(DC):
                t, u = TILE["pproj", i], UNIT["pproj"][0] + i // 4
                wait_bank(t)
                pe.wait_ge(unit_split, u + 1)
                if i == 0:
                    pe.wait_ge(act_ready, SPLIT["p"] + 2)
                for c in range(2):
                    cols = slice((2 * (i % 4) + c) * P, (2 * (i % 4) + c + 1) * P)
                    wh, wl = w_hi[:, u % SPLIT_SLOTS, cols], w_lo[:, u % SPLIT_SLOTS, cols]
                    mm(bank[t % BANKS][:, :], wh, a_hi[:, c, :], start=(c == 0), stop=False)
                    mm(bank[t % BANKS][:, :], wh, a_hi[:, 2 + c, :], start=False, stop=False)
                    step = mm(bank[t % BANKS][:, :], wl, a_hi[:, c, :], start=False, stop=(c == 1))
                step.then_inc(unit_done if i % 4 == 3 else head_ready, 1)
            total_x("post2")
            total_x("plepre")
            for i in range(DC):
                project("ple", i, (act_ready, SPLIT["plepre"]) if i == 0 else None)
            total_x("plepost")

        @block.scalar
        def _(act):
            fn = nc.scalar.activation

            def wait(pair):
                act.wait_ge(pair[0], pair[1])

            def unit_high_part(u, it=0, per_loop=0):
                if u >= LAST_UNIT:
                    return
                slot, size = u % RAW_SLOTS, BLOCKS_OF[u] * P
                act.wait_ge(raw_loaded[slot], 16 * (u // RAW_SLOTS + 1) + it * (16 * per_loop // RAW_SLOTS))
                fn(w_hi[:, u % SPLIT_SLOTS, 0:size], raw[:, slot, 0:size], ACT.Copy).then_inc(unit_high, 1)

            def units_done(v, it=0, per_loop=0):
                act.wait_ge(unit_done, v + it * per_loop)
                unit_high_part(v + 1, it, per_loop)

            def tile_finished(stage, i):
                per_tile = 2 if stage.startswith("down") else 1
                for n in range(per_tile):
                    units_done(UNIT[stage][0] + per_tile * i + n + 1)

            def square(stage, k, src, made):
                q = SQUARE[stage] + k
                wait(made)
                if q >= 2:
                    act.wait_ge(sum_added, q - 1)
                fn(sq[:, q % 2, :], src, ACT.Square).then_inc(sq_ready, 1)

            def take_root(name, width):
                n = STAT[name]
                act.wait_ge(total_ready, n + 1)
                if n:
                    act.wait_ge(rstd_ready, n)
                fn(root[:, :], stat_bank[:, :], ACT.Sqrt, bias=prm("eps"), scale=1.0 / width).then_inc(root_ready, 1)

            def high(c, dst):
                act.wait_ge(chunk_ready, c + 1)
                fn(dst, chunk[:, c % 2, :], ACT.Copy).then_inc(hi_ready, 1)

            def highs(stage, first=0, n=DC, dst=a_hi):
                for k in range(first, first + n):
                    high(SPLIT[stage] + k, dst[:, k, :])

            def keep_branch(stage, square_stage):
                for k in range(DC):
                    tile_finished(stage, k)
                    square(square_stage, k, tile_bank(stage, k)[:, :], tile_done(stage, k))
                    fn(y[:, k, :], tile_bank(stage, k)[:, :], ACT.Copy).then_inc(tile_sem(stage, k), 1)

            for dst, name in ((rot[:, :], "c_rot"), (pool_w[:, :, :], "pool_w"), (count[:, :, :], "c_count"),
                              (onehot[:, :], "c_onehot"), (rel[:, :], "rel")):
                src = ins[name].rearrange("p (g c) -> p g c", g=4) if name == "c_count" else ins[name]
                act.dma_start(dst, src).then_inc(const1_loaded, 16)
            lam_src = ins["lambdas"]
            act.dma_start(lam_in[:, :, :], bass.AP(lam_src.tensor, lam_src.offset, [[0, P], [64, 4], [1, 64]])
                          ).then_inc(const1_loaded, 16)
            pos_src = ins["positions"]
            act.dma_start(pos_i[:, :], bass.AP(pos_src.tensor, pos_src.offset, [[0, P], [1, T]])
                          ).then_inc(const1_loaded, 16)
            unit_high_part(0)
            unit_high_part(1)
            act.wait_ge(trig_in, 1)
            fn(sin[:, :], sin[:, :], ACT.Sin).then_inc(trig, 1)
            act.wait_ge(trig_in, 2)
            fn(cos[:, :], cos[:, :], ACT.Sin).then_inc(trig, 1)
            for k in range(DC):
                square("norm1", k, x[:, k, :], (x_loaded, 16 * DC))
            take_root("norm1", D)
            highs("norm1")
            for t in range(16):
                tile_finished("proj1", t)
                if t < 8:
                    if t >= 2:
                        wait(aux_read("rope", t - 2))
                    fn(unrot[:, t % 2, :], tile_bank("proj1", t)[:, :], ACT.Copy).then_inc(tile_sem("proj1", t), 1)
                elif t < 12:
                    if t >= 10:
                        act.wait_ge(aux_ready, AUX["vtok", t - 10] + 1)
                    fn(v1t[:, t % 2, :], tile_bank("proj1", t)[:, :], ACT.Copy).then_inc(tile_sem("proj1", t), 1)
                else:
                    if t >= 14:
                        act.wait_ge(pool_ready, t - 13)
                    fn(pool_in[:, t % 2, PAD:], tile_bank("proj1", t)[:, :], ACT.Copy).then_inc(
                        tile_sem("proj1", t), 1)
                if 9 <= t < 13:
                    h = t - 9
                    act.wait_ge(aux_ready, AUX["vtok", h] + 1)
                    fn(v1[:, :, h, :], aux_bank("vtok", h)[:, :].rearrange("p (j d) -> p j d", j=QB),
                       ACT.Copy).then_inc(aux_sem("vtok", h), 1)
            highs("mix1", 0, 4)
            act.wait_ge(lam_sum, 1)
            fn(small[:, 3:5], small[:, 1:3], ACT.Exp).then_inc(lam_exp, 1)
            for a in range(18):
                if a < 16:
                    h, i = a // QB, a % QB
                    end = (i + 1) * P
                    if a >= 2:
                        act.wait_ge(attn_ready, a - 1)
                    for n in range(2):
                        act.wait_ge(neg_max, 2 * a + n + 1)
                        s = 2 * (a % 2) + n
                        fn(prob[:, a % 2, n, 0:end], aux_bank("score", a, n)[:, 0:end], ACT.Exp,
                           bias=small[:, 8 + s:9 + s], scale=DIFF_SCALE,
                           accum_out=small[:, 12 + s:13 + s]).then_inc(aux_sem("score", a, n), 1)
                    act.wait_ge(aux_ready, AUX["bias", a] + 1)
                    h = a // 2
                    if h >= 2:
                        act.wait_ge(bias_out[h % 2], 16 * (h // 2))
                    cols = slice(0, T) if a % 2 == 0 else slice(T, BIAS_COLS)
                    fn(bias_slot[:, h % 2, cols], aux_bank("bias", a)[:, 0:cols.stop - cols.start],
                       ACT.Copy).then_inc(aux_sem("bias", a), 1)
                    if a % 2:
                        wait(aux_read("bias", a))
                        wait(aux_read("bias", a - 1))
                        act.dma_start(bias_rows[h], bias_slot[:, h % 2, :]).then_inc(bias_out[h % 2], 16)
                if 1 <= a <= 16:
                    act.wait_ge(aux_ready, AUX["turn", a - 1] + 1)
                    n = ((a - 1) % QB + 1) * P
                    fn(attn_t[:, (a - 1) % 2, 0:n], aux_bank("turn", a - 1)[:, 0:n], ACT.Copy).then_inc(
                        aux_sem("turn", a - 1), 1)
                if a >= 2 and (a - 2) % QB == QB - 1:
                    h = (a - 2) // QB
                    act.wait_ge(head_ready, h + 1)
                    fn(o1[:, h, :], tile_bank("attn", h)[:, :], ACT.Copy).then_inc(tile_sem("attn", h), 1)
            for h in range(HEADS):
                wait(tile_read("attn", h))
                if h == 0:
                    act.wait_ge(sum_added, DC)
                if h >= 2:
                    act.wait_ge(total_ready, STAT[f"head{h - 2}"] + 1)
                fn(sq[:, h % 2, :], o1[:, h, :], ACT.Square).then_inc(head_sq, 1)
                take_root(f"head{h}", P)
                highs("mix1", 4 + h, 1)
            for k in range(DC):
                tile_finished("wo", k)
                square("norm2", k, x[:, k, :], tile_read("wo", k))
            take_root("norm2", D)
            highs("norm2")
            def silu_pairs(i, it=0, per_loop=0):
                first = UNIT["up1"][0]
                for j in (i, i + 1):
                    units_done(first + 2 * j + 1, it, 2 * per_loop)
                    units_done(first + 2 * j + 2, it, 2 * per_loop)
                    act.wait_ge(gate_ready, j + 1 + it * per_loop)
                    fn(silu[:, :], gate[:, :], ACT.Silu).then_inc(silu_ready, 1)

            with act.Fori(0, FC // 2 - 1) as it:
                silu_pairs(0, it, 2)
            silu_pairs(FC - 2)
            for k in range(DC):
                tile_finished("down1", k)
                square("final1", k, x[:, k, :], tile_read("down1", k))
            take_root("final1", D)
            for k in range(DC):
                square("pre1", k, x[:, k, :], (x_ready, k + 1))
            take_root("pre1", D)
            highs("pre1")

            def silus(stage, turn):
                t, first = TILE[stage, 0], UNIT[stage][0]
                slots = [gate, silu]

                def one(i, it=0, per_loop=0):
                    units_done(first + 2 * i + 1, it, 2 * per_loop)
                    if i >= 2:
                        act.wait_ge(hidden_ready, FC * turn + i - 1 + it * per_loop)
                    fn(slots[i % 2][:, :], bank[(t + 2 * i) % BANKS][:, :], ACT.Silu).then_inc(
                        bank_free[(t + 2 * i) % BANKS], 1)
                    units_done(first + 2 * i + 2, it, 2 * per_loop)

                one(0)
                one(1)
                with act.Fori(0, FC // 2 - 2) as it:
                    one(2, it, 2)
                    one(3, it, 2)
                one(FC - 2)
                one(FC - 1)

            silus("up2", 1)
            keep_branch("down2", "post1")
            take_root("post1", D)
            act.dma_start(wuk[:, :, :], ins["wuk"]).then_inc(const2_loaded, 16)
            act.dma_start(wuv[:, :, :], ins["wuv"]).then_inc(const2_loaded, 16)
            act.dma_start(tri[:, :], ins["c_tri"]).then_inc(const2_loaded, 16)

            def load_bias(h):
                src = bias_rows[h]
                act.dma_start(t_bias[:, h % 2, :], bass.AP(src.tensor, src.offset + P - 1,
                                                           [[BIAS_COLS - 1, P], [1, T]])
                              ).then_inc(bias_in[h % 2], 16)

            for n in range(2):
                act.wait_ge(bias_out[n], 16 * (DSA_HEADS // 2))
            load_bias(0)
            load_bias(1)
            for k in range(DC):
                square("mixpre", k, x[:, k, :], (x_ready, DC + k + 1))
            take_root("mixpre", D)
            highs("mixpre")
            act.wait_ge(lam_sum, 2)
            fn(small[:, 36:40], small[:, 32:36], ACT.Sigmoid).then_inc(lam_exp, 1)
            for n, name in enumerate(TILES2):
                src, done = tile_bank("proj2", n)[:, :], tile_sem("proj2", n)
                kind, t = name.rstrip("0123456789"), int(name[len(name.rstrip("0123456789")):] or 0)
                tile_finished("proj2", n)
                if kind in ("ckv", "kidx"):
                    if n == 0:
                        act.wait_ge(sum_added, SQUARE["mixpre"] + DC)
                    fn(sq[:, n, :], src, ACT.Square).then_inc(head_sq, 1)
                    fn((ckv_raw, kidx_raw)[n][:, :], src, ACT.Copy).then_inc(done, 1)
                elif kind == "widx":
                    fn(widx_t[:, :], src, ACT.Copy).then_inc(done, 1)
                elif kind == "qi":
                    fn(qidx[:, t, :], src, ACT.Copy).then_inc(done, 1)
                elif kind == "qa":
                    if t >= 2:
                        act.wait_ge(aux_ready, AUX["qlat", 2 * t - 3] + 1)
                    fn(qa[:, t % 2, :], src, ACT.Copy).then_inc(done, 1)
                elif kind == "i":
                    if t >= 2:
                        act.wait_ge(aux_ready, AUX["vturn", t - 2] + 1)
                    fn(i_t[:, t % 2, :], src, ACT.Copy).then_inc(done, 1)
                else:
                    s = {"qh": 0, "gh": 4, "fh": 8, "gate": 12}[kind] + t
                    if s >= 3:
                        act.wait_ge(spill_out[s % 3], 16 * (s // 3))
                    f = ACT.Silu if s < 8 else ACT.Sigmoid
                    bias = prm("b_gate", t) if kind == "gate" else 0.0
                    fn(spill_slot[s % 3][:, :], src, f, bias=bias).then_inc(done, 1)
                    wait(tile_read("proj2", n))
                    act.dma_start(spill[s], spill_slot[s % 3][:, :]).then_inc(spill_out[s % 3], 16)
                for ev, m in AFTER2[n]:
                    if ev == "stat":
                        take_root(m, P)
                        continue
                    if ev == "wturn":
                        continue
                    small_out = aux_bank(ev, m)[:, :]
                    act.wait_ge(aux_ready, AUX[ev, m] + 1)
                    if ev == "ckvtok":
                        fn(ckv_tok[:, :, :], small_out.rearrange("p (j d) -> p j d", j=QB), ACT.Copy).then_inc(
                            aux_sem(ev, m), 1)
                    elif ev == "qlat":
                        fn(qlat[:, m, :], small_out, ACT.Copy, scale=ATT_SCALE).then_inc(aux_sem(ev, m), 1)
                    elif ev == "vturn":
                        fn(v2[:, :, m, :], small_out.rearrange("p (j d) -> p j d", j=QB), ACT.Copy).then_inc(
                            aux_sem(ev, m), 1)
                    else:
                        if m >= 2:
                            act.wait_ge(relu_used, m - 1)
                        w = (IDX_STEPS[m][0] + 1) * P
                        fn(relu[:, m % 2, 0:w], small_out[:, 0:w], ACT.Relu).then_inc(aux_sem(ev, m), 1)
            for a in range(35):
                if a < 32:
                    h, i = a // QB, a % QB
                    end = (i + 1) * P
                    act.wait_ge(logit_max, a + 1)
                    if a >= 2:
                        act.wait_ge(attn2_ready, a - 1)
                    fn(prob2[:, a % 2, 0:end], logit[:, a % 2, 0:end], ACT.Exp,
                       bias=small[:, 24 + a % 2:25 + a % 2],
                       accum_out=small[:, 26 + a % 2:27 + a % 2]).then_inc(exp2_done, 1)
                    if i == 1 and 1 <= h < DSA_HEADS - 1:
                        act.wait_ge(attn2_ready, QB * h)
                        load_bias(h + 1)
                if 1 <= a <= 32:
                    act.wait_ge(aux_ready, AUX["turn2", a - 1] + 1)
                    n = ((a - 1) % QB + 1) * P
                    fn(attn2_t[:, (a - 1) % 2, 0:n], aux_bank("turn2", a - 1)[:, 0:n], ACT.Copy).then_inc(
                        aux_sem("turn2", a - 1), 1)
                if 2 <= a <= 33 and (a - 2) % QB == QB - 1:
                    h = (a - 2) // QB
                    act.wait_ge(head_ready, HEADS + h + 1)
                    if h >= 2:
                        act.wait_ge(aux_ready, AUX["ya", (h - 2) // 2] + 1)
                    fn(olat[:, h % 2, :], tile_bank("olat", h)[:, :], ACT.Copy).then_inc(tile_sem("olat", h), 1)
                if a >= 10 and a % 8 == 2:
                    highs("y", (a - 10) // 8, 1)
            act.wait_ge(aux_ready, AUX["ya", 3] + 1)
            act.wait_ge(act_ready, SPLIT["y"] + 4)
            act.dma_start(masks[:, :, :], ins["c_masks"].rearrange("p (l t) -> p l t", l=8)).then_inc(
                const3_loaded, 16)
            act.dma_start(resets[:, :, :], ins["c_resets"].rearrange("p (l t) -> p l t", l=3)).then_inc(
                const3_loaded, 16)
            for n in range(3):
                act.wait_ge(spill_out[n], 16 * len(range(n, 28, 3)))

            def load_head(h):
                act.dma_start(hq[:, h % 2, :], spill[h]).then_inc(h_loaded[h % 2], 16)
                act.dma_start(hf[:, h % 2, :], spill[8 + h]).then_inc(h_loaded[h % 2], 16)

            load_head(0)
            load_head(1)
            for h in range(HEADS):
                act.dma_start(hg[:, h, :], spill[4 + h]).then_inc(hg_loaded, 16)

            def keep_head(h):
                act.wait_ge(head_ready, HEADS + DSA_HEADS + h + 1)
                fn(oh[:, h, :], tile_bank("hgrn", h)[:, :], ACT.Copy).then_inc(tile_sem("hgrn", h), 1)

            for h in range(HEADS):
                act.wait_ge(f_ready, h + 1)
                fn(logf[:, :], hf[:, h % 2, :], ACT.Ln).then_inc(logf_ready, 1)
                for l, b in enumerate(LEVELS):
                    e = h * len(LEVELS) + l
                    act.wait_ge(diff_ready, e + 1)
                    if e >= 2:
                        act.wait_ge(qk_ready, e - 1)
                    if b <= 32:
                        fn(decay[:, e % 2, :], diff[:, e % 2, :], ACT.Exp).then_inc(decay_ready, 1)
                    else:
                        split_ap = lambda ap: ap.rearrange("p (n c) -> p n c", c=2 * b)
                        to = split_ap(decay[:, e % 2, :])
                        fn(to[:, :, 0:b], split_ap(diff[:, e % 2, :])[:, :, 0:b], ACT.Exp).then_inc(decay_ready, 1)
                        fn(to[:, :, b:2 * b], split_ap(run[:, h % 2, l - 6, :])[:, :, b:2 * b],
                           ACT.Exp).then_inc(decay_ready, 1)
                    if h and l == 4:
                        keep_head(h - 1)
                    if l >= 8:
                        for m in (7, 8):
                            if h >= 2:
                                act.wait_ge(head_ready, HEADS + DSA_HEADS + h - 1)
                            act.wait_ge(aux_ready, AUX["pair", h, m] + 1)
                            src = aux_bank("pair", h, m)
                            if m == 7:
                                fn(pair_1[:, h % 2, :, :], src[:, 0:2 * P].rearrange("p (n t) -> p n t", n=2),
                                   ACT.Copy).then_inc(aux_sem("pair", h, m), 1)
                            else:
                                fn(pair_2[:, h % 2, :, :], src[:, :].rearrange("p (n t) -> p n t", n=2),
                                   ACT.Copy).then_inc(aux_sem("pair", h, m), 1)
                if h + 2 < HEADS:
                    wait(aux_read("pair", h, 6))
                    act.wait_ge(qk_ready, (h + 1) * len(LEVELS))
                    load_head(h + 2)
            keep_head(HEADS - 1)
            for h in range(HEADS):
                wait(tile_read("hgrn", h))
                if h >= 2:
                    act.wait_ge(total_ready, STAT[f"hgrn{h - 2}"] + 1)
                fn(sq[:, h % 2, :], oh[:, h, :], ACT.Square).then_inc(head_sq, 1)
                take_root(f"hgrn{h}", P)
                highs("y", 4 + h, 1)

            def load_gates(m):
                for n in range(2):
                    act.dma_start(gates_in[:, 2 * (m % 2) + n, :], spill[12 + 8 * n + m]).then_inc(
                        gates_loaded[m % 2], 16)

            act.wait_ge(aux_ready, len(AUX))
            load_gates(0)
            load_gates(1)
            for m in range(DC):
                tile_finished("branch", 2 * m)
                tile_finished("branch", 2 * m + 1)
                high(SPLIT["merged"] + m, h_hi[:, m, :])
                if m + 2 < DC:
                    load_gates(m + 2)
            keep_branch("out", "postmix")
            take_root("postmix", D)
            for k in range(DC):
                square("pre2", k, x[:, k, :], (x_ready, 2 * DC + k + 1))
            take_root("pre2", D)
            highs("pre2")
            silus("up3", 2)
            for c in range(2):
                act.dma_start(pe_in[:, c, :], ins["pt"][c]).then_inc(p_loaded, 16)
            highs("p", 0, 2)
            keep_branch("down3", "post2")
            for i in range(DC):
                if i % 4 == 3:
                    units_done(UNIT["pproj"][0] + i // 4 + 1)
                else:
                    act.wait_ge(head_ready, 2 * HEADS + DSA_HEADS + i - i // 4 + 1)
                fn(p_proj[:, i, :], tile_bank("pproj", i)[:, :], ACT.Copy).then_inc(tile_sem("pproj", i), 1)
            take_root("post2", D)
            for k in range(DC):
                square("plepre", k, x[:, k, :], (x_ready, 3 * DC + k + 1))
            take_root("plepre", D)
            highs("plepre")
            slots = [gate, silu]
            for i in range(DC + 1):
                if i < DC:
                    tile_finished("ple", i)
                    if i >= 2:
                        act.wait_ge(y_ready, i - 1)
                    fn(slots[i % 2][:, :], tile_bank("ple", i)[:, :], ACT.Sigmoid).then_inc(tile_sem("ple", i), 1)
                if i:
                    square("plepost", i - 1, p_proj[:, i - 1, :], (y_ready, i))
            take_root("plepost", D)

        @block.vector
        def _(dve):
            v = nc.vector
            steps = [0]

            def step(ins_, it=0, per_loop=0):
                steps[0] += 1
                ins_.then_inc(dve_step, 1)
                dve.wait_ge(dve_step, steps[0] + (it * per_loop if per_loop else 0))

            def wait(pair):
                dve.wait_ge(pair[0], pair[1])

            def rsqrt(name):
                n = STAT[name]
                dve.wait_ge(root_ready, n + 1)
                v.reciprocal(rstd[:, :], root[:, :]).then_inc(rstd_ready, 1)
                dve.wait_ge(rstd_ready, n + 1)

            def low(c, dst, hi):
                dve.wait_ge(hi_ready, c + 1)
                v.tensor_tensor(dst, chunk[:, c % 2, :], hi.bitcast(F32), ALU.subtract).then_inc(act_ready, 1)

            def made(c):
                dve.wait_ge(chunk_ready, c + 1)

            def slot_free(c):
                if c >= 2:
                    dve.wait_ge(act_ready, c - 1)

            def norm_to_split(name, stage, g):
                rsqrt(name)
                c0 = SPLIT[stage]
                for k in range(DC + 1):
                    if k < DC:
                        slot_free(c0 + k)
                        v.scalar_tensor_tensor(chunk[:, (c0 + k) % 2, :], x[:, k, :], prm(g, k), rstd[:, :],
                                               ALU.mult, ALU.mult).then_inc(chunk_ready, 1)
                    if k:
                        made(c0 + k - 1)
                        low(c0 + k - 1, a_lo[:, k - 1, :], a_hi[:, k - 1, :])

            def add_square(stage, k):
                q = SQUARE[stage] + k
                dve.wait_ge(sq_ready, q + 1)
                if k == 0:
                    v.tensor_copy(sum_sq[:, :], sq[:, q % 2, :]).then_inc(sum_added, 1)
                else:
                    dve.wait_ge(sum_added, q)
                    v.tensor_tensor(sum_sq[:, :], sum_sq[:, :], sq[:, q % 2, :], ALU.add).then_inc(sum_added, 1)

            def add_tiles(stage, square_stage):
                for k in range(DC + 1):
                    if k < DC:
                        wait(tile_done(stage, k))
                        v.tensor_tensor(x[:, k, :], x[:, k, :], tile_bank(stage, k)[:, :], ALU.add).then_inc(
                            tile_sem(stage, k), 1)
                    if k:
                        add_square(square_stage, k - 1)

            def add_branch(name, g, src, last_read, signal, before, square_stage=None):
                rsqrt(name)
                for k in range(DC + 1):
                    if k < DC:
                        if last_read is not None:
                            wait(last_read(k))
                        if k >= 2:
                            dve.wait_ge(signal, before + k - 1)
                        step(v.scalar_tensor_tensor(chunk[:, k % 2, :], src[:, k, :], prm(g, k), rstd[:, :],
                                                    ALU.mult, ALU.mult))
                        v.tensor_tensor(x[:, k, :], x[:, k, :], chunk[:, k % 2, :], ALU.add).then_inc(signal, 1)
                    if k and square_stage:
                        add_square(square_stage, k - 1)

            v.memset(pool_in[:, :, 0:PAD], 0.0)
            v.memset(pool_s[:, :, 0:PAD], 0.0)
            v.memset(neg_row[:, 0:64], NEG)
            v.memset(neg_row[:, 64:P], 0.0)
            step(v.memset(one_row[:, :], 1.0))
            dve.wait_ge(const_loaded, 48)
            for name, factor in (("attn_norm_g", 1.0 - LAM_INIT), ("ffn1_post_g", 0.5), ("ffn2_post_g", 0.5)):
                first, n = PARAMS[name]
                step(v.tensor_scalar(par[:, first:first + n], par[:, first:first + n], factor, None, ALU.mult))
            dve.wait_ge(const1_loaded, 16 * 7)
            v.tensor_copy(rel_wide[:, :, :], rel[:, :].rearrange("p (h o) -> p h o", o=1).broadcast_to([32, DSA_HEADS, P])).then_inc(rel_set, 1)
            step(v.tensor_copy(angle[:, :], pos_i[:, :]))
            step(v.tensor_scalar(angle[:, :], angle[:, :], prm("inv_freq"), None, ALU.mult))
            step(v.tensor_scalar(turns[:, :], angle[:, :], float(1 / (2 * np.pi)), ROUND, ALU.mult, ALU.add))
            step(v.tensor_scalar(turns[:, :], turns[:, :], ROUND, None, ALU.subtract))
            for part in TURN_PARTS:
                step(v.scalar_tensor_tensor(angle[:, :], turns[:, :], -part, angle[:, :], ALU.mult, ALU.add))
            v.tensor_scalar(sin[:, :], angle[:, :], PI_BELOW, -PI_BELOW, ALU.min, ALU.max).then_inc(trig_in, 1)
            step(v.scalar_tensor_tensor(cos[:, :], angle[:, :], -1.0, angle[:, :], ALU.mult, ALU.max))
            v.tensor_scalar(cos[:, :], cos[:, :], -1.0, float(np.pi / 2), ALU.mult, ALU.add).then_inc(trig_in, 1)
            step(v.tensor_tensor(lam_in[:, 0:3:2, :], lam_in[:, 0:3:2, :], lam_in[:, 1:4:2, :], ALU.mult))
            v.tensor_reduce(small[:, 1:3], lam_in[:, 0:3:2, :], AX_X, ALU.add).then_inc(lam_sum, 1)
            lb = PARAMS["hgrn_lb0"][0]
            v.tensor_tensor(small[:, 32:36], par[:, lb:lb + 4], par[:, lb + 4:lb + 8], ALU.subtract).then_inc(
                lam_sum, 1)

            for k in range(DC):
                add_square("norm1", k)
            norm_to_split("norm1", "norm1", "norm_mix_g")
            dve.wait_ge(trig, 2)
            for t in range(8):
                raw_q = unrot[:, t % 2, :]
                dst = (q1 if t < 4 else k1)[:, t % 4, :]
                wait(tile_read("proj1", t))
                v.tensor_tensor(dst, raw_q, cos[:, :], ALU.mult)
                dve.wait_ge(aux_ready, AUX["rope", t] + 1)
                if t:
                    dve.wait_ge(rope_done, t)
                v.tensor_tensor(rope_a[:, :], aux_bank("rope", t)[:, :], sin[:, :], ALU.mult).then_inc(
                    aux_sem("rope", t), 1)
                wait(aux_read("rope", t))
                v.tensor_tensor(dst, dst, rope_a[:, :], ALU.add).then_inc(rope_done, 1)
            dve.wait_ge(rope_done, 8)
            for g, w in enumerate(WINDOWS):
                wait(tile_read("proj1", 12 + g))
                if g >= 2:
                    dve.wait_ge(aux_ready, AUX["pool", g - 2] + 1)
                token = pool_in[:, g % 2, PAD:]
                src, shift, n = pool_in[:, g % 2, :], 1, 0
                while shift < w:
                    to = pool_s[:, n % 2, :]
                    step(v.tensor_tensor(to[:, PAD:], src[:, PAD:], src[:, PAD - shift:PAD + T - shift], ALU.add))
                    src, shift, n = to, 2 * shift, n + 1
                diff_ = pool_d[:, g % 2, :]
                step(v.scalar_tensor_tensor(diff_, src[:, PAD:], 1.0 / w, token, ALU.mult, ALU.subtract))
                step(v.tensor_tensor(rope_a[:, 0:w], src[:, PAD:PAD + w], count[:, g, 0:w], ALU.mult))
                v.tensor_tensor(diff_[:, 0:w], rope_a[:, 0:w], token[:, 0:w], ALU.subtract).then_inc(pool_ready, 1)
                dve.wait_ge(pool_ready, g + 1)
            for g in range(4):
                c = SPLIT["mix1"] + g
                dve.wait_ge(aux_ready, AUX["pool", g] + 1)
                slot_free(c)
                step(v.tensor_scalar(chunk[:, c % 2, :], aux_bank("pool", g)[:, :], prm("pool_scale", g), None,
                                     ALU.mult))
                dve.sem_inc(aux_sem("pool", g), 1)
                dve.sem_inc(chunk_ready, 1)
                low(c, a_lo[:, g, :], a_hi[:, g, :])
            dve.wait_ge(lam_exp, 1)
            step(v.tensor_tensor(small[:, 5:6], small[:, 4:5], small[:, 3:4], ALU.subtract))
            step(v.tensor_scalar(small[:, 5:6], small[:, 5:6], -LAM_INIT, None, ALU.add))
            for a in range(17):
                if a < 16:
                    end = (a % QB + 1) * P
                    for n in range(2):
                        s = 2 * (a % 2) + n
                        dve.wait_ge(aux_ready, AUX["score", a, n] + 1)
                        step(v.tensor_reduce(small[:, 6:7], aux_bank("score", a, n)[:, 0:end], AX_X, ALU.max))
                        v.tensor_scalar(small[:, 8 + s:9 + s], small[:, 6:7], -DIFF_SCALE, None,
                                        ALU.mult).then_inc(neg_max, 1)
                        dve.wait_ge(neg_max, 2 * a + n + 1)
                if a:
                    b = a - 1
                    end, s = (b % QB + 1) * P, 2 * (b % 2)
                    wait(aux_read("score", b, 0))
                    wait(aux_read("score", b, 1))
                    if b >= 2:
                        dve.wait_ge(aux_ready, AUX["turn", b - 2] + 1)
                        dve.wait_ge(attn_ready, b)
                    step(v.reciprocal(small[:, 16 + s:18 + s], small[:, 12 + s:14 + s]))
                    step(v.tensor_tensor(small[:, 17 + s:18 + s], small[:, 17 + s:18 + s], small[:, 5:6], ALU.mult))
                    p0, p1 = prob[:, b % 2, 0, 0:end], prob[:, b % 2, 1, 0:end]
                    step(v.tensor_scalar(p1, p1, small[:, 17 + s:18 + s], None, ALU.mult))
                    v.scalar_tensor_tensor(attn[:, b % 2, 0:end], p0, small[:, 16 + s:17 + s], p1, ALU.mult,
                                           ALU.add).then_inc(attn_ready, 1)
            for h in range(HEADS):
                c = SPLIT["mix1"] + 4 + h
                rsqrt(f"head{h}")
                slot_free(c)
                v.scalar_tensor_tensor(chunk[:, c % 2, :], o1[:, h, :], prm("attn_norm_g", h), rstd[:, :],
                                       ALU.mult, ALU.mult).then_inc(chunk_ready, 1)
                made(c)
                low(c, a_lo[:, 4 + h, :], a_hi[:, 4 + h, :])
            add_tiles("wo", "norm2")
            norm_to_split("norm2", "norm2", "norm_ffn_g")

            def hidden_at(buf, it, j):
                return buf[:, bass.ds(it * 2 + j, 1), :].rearrange("p k t -> p (k t)")

            for n in range(2):
                dve.wait_ge(bias_out[n], 16 * (DSA_HEADS // 2))
            first, t0 = UNIT["up1"][0], TILE["up1", 0]
            per = 10
            at_loop = steps[0]
            with dve.Fori(0, FC // 2) as it:
                def tap(name, tile):
                    at = PARAMS[name][0] + tile
                    return par[:, bass.ds(it * 4 + at, 1)]

                for j in range(2):
                    for n, dst in ((0, gate), (1, val)):
                        i = 2 * j + n
                        b = bank[(t0 + i) % BANKS]
                        dve.wait_ge(unit_done, first + i + 1 + it * 4)
                        step(v.tensor_scalar(dst[:, :], b[:, :], tap("conv_w2", i), tap("conv_b", i), ALU.mult,
                                             ALU.add), it, per)
                        step(v.scalar_tensor_tensor(dst[:, 1:T], b[:, 0:T - 1], tap("conv_w1", i), dst[:, 1:T],
                                                    ALU.mult, ALU.add), it, per)
                        v.scalar_tensor_tensor(dst[:, 2:T], b[:, 0:T - 2], tap("conv_w0", i), dst[:, 2:T],
                                               ALU.mult, ALU.add).then_inc(bank_free[(t0 + i) % BANKS], 1)
                        dve.wait_ge(bank_free[(t0 + i) % BANKS], (t0 + i) // BANKS + 1 + it)
                        if n == 0:
                            dve.sem_inc(gate_ready, 1)
                    dve.wait_ge(silu_ready, it * 2 + (j + 1))
                    step(v.tensor_tensor(val[:, :], silu[:, :], val[:, :], ALU.mult), it, per)
                    v.tensor_scalar(hidden_at(h_hi, it, j), val[:, :], 1.0, None, ALU.mult).then_inc(high_done, 1)
                    dve.wait_ge(high_done, it * 2 + (j + 1))
                    v.tensor_tensor(hidden_at(h_lo, it, j), val[:, :], hidden_at(h_hi, it, j).bitcast(F32),
                                    ALU.subtract).then_inc(hidden_ready, 1)
                    dve.wait_ge(hidden_ready, it * 2 + (j + 1))
            assert steps[0] - at_loop == per
            steps[0] += per * (FC // 2 - 1)
            add_tiles("down1", "final1")
            rsqrt("final1")
            for k in range(DC + 1):
                if k < DC:
                    v.scalar_tensor_tensor(x[:, k, :], x[:, k, :], prm("norm_final_g", k), rstd[:, :], ALU.mult,
                                           ALU.mult).then_inc(x_ready, 1)
                if k:
                    add_square("pre1", k - 1)
            norm_to_split("pre1", "pre1", "ffn1_pre_g")

            def hiddens(stage, turn):
                first, t0 = UNIT[stage][0], TILE[stage, 0]
                slots = [gate, silu]
                with dve.Fori(0, FC // 2) as it:
                    for j in range(2):
                        g, u = (t0 + 2 * j) % BANKS, (t0 + 2 * j + 1) % BANKS
                        dve.wait_ge(bank_free[g], (t0 + 2 * j) // BANKS + 1 + it)
                        dve.wait_ge(unit_done, first + 2 * j + 2 + it * 4)
                        v.tensor_tensor(val[:, :], slots[j][:, :], bank[u][:, :], ALU.mult).then_inc(
                            bank_free[u], 1)
                        dve.wait_ge(bank_free[u], (t0 + 2 * j + 1) // BANKS + 1 + it)
                        v.tensor_scalar(hidden_at(h_hi, it, j), val[:, :], 1.0, None, ALU.mult).then_inc(
                            high_done, 1)
                        dve.wait_ge(high_done, FC * turn + j + 1 + it * 2)
                        v.tensor_tensor(hidden_at(h_lo, it, j), val[:, :],
                                        hidden_at(h_hi, it, j).bitcast(F32), ALU.subtract).then_inc(
                            hidden_ready, 1)
                        dve.wait_ge(hidden_ready, FC * turn + j + 1 + it * 2)

            def branch_kept(stage, square_stage):
                for k in range(DC):
                    add_square(square_stage, k)

            hiddens("up2", 1)
            branch_kept("down2", "post1")
            add_branch("post1", "ffn1_post_g", y, lambda k: tile_read("down2", k), x_ready, DC, "mixpre")
            norm_to_split("mixpre", "mixpre", "mix_pre_g")
            rsqrt("ckv")
            wait(tile_read("proj2", 0))
            v.scalar_tensor_tensor(ckv[:, :], ckv_raw[:, :], prm("kv_norm_g"), rstd[:, :], ALU.mult,
                                   ALU.mult).then_inc(norm_ready, 1)
            dve.wait_ge(norm_ready, 1)
            rsqrt("kidx")
            wait(tile_read("proj2", 1))
            v.scalar_tensor_tensor(kidx[:, :], kidx_raw[:, :], prm("kidx_norm_g"), rstd[:, :], ALU.mult,
                                   ALU.mult).then_inc(norm_ready, 1)
            dve.wait_ge(aux_ready, AUX["wturn", 0] + 1)
            v.tensor_scalar(widx[:, :, :], aux_bank("wturn", 0)[:, 0:32].rearrange("p (j h) -> p j h", j=QB),
                            IDX_W_SCALE, None, ALU.mult).then_inc(aux_sem("wturn", 0), 1)
            wait(aux_read("wturn", 0))

            def top8(i):
                step(v.max(best[:, :], score[i][:, :]))
                step(v.match_replace(score[i][:, :], best[:, :], score[i][:, :], TAKEN))

            def selected(i):
                step(v.tensor_scalar(score[i][:, :], score[i][:, :], -2e38, NEG, ALU.is_gt, ALU.mult))

            dve.wait_ge(const2_loaded, 16 * 3)
            for s, (i, h) in enumerate(IDX_STEPS):
                w = (i + 1) * P
                wait(aux_read("idx", s))
                if h == 0:
                    v.tensor_scalar(score[i][:, :], relu[:, s % 2, 0:w], widx[:, i, h:h + 1], None,
                                    ALU.mult).then_inc(relu_used, 1)
                else:
                    v.scalar_tensor_tensor(score[i][:, :], relu[:, s % 2, 0:w], widx[:, i, h:h + 1],
                                           score[i][:, :], ALU.mult, ALU.add).then_inc(relu_used, 1)
                dve.wait_ge(relu_used, s + 1)
                if h == DSA_HEADS - 1:
                    step(v.tensor_tensor(score[i][:, i * P:], score[i][:, i * P:], tri[:, :], ALU.add))
                if i < QB - 1:
                    for _r in range(2):
                        top8(i + 1)
                    if h == DSA_HEADS - 1:
                        selected(i + 1)
            for _r in range(TOPK // 8):
                top8(1)
            selected(1)
            for a in range(35):
                if a < 32:
                    h, i = a // QB, a % QB
                    end, s = (i + 1) * P, a % 2
                    if i == 0:
                        dve.wait_ge(bias_in[h % 2], 16 * (h // 2 + 1))
                    dve.wait_ge(aux_ready, AUX["logit", a] + 1)
                    if a >= 2:
                        dve.wait_ge(exp2_done, a - 1)
                    first_col = (QB - 1 - i) * P
                    v.tensor_tensor(logit[:, s, 0:end], aux_bank("logit", a)[:, 0:end],
                                    t_bias[:, h % 2, first_col:first_col + end], ALU.add).then_inc(
                        aux_sem("logit", a), 1)
                    wait(aux_read("logit", a))
                    step(v.tensor_tensor(logit[:, s, 0:end], logit[:, s, 0:end], score[i][:, :], ALU.add))
                    step(v.tensor_reduce(small[:, 6:7], logit[:, s, 0:end], AX_X, ALU.max))
                    v.tensor_scalar(small[:, 24 + s:25 + s], small[:, 6:7], -1.0, None, ALU.mult).then_inc(
                        logit_max, 1)
                    dve.wait_ge(logit_max, a + 1)
                if 1 <= a <= 32:
                    b = a - 1
                    end, s = (b % QB + 1) * P, b % 2
                    dve.wait_ge(exp2_done, b + 1)
                    if b >= 2:
                        dve.wait_ge(aux_ready, AUX["turn2", b - 2] + 1)
                        dve.wait_ge(attn2_ready, b)
                    step(v.reciprocal(small[:, 28 + s:29 + s], small[:, 26 + s:27 + s]))
                    v.tensor_scalar(attn2[:, s, 0:end], prob2[:, s, 0:end], small[:, 28 + s:29 + s], None,
                                    ALU.mult).then_inc(attn2_ready, 1)
                if a >= 10 and a % 8 == 2:
                    t = (a - 10) // 8
                    c = SPLIT["y"] + t
                    dve.wait_ge(aux_ready, AUX["ya", t] + 1)
                    slot_free(c)
                    step(v.tensor_copy(chunk[:, c % 2, :], aux_bank("ya", t)[:, :]))
                    dve.sem_inc(aux_sem("ya", t), 1)
                    dve.sem_inc(chunk_ready, 1)
                    low(c, a_lo[:, t, :], a_hi[:, t, :])
            dve.wait_ge(lam_exp, 2)
            step(v.tensor_scalar(small[:, 40:44], small[:, 36:40], -1.0, 1.0, ALU.mult, ALU.add))
            dve.wait_ge(const3_loaded, 32)
            step(v.memset(pair_d[:, :, :], 0.0))
            for h in range(HEADS):
                s = h % 2
                dve.wait_ge(h_loaded[s], 32 * (h // 2 + 1))
                v.tensor_scalar(hf[:, s, :], hf[:, s, :], small[:, 40 + h:41 + h], small[:, 36 + h:37 + h],
                                ALU.mult, ALU.add).then_inc(f_ready, 1)
                dve.wait_ge(f_ready, h + 1)
                v.tensor_scalar(hk[:, s, :], hf[:, s, :], -1.0, 1.0, ALU.mult, ALU.add).then_inc(k_ready, 1)
                dve.wait_ge(k_ready, h + 1)
                dve.wait_ge(logf_ready, h + 1)
                for n in range(3):
                    step(v.tensor_tensor_scan(run[:, s, n, :], resets[:, n, :], logf[:, :], 0.0, ALU.mult,
                                              ALU.add))

                def make_diff(l):
                    e, b = h * len(LEVELS) + l, LEVELS[l]
                    src = run[:, s, max(0, l - 6), :].rearrange("p (n c) -> p n c", c=2 * b)
                    to = diff[:, e % 2, :].rearrange("p (n c) -> p n c", c=2 * b)
                    mid = src[:, :, b - 1:b].broadcast_to([P, T // (2 * b), b])
                    ins_ = v.tensor_tensor(to[:, :, 0:b], mid, src[:, :, 0:b], ALU.subtract)
                    if b <= 32:
                        ins_ = v.tensor_tensor(to[:, :, b:2 * b], src[:, :, b:2 * b], mid, ALU.subtract)
                    ins_.then_inc(diff_ready, 1)

                def make_qk(l):
                    e, b = h * len(LEVELS) + l, LEVELS[l]
                    part = lambda ap: ap.rearrange("p (n c) -> p n c", c=2 * b)
                    dve.wait_ge(decay_ready, decays(h, l))
                    if e >= 2:
                        dve.wait_ge(aux_ready, AUX["pair", (e - 2) // 9, (e - 2) % 9] + 1)
                    to, d = part(qk[:, e % 2, :]), part(decay[:, e % 2, :])
                    v.tensor_tensor(to[:, :, 0:b], part(hk[:, s, :])[:, :, 0:b], d[:, :, 0:b], ALU.mult)
                    v.tensor_tensor(to[:, :, b:2 * b], part(hq[:, s, :])[:, :, b:2 * b], d[:, :, b:2 * b],
                                    ALU.mult).then_inc(qk_ready, 1)

                def keep_pairs(name, level):
                    dve.wait_ge(aux_ready, AUX[name] + 1)
                    view = lambda ap: ap.rearrange("p (n t) -> p n t", n=QB)
                    mask = masks[:, level:level + 1, :]
                    v.copy_predicated(view(pair_d[:, s, :]), mask.broadcast_to([P, QB, P]),
                                      view(aux_bank(*name)[:, :])).then_inc(aux_sem(*name), 1)
                    wait(aux_read(*name))

                if h >= 2:
                    dve.wait_ge(head_ready, HEADS + DSA_HEADS + h - 1)
                if h:
                    dve.wait_ge(decay_ready, decays(h, 0) - 1)
                make_diff(0)
                keep_pairs(("pair0", h), 0)
                for l in range(len(LEVELS)):
                    if l + 1 < len(LEVELS):
                        if l >= 1:
                            dve.wait_ge(decay_ready, decays(h, l - 1))
                        make_diff(l + 1)
                    make_qk(l)
                    if 1 <= l <= 7:
                        keep_pairs(("pair", h, l - 1), l)
            for h in range(HEADS):
                c = SPLIT["y"] + 4 + h
                if h == 0:
                    dve.wait_ge(hg_loaded, 16 * HEADS)
                rsqrt(f"hgrn{h}")
                wait(tile_read("hgrn", h))
                step(v.scalar_tensor_tensor(oh[:, h, :], oh[:, h, :], prm("hgrn_norm_g"), rstd[:, :], ALU.mult,
                                            ALU.mult))
                slot_free(c)
                v.tensor_tensor(chunk[:, c % 2, :], oh[:, h, :], hg[:, h, :], ALU.mult).then_inc(chunk_ready, 1)
                made(c)
                low(c, a_lo[:, 4 + h, :], a_hi[:, 4 + h, :])
            for m in range(DC):
                c = SPLIT["merged"] + m
                dve.wait_ge(gates_loaded[m % 2], 32 * (m // 2 + 1))
                for n in range(2):
                    wait(tile_done("branch", 2 * m + n))
                    v.tensor_tensor(gated[:, n, :], gates_in[:, 2 * (m % 2) + n, :],
                                    tile_bank("branch", 2 * m + n)[:, :], ALU.mult).then_inc(
                        tile_sem("branch", 2 * m + n), 1)
                    wait(tile_read("branch", 2 * m + n))
                slot_free(c)
                v.tensor_tensor(chunk[:, c % 2, :], gated[:, 0, :], gated[:, 1, :], ALU.add).then_inc(
                    chunk_ready, 1)
                made(c)
                low(c, h_lo[:, m, :], h_hi[:, m, :])
            branch_kept("out", "postmix")
            add_branch("postmix", "mix_post_g", y, lambda k: tile_read("out", k), x_ready, 2 * DC, "pre2")
            norm_to_split("pre2", "pre2", "ffn2_pre_g")
            hiddens("up3", 2)
            for c in range(2):
                dve.wait_ge(p_loaded, 32)
                n = SPLIT["p"] + c
                slot_free(n)
                v.tensor_copy(chunk[:, n % 2, :], pe_in[:, c, :]).then_inc(chunk_ready, 1)
                made(n)
                low(n, a_hi[:, 2 + c, :], a_hi[:, c, :])
            branch_kept("down3", "post2")
            add_branch("post2", "ffn2_post_g", y, lambda k: tile_read("down3", k), x_ready, 3 * DC, "plepre")
            norm_to_split("plepre", "plepre", "ple_pre_g")
            slots = [gate, silu]
            for k in range(DC + 1):
                if k < DC:
                    wait(tile_read("ple", k))
                    wait(tile_read("pproj", k))
                    v.tensor_tensor(p_proj[:, k, :], p_proj[:, k, :], slots[k % 2][:, :], ALU.mult).then_inc(
                        y_ready, 1)
                if k:
                    add_square("plepost", k - 1)
            add_branch("plepost", "ple_post_g", p_proj, None, out_ready, 0)


def _units(w, blocks, columns=None):
    k, n = w.shape
    tiles = w.reshape(k // P, P, n // P, P).transpose(2, 0, 1, 3)
    parts = tiles.reshape(n // P, k // P // blocks, blocks, P, P)
    return parts.transpose(0, 1, 3, 2, 4).reshape(-1, P, blocks * P)


def _interleave(a, b, blocks):
    a, b = _units(a, blocks), _units(b, blocks)
    return np.stack([a, b], axis=1).reshape(-1, P, blocks * P)


def _cols(v):
    return np.asarray(v).reshape(-1, P).T


def _layout(i):
    w2 = i["w_in_2"][0]
    at = {}
    pos = 0
    for name, n in (("qa", 512), ("ckv", 128), ("qi", 512), ("kidx", 64), ("widx", 8), ("qh", 512), ("fh", 512),
                    ("i", 512), ("gh", 512), ("gate", 2048)):
        at[name] = pos
        pos += n

    def w2_cols(tile):
        name = tile.rstrip("0123456789")
        first = at[name] + P * int(tile[len(name):] or 0)
        if name == "kidx":
            return np.concatenate([w2[:, first:first + 64]] * 2, axis=1)
        return w2[:, first:first + P]

    w1 = i["w_in"][0]
    proj1 = np.concatenate([w1[:, 512:], w1[:, :512]], axis=1)
    up1 = i["w_up"][0]
    pproj = _units(i["w_ple_proj_2"][0], 2)
    arrays = {
        "w_proj1": _units(proj1, DC),
        "w_wo": _units(i["w_o"][0], DC),
        "w_up1": _interleave(up1[:, :FF], up1[:, FF:], DC),
        "w_down1": _units(i["w_down"][0], DOWN_CHUNKS),
        "w_up2": _interleave(i["ffn1_w_gate_2"][0], i["ffn1_w_up_2"][0], DC),
        "w_down2": _units(i["ffn1_w_down_2"][0], DOWN_CHUNKS),
        "w_proj2": _units(np.concatenate([w2_cols(t) for t in TILES2], axis=1), DC),
        "w_branch": _interleave(i["w_br_a_2"][0], i["w_br_b_2"][0], 4),
        "w_out": _units(i["w_out_2"][0], DC),
        "w_up3": _interleave(i["ffn2_w_gate_2"][0], i["ffn2_w_up_2"][0], DC),
        "w_down3": _units(i["ffn2_w_down_2"][0], DOWN_CHUNKS),
        "w_pproj": pproj.reshape(2, 4, P, 2 * P).transpose(0, 2, 1, 3).reshape(2, P, 8 * P),
        "w_ple": _units(i["w_ple_gate_2"][0], DC),
    }
    conv = i["conv_w"][0]
    inter = lambda v: np.stack([_cols(v[:FF]), _cols(v[FF:])], axis=2).reshape(P, -1)
    i_freq = (np.float32(10000.0) ** (-np.arange(0, 64, 2, dtype=np.float32) / np.float32(64))).astype(np.float32)
    par = {
        "norm_mix_g": _cols(i["norm_mix_g"]), "norm_ffn_g": _cols(i["norm_ffn_g"]),
        "norm_final_g": _cols(i["norm_final_g"]), "pool_scale": _cols(i["pool_scale"]),
        "attn_norm_g": _cols(i["attn_norm_g"]), "conv_w0": inter(conv[0]), "conv_w1": inter(conv[1]),
        "conv_w2": inter(conv[2]), "conv_b": inter(i["conv_b"][0]),
        "ffn1_pre_g": _cols(i["ffn1_pre_g_2"]), "ffn1_post_g": _cols(i["ffn1_post_g_2"]),
        "mix_pre_g": _cols(i["mix_pre_g_2"]), "mix_post_g": _cols(i["mix_post_g_2"]),
        "kv_norm_g": _cols(i["kv_norm_g_2"]),
        "kidx_norm_g": _cols(np.concatenate([i["kidx_norm_g_2"][0]] * 2)),
        "hgrn_norm_g": _cols(i["hgrn_norm_g_2"]), "b_gate": _cols(i["b_gate_2"]),
        "ffn2_pre_g": _cols(i["ffn2_pre_g_2"]), "ffn2_post_g": _cols(i["ffn2_post_g_2"]),
        "ple_pre_g": _cols(i["ple_pre_g_2"]), "ple_post_g": _cols(i["ple_post_g_2"]),
        "hgrn_lb0": _cols(i["hgrn_lb_2"][0]), "hgrn_lb1": _cols(i["hgrn_lb_2"][1]),
        "inv_freq": _cols(np.tile(i_freq, 4)), "eps": np.full((P, 1), EPS, np.float32),
    }
    arrays["par"] = np.concatenate([par[name] for name in PARAMS], axis=1)
    arrays["xt"] = i["x"][0].T.reshape(DC, P, T)
    arrays["pt"] = i["p_2"][0, 0].T.reshape(2, P, T)
    arrays["positions"] = i["positions"]
    arrays["pool_w"] = i["pool_w"][0].transpose(1, 0, 2)
    arrays["lambdas"] = np.concatenate([i[n] for n in ("lambda_q1", "lambda_k1", "lambda_q2", "lambda_k2")])
    arrays["rel"] = i["rel_bias_2"]
    arrays["wuk"] = i["w_uk_2"][0].transpose(2, 0, 1).reshape(64, 4, 2, P).transpose(2, 0, 1, 3).reshape(P, 4, P)
    arrays["wuv"] = i["w_uv_2"][0].transpose(1, 0, 2)
    arrays.update(constants())
    return {name: np.ascontiguousarray(a) for name, a in arrays.items()}


def kernel(**inputs):
    import concourse.bacc as bacc
    from concourse.bass_utils import run_bass_kernel_spmd

    nc = bacc.Bacc("TRN2", target_bir_lowering=False, num_devices=1)
    arrays = _layout({name: np.asarray(a) for name, a in inputs.items()})
    ins = {name: nc.dram_tensor(f"in_{name}", a.shape, mybir.dt.from_np(a.dtype), kind="ExternalInput").ap()
           for name, a in arrays.items()}
    spill = nc.dram_tensor("spill", (28, P, T), F32, kind="Internal").ap()
    bias_rows = nc.dram_tensor("bias_rows", (DSA_HEADS, P, BIAS_COLS), F32, kind="Internal").ap()
    out = nc.dram_tensor("out_t", (DC, P, T), F32, kind="ExternalOutput").ap()
    two_blocks(nc, ins, spill, bias_rows, out)
    result = run_bass_kernel_spmd(nc, [{f"in_{name}": a for name, a in arrays.items()}], core_ids=[0])
    return np.ascontiguousarray(result.results[0]["out_t"].reshape(D, T).T)[None]
```

```python
from contextlib import ExitStack

import numpy as np

import concourse.bass as bass
from concourse import mybir

F32 = mybir.dt.float32
F32R = mybir.dt.float32r
I32 = mybir.dt.int32
ALU = mybir.AluOpType
ACT = mybir.ActivationFunctionType
AX_X = mybir.AxisListType.X

P = 128
T = 512
D = 1024
DC = D // P
FF = 2816
FC = FF // P
QB = T // P
EPS = 1e-6
HEADS = 4
DSA_HEADS = 8
DIFF_SCALE = 64 ** -0.5
ATT_SCALE = 64 ** -0.5
IDX_W_SCALE = (8 ** -0.5) * (64 ** -0.5)
TOPK = 128
LAM_INIT = 0.2
WINDOWS = (2, 4, 8, 16)
PAD = max(WINDOWS)
NEG = -1e30
TAKEN = -3e38
LEVELS = (1, 2, 4, 8, 16, 32, 64, 128, 256)
DOWN_CHUNKS = FC // 2
SLOT = DOWN_CHUNKS * P
RAW_SLOTS = 4
SPLIT_SLOTS = 2
BANKS = 4
AUX_BANKS = 3
BIAS_COLS = 640

PARAMS = {}
_at = 0
for _name, _n in (("norm_mix_g", 8), ("norm_ffn_g", 8), ("norm_final_g", 8), ("pool_scale", 4),
                  ("attn_norm_g", 4), ("conv_w0", 44), ("conv_w1", 44), ("conv_w2", 44), ("conv_b", 44),
                  ("ffn1_pre_g", 8), ("ffn1_post_g", 8), ("mix_pre_g", 8), ("mix_post_g", 8),
                  ("kv_norm_g", 1), ("kidx_norm_g", 1), ("hgrn_norm_g", 1), ("b_gate", 16),
                  ("ffn2_pre_g", 8), ("ffn2_post_g", 8), ("ple_pre_g", 8), ("ple_post_g", 8),
                  ("hgrn_lb0", 4), ("hgrn_lb1", 4), ("inv_freq", 1), ("eps", 1)):
    PARAMS[_name] = (_at, _n)
    _at += _n
N_PARAMS = _at

TILES2 = (["ckv", "kidx", "widx"] + [f"qi{t}" for t in range(4)] + [f"qa{t}" for t in range(4)]
          + [f"i{t}" for t in range(4)] + [f"qh{t}" for t in range(4)] + [f"gh{t}" for t in range(4)]
          + [f"fh{t}" for t in range(4)] + [f"gate{t}" for t in range(16)])
TILES1 = [(kind, h) for h in range(HEADS) for kind in "qkv"] + [("p", g) for g in range(len(WINDOWS))]
LEAD1 = 3
LEAD2 = TILES2.index("gate0") + 2
STAGES = (("proj1", 16, DC), ("wo", DC, DC), ("up1", 2 * FC, DC), ("down1", 2 * DC, DOWN_CHUNKS),
          ("up2", 2 * FC, DC), ("down2", 2 * DC, DOWN_CHUNKS), ("proj2", len(TILES2), DC),
          ("branch", 2 * DC, 4), ("out", DC, DC),
          ("up3", 2 * FC, DC), ("down3", 2 * DC, DOWN_CHUNKS), ("pproj", 2, DC), ("ple", DC, DC))
UNIT = {}
_at = 0
for _name, _n, _c in STAGES:
    UNIT[_name] = (_at, _n, _c)
    _at += _n

BLOCKS_OF = [c for _, n, c in STAGES for _i in range(n)]



def spread(first_tile, end_tile, rates):
    steps, at, end = [], first_tile * DC, end_tile * DC
    for rate in rates:
        pieces, left = [], min(rate, end - at)
        while left:
            n = min(left, DC - at % DC)
            pieces.append((at // DC, at % DC, at % DC + n))
            at, left = at + n, left - n
        steps.append(pieces)
    assert at == end, (at, end)
    return steps


def closed(pieces):
    return [t for t, _, end in pieces if end == DC]


ATT_STEPS = 16
FILL1 = spread(LEAD1, len(TILES1), [7] * ATT_STEPS)
DSA_STEPS = DSA_HEADS * QB
HGRN_STEPS = HEADS * len(LEVELS)
_dsa_rate = 2
_left = (len(TILES2) - LEAD2) * DC - _dsa_rate * (DSA_STEPS + 3)
FILL2 = spread(LEAD2, len(TILES2), [_dsa_rate] * (DSA_STEPS + 3) + [
    _left * (e + 1) // HGRN_STEPS - _left * e // HGRN_STEPS for e in range(HGRN_STEPS)])

TILE = {}
_uses = [0] * BANKS


def _tile(name, i, bank_):
    TILE[name, i] = (bank_, _uses[bank_])
    _uses[bank_] += 1


def _tiles(name, first, end, over=BANKS, start=0):
    for i in range(first, end):
        _tile(name, i, start + i % over)


_tiles("proj1", 0, 16, 2)
_tiles("attn", 0, HEADS, 2, 2)
_tiles("wo", 0, DC)
_tiles("up1", 0, 2 * FC)
_tiles("down1", 0, DC)
_tiles("up2", 0, 2 * FC)
_tiles("down2", 0, DC)
_tiles("proj2", 0, TILES2.index("gate0"))
_tiles("proj2", TILES2.index("gate0"), len(TILES2), 2)
_tiles("olat", 0, DSA_HEADS, 2, 2)
_tiles("hgrn", 0, HEADS, 2, 2)
_tiles("branch", 0, 2 * DC)
_tiles("out", 0, DC)
_tiles("up3", 0, 2 * FC)
_tiles("down3", 0, DC)
_tiles("pproj", 0, DC)
_tiles("ple", 0, DC)

AUX = {}


def _aux(*name):
    AUX[name] = len(AUX)


def aux_of_tile1(t):
    kind, h = TILES1[t]
    return {"q": ("rope", 2 * h), "k": ("rope", 2 * h + 1), "v": ("vtok", h), "p": None}[kind]


AUX1 = [[LEAD1 - 1] if a == 0 else [t for t in closed(FILL1[a - 1]) if aux_of_tile1(t)] for a in range(ATT_STEPS)]
for _t in range(LEAD1 - 1):
    _aux(*aux_of_tile1(_t))
for _a in range(ATT_STEPS + 1):
    if _a == 0:
        _aux(*aux_of_tile1(LEAD1 - 1))
    if _a < ATT_STEPS:
        _aux("score", _a, 0)
        _aux("score", _a, 1)
    if 0 < _a < ATT_STEPS:
        for _t in AUX1[_a]:
            _aux(*aux_of_tile1(_t))
    if _a:
        _aux("turn", _a - 1)
    if _a < ATT_STEPS:
        _aux("bias", _a)
for _g in range(len(WINDOWS)):
    _aux("pool", _g)
IDX_STEPS = [(i, h) for i in (3, 2, 1) for h in range(DSA_HEADS)]
AFTER2 = {n: [] for n in range(len(TILES2))}
AFTER2[1].append(("stat", "ckv"))
AFTER2[2].append(("stat", "kidx"))
AFTER2[3].append(("wturn", 0))
AFTER2[4].append(("ckvtok", 0))
for _t in range(4):
    AFTER2[8 + _t] += [("qlat", 2 * _t), ("qlat", 2 * _t + 1)]
    AFTER2[12 + _t].append(("vturn", _t))
_room = TILES2.index("gate0") - 1 - 7
for _s in range(len(IDX_STEPS)):
    AFTER2[7 + _s * _room // (len(IDX_STEPS) - 1)].append(("idx", _s))
for _n in AFTER2:
    for _ev in AFTER2[_n]:
        if _ev[0] != "stat":
            _aux(*_ev)
for _a in range(DSA_STEPS + 4):
    if _a < DSA_STEPS:
        _aux("logit", _a)
    if 2 <= _a < DSA_STEPS + 2:
        _aux("turn2", _a - 2)
    if _a >= 11 and _a % 8 == 3:
        _aux("ya", (_a - 11) // 8)
for _h in range(HEADS):
    _aux("pair0", _h)
    for _l in range(len(LEVELS)):
        _aux("pair", _h, _l)

STAT = {n: i for i, n in enumerate(
    ["norm1"] + [f"head{h}" for h in range(4)] + ["norm2", "final1", "pre1", "post1", "mixpre", "ckv", "kidx"]
    + [f"hgrn{h}" for h in range(4)] + ["postmix", "pre2", "post2", "plepre", "plepost"])}
SQUARE = {n: 8 * i for i, n in enumerate(
    ["norm1", "norm2", "final1", "pre1", "post1", "mixpre", "postmix", "pre2", "post2", "plepre", "plepost"])}
SPLIT = {}
_at = 0
for _name, _n in (("norm1", 8), ("mix1", 8), ("norm2", 8), ("pre1", 8), ("mixpre", 8), ("y", 8), ("merged", 8),
                  ("pre2", 8), ("p", 2), ("plepre", 8)):
    SPLIT[_name] = _at
    _at += _n


def bucket(dist):
    d_f = np.maximum(dist, 1).astype(np.float32)
    log_b = 16 + (np.log(d_f / np.float32(16)) / np.float32(np.log(8.0)) * np.float32(16)).astype(np.int32)
    return np.where(dist < 16, dist, np.minimum(log_b, 31))


def constants():
    i = np.arange(P)
    ident = np.eye(P, dtype=np.float32)
    rot = np.zeros((P, P), np.float32)
    for g in (0, 64):
        for j in range(32):
            rot[g + j + 32, g + j] = -1.0
            rot[g + j, g + j + 32] = 1.0
    onehot = np.zeros((P, BIAS_COLS), np.float32)
    onehot[bucket(np.maximum(T - 1 - np.arange(BIAS_COLS), 0)), np.arange(BIAS_COLS)] = 1.0
    count = np.ones((P, len(WINDOWS), PAD), np.float32)
    for g, w in enumerate(WINDOWS):
        count[:, g, :] = (1.0 / np.minimum(np.arange(PAD) + 1, w)).astype(np.float32)
    tri = np.where(i[None, :] > i[:, None], np.float32(-1e38), np.float32(0)).astype(np.float32)
    masks = np.zeros((P, 8, P), np.int32)
    masks[:, 0, :] = np.eye(P, dtype=np.int32)
    for l in range(7):
        b = LEVELS[l]
        s, t = i[:, None], i[None, :]
        masks[:, l + 1, :] = (s // (2 * b) == t // (2 * b)) & (s % (2 * b) < b) & (t % (2 * b) >= b)
    resets = np.ones((P, 3, T), np.float32)
    for n, seg in enumerate((64, 128, 256)):
        resets[:, n, ::seg] = 0.0
    return {"c_ident": ident, "c_ones": np.ones((P, P), np.float32), "c_rot": rot, "c_onehot": onehot[:32],
            "c_count": count.reshape(P, -1), "c_tri": tri, "c_masks": masks.reshape(P, -1),
            "c_resets": resets.reshape(P, -1)}

ROUND = 12582912.0
PI_BELOW = 3.1415925
TURN_PARTS = (6.28125, 8117 / 2 ** 22, float(2 * np.pi - 6.28125 - 8117 / 2 ** 22))


def decays(h, l):
    return 12 * h + (l + 1 if l < 6 else 6 + 2 * (l - 5))


LAST_UNIT = sum(n for _, n, _ in STAGES)


def two_blocks(nc, ins, spill, bias_rows, out):
    with ExitStack() as ctx:
        base = (nc.sbuf_base + 31) // 32 * 32
        arena_bytes = (nc.sbuf_usable_end - base) // 32 * 32 - 64
        ctx.enter_context(nc.sbuf_tensor("arena", [P, arena_bytes // 4], F32))
        limit = base + arena_bytes

        def placer(start, end):
            at = [start]

            def put(name, shape, dtype=F32):
                size = (int(np.prod(shape[1:])) * 4 + 31) // 32 * 32
                tensor = nc.alloc_sbuf_tensor_at(name, shape, dtype, offset=at[0])
                at[0] += size
                assert at[0] <= end, (name, at[0] - end)
                return tensor

            put.at = at
            return put

        keep = placer(base, limit)
        raw = keep("raw", [P, RAW_SLOTS, SLOT])
        w_hi = keep("w_hi", [P, SPLIT_SLOTS, SLOT], F32R)
        w_lo = keep("w_lo", [P, SPLIT_SLOTS, SLOT], F32R)
        x = keep("x", [P, DC, T])
        a_hi = keep("a_hi", [P, DC, T], F32R)
        y_at = keep.at[0]
        a_lo = keep("a_lo", [P, DC, T], F32R)
        room_at = keep.at[0]
        h_hi = keep("h_hi", [P, FC, T], F32R)
        h_lo = keep("h_lo", [P, FC, T], F32R)
        room_end = keep.at[0]
        par = keep("par", [P, N_PARAMS])
        ident = keep("ident", [P, P])
        ones = keep("ones", [P, P])
        sum_sq = keep("sum_sq", [P, T])
        sq = keep("sq", [P, 2, T])
        chunk = keep("chunk", [P, 2, T])
        root = keep("root", [P, T])
        rstd = keep("rstd", [P, T])
        gate = keep("gate", [P, T])
        val = keep("val", [P, T])
        silu = keep("silu", [P, T])
        small = keep("small", [P, 64])
        lam_in = keep("lam_in", [P, 4, 64])
        y = placer(y_at, room_at)("y", [P, DC, T])
        spill_slot = [gate, val]
        logf = silu

        r1 = placer(room_at, room_end)
        rot = r1("rot", [P, P])
        pool_w = r1("pool_w", [P, 4, P])
        count = r1("count", [P, 4, PAD])
        cos = r1("cos", [P, T])
        sin = r1("sin", [P, T])
        q1 = r1("q1", [P, HEADS, T])
        k1 = r1("k1", [P, HEADS, T])
        v1 = r1("v1", [P, QB, HEADS, P])
        o1 = r1("o1", [P, HEADS, T])
        neg_row = r1("neg_row", [1, P])
        one_row = r1("one_row", [1, 64])
        onehot = r1("onehot", [32, BIAS_COLS])
        rel = r1("rel", [32, DSA_HEADS])
        rel_wide = r1("rel_wide", [32, DSA_HEADS, P])
        bias_slot = r1("bias_slot", [P, 2, BIAS_COLS])
        before_softmax = r1.at[0]
        r1_angle = placer(before_softmax, room_end)
        pos_i = r1_angle("pos_i", [P, T], I32)
        angle = r1_angle("angle", [P, T])
        turns = r1_angle("turns", [P, T])
        prob = r1("prob", [P, 2, 2, T])
        unrot = r1("unrot", [P, 2, T])
        pool_in = r1("pool_in", [P, 2, PAD + T])
        pool_s = r1("pool_s", [P, 2, PAD + T])
        pool_d = r1("pool_d", [P, 4, T])
        rope_a = silu
        v1t = [gate, val]
        attn = r1("attn", [P, 2, T])
        attn_t = r1("attn_t", [P, 2, T])

        ya_at = room_end - 4 * T * 4
        ya = placer(ya_at, room_end)("ya", [P, 4, T])
        r2 = placer(room_at, ya_at)
        v2 = r2("v2", [P, QB, HEADS, P])
        r2_split = r2.at[0]
        ckv_raw = r2("ckv_raw", [P, T])
        ckv = r2("ckv", [P, T])
        ckv_tok = r2("ckv_tok", [P, QB, P])
        kidx_raw = r2("kidx_raw", [P, T])
        kidx = r2("kidx", [P, T])
        widx_t = r2("widx_t", [P, T])
        widx = r2("widx", [P, QB, DSA_HEADS])
        wuk = r2("wuk", [P, 4, P])
        wuv = r2("wuv", [P, DSA_HEADS, 64])
        tri = r2("tri", [P, P])
        qlat = r2("qlat", [P, DSA_HEADS, T])
        score = [tri] + [r2(f"score{i}", [P, (i + 1) * P]) for i in range(1, QB)]
        best = r2("best", [P, 8])
        t_bias = r2("t_bias", [P, 2, T])
        r2_under = placer(r2.at[0], ya_at)
        qa = r2_under("qa", [P, 2, T])
        relu = r2_under("relu", [P, 2, T])
        i_t = r2_under("i_t", [P, 2, T])
        logit = r2("logit", [P, 2, T])
        prob2 = r2("prob2", [P, 2, T])
        attn2 = r2("attn2", [P, 2, T])
        attn2_t = r2("attn2_t", [P, 2, T])
        olat = r2("olat", [P, 2, T])
        qidx = r2("qidx", [P, 4, T])
        r3 = placer(r2_split, ya_at)
        masks = r3("masks", [P, 8, P], I32)
        resets = r3("resets", [P, 3, T])
        hq = r3("hq", [P, 2, T])
        hf = r3("hf", [P, 2, T])
        hk = r3("hk", [P, 2, T])
        run = r3("run", [P, 2, 3, T])
        diff = r3("diff", [P, 2, T])
        decay = r3("decay", [P, 2, T])
        qk = r3("qk", [P, 2, T])
        pair_d = r3("pair_d", [P, 2, T])
        pair_1 = r3("pair_1", [P, 2, 2, P])
        pair_2 = r3("pair_2", [P, 2, 2, 2 * P])
        oh = r3("oh", [P, HEADS, T])
        hg = r3("hg", [P, HEADS, T])
        r4 = placer(room_at + 8 * T * 4, room_at + FC * T * 4)
        gates_in = r4("gates_in", [P, 4, T])
        gated = r4("gated", [P, 2, T])
        pe_in = placer(y_at - 4 * T * 4, y_at)("pe_in", [P, 2, T])
        p_proj = placer(room_at, room_end)("p_proj", [P, DC, T])

        bank = [ctx.enter_context(nc.psum_tensor(f"bank{i}", [P, T], F32)) for i in range(8)]
        stat_bank = bank[7]

        def tile_bank(stage, i):
            return bank[TILE[stage, i][0]]

        def aux_bank(*name):
            return bank[BANKS + AUX[name] % AUX_BANKS]

        def tile_sem(stage, i):
            return bank_free[TILE[stage, i][0]]

        def tile_read(stage, i):
            return tile_sem(stage, i), TILE[stage, i][1] + 1

        def tile_done(stage, i):
            per_tile = 2 if stage.startswith("down") else 1
            return unit_done, UNIT[stage][0] + per_tile * (i + 1)

        def aux_sem(*name):
            return aux_free[AUX[name] % AUX_BANKS]

        def aux_read(*name):
            return aux_sem(*name), AUX[name] // AUX_BANKS + 1

        def prm(name, i=0, rows=P):
            return par[0:rows, PARAMS[name][0] + i:PARAMS[name][0] + i + 1]

        def sem(name):
            return ctx.enter_context(nc.semaphore(name))

        raw_loaded = [sem(f"raw_loaded{i}") for i in range(RAW_SLOTS)]
        unit_high = sem("unit_high")
        unit_split = sem("unit_split")
        unit_done = sem("unit_done")
        bank_free = [sem(f"bank_free{i}") for i in range(BANKS)]
        aux_ready = sem("aux_ready")
        aux_free = [sem(f"aux_free{i}") for i in range(AUX_BANKS)]
        head_ready = sem("head_ready")
        total_ready = sem("total_ready")
        root_ready = sem("root_ready")
        rstd_ready = sem("rstd_ready")
        sq_ready = sem("sq_ready")
        sum_added = sem("sum_added")
        head_sq = sem("head_sq")
        chunk_ready = sem("chunk_ready")
        hi_ready = sem("hi_ready")
        act_ready = sem("act_ready")
        x_ready = sem("x_ready")
        y_ready = sem("y_ready")
        x_loaded = sem("x_loaded")
        const_loaded = sem("const_loaded")
        const1_loaded = sem("const1_loaded")
        const2_loaded = sem("const2_loaded")
        const3_loaded = sem("const3_loaded")
        p_loaded = sem("p_loaded")
        dve_step = sem("dve_step")
        act_step = sem("act_step")
        trig_in = sem("trig_in")
        trig = sem("trig")
        lam_sum = sem("lam_sum")
        lam_exp = sem("lam_exp")
        rel_set = sem("rel_set")
        rope_done = sem("rope_done")
        pool_ready = sem("pool_ready")
        neg_max = sem("neg_max")
        attn_ready = sem("attn_ready")
        bias_out = [sem(f"bias_out{i}") for i in range(2)]
        high_done = sem("high_done")
        silu_ready = sem("silu_ready")
        gate_ready = sem("gate_ready")
        hidden_ready = sem("hidden_ready")
        norm_ready = sem("norm_ready")
        relu_used = sem("relu_used")
        spill_out = [sem(f"spill_out{i}") for i in range(2)]
        bias_in = [sem(f"bias_in{i}") for i in range(2)]
        logit_max = sem("logit_max")
        exp2_done = sem("exp2_done")
        attn2_ready = sem("attn2_ready")
        h_loaded = [sem(f"h_loaded{i}") for i in range(2)]
        hg_loaded = sem("hg_loaded")
        f_ready = sem("f_ready")
        logf_ready = sem("logf_ready")
        k_ready = sem("k_ready")
        diff_ready = sem("diff_ready")
        decay_ready = sem("decay_ready")
        qk_ready = sem("qk_ready")
        gates_loaded = [sem(f"gates_loaded{i}") for i in range(2)]
        gates_open = sem("gates_open")
        out_ready = sem("out_ready")
        stored = sem("stored")

        block = ctx.enter_context(nc.Block())

        @block.sync
        def _(sp):
            def load_unit(src, u, slot, size):
                sp.dma_start(raw[:, slot, 0:size], src).then_inc(raw_loaded[slot], 16)

            def load_stage(name):
                first, n, blocks = UNIT[name]
                src = ins["w_" + name]
                size = blocks * P
                straight = max(0, RAW_SLOTS - first)
                for i in range(straight):
                    load_unit(src[i], first + i, (first + i) % RAW_SLOTS, size)
                loops = (n - straight) // RAW_SLOTS
                if loops:
                    with sp.Fori(0, loops) as it:
                        for j in range(RAW_SLOTS):
                            u = first + straight + j
                            sp.wait_ge(unit_split, u - RAW_SLOTS + 1 + it * RAW_SLOTS)
                            unit = src[bass.ds(it * RAW_SLOTS + (straight + j), 1), :, :]
                            load_unit(unit.rearrange("u p m -> (u p) m"), u, u % RAW_SLOTS, size)
                for i in range(straight + loops * RAW_SLOTS, n):
                    u = first + i
                    sp.wait_ge(unit_split, u - RAW_SLOTS + 1)
                    load_unit(src[i], u, u % RAW_SLOTS, size)

            for k in range(DC):
                sp.dma_start(x[:, k, :], ins["xt"][k]).then_inc(x_loaded, 16)
            sp.dma_start(par[:, :], ins["par"]).then_inc(const_loaded, 16)
            sp.dma_start(ident[:, :], ins["c_ident"]).then_inc(const_loaded, 16)
            sp.dma_start(ones[:, :], ins["c_ones"]).then_inc(const_loaded, 16)
            for name, n, _ in STAGES:
                load_stage(name)
            for k in range(DC):
                sp.wait_ge(out_ready, k + 1)
                sp.dma_start(out[k], x[:, k, :]).then_inc(stored, 16)
            sp.wait_ge(stored, 16 * DC)

        @block.gpsimd
        def _(pool):
            def split_unit(u, size, it=0, per_loop=0):
                slot, half = u % RAW_SLOTS, u % SPLIT_SLOTS
                hi, lo, src = w_hi[:, half, 0:size], w_lo[:, half, 0:size], raw[:, slot, 0:size]
                pool.wait_ge(unit_high, u + 1 + it * per_loop)
                pool.tensor_tensor(lo, src, hi.bitcast(F32), ALU.subtract).then_inc(unit_split, 1)

            for name, n, blocks in STAGES:
                first = UNIT[name][0]
                loops = n // RAW_SLOTS
                if loops:
                    with pool.Fori(0, loops) as it:
                        for j in range(RAW_SLOTS):
                            split_unit(first + j, blocks * P, it, RAW_SLOTS)
                for i in range(loops * RAW_SLOTS, n):
                    split_unit(first + i, blocks * P)

        @block.tensor
        def _(pe):
            mm = nc.tensor.matmul

            def wait(pair):
                pe.wait_ge(pair[0], pair[1])

            def wait_bank(stage, i, turn=0):
                number, former = TILE[stage, i]
                if former:
                    pe.wait_ge(bank_free[number], former + turn)

            def unit_blocks(u, n, dst, chunk_at, hi, lo, first, last, it=0, per_loop=0, ready=None):
                half = u % SPLIT_SLOTS
                pe.wait_ge(unit_split, u + 1 + it * per_loop)
                for c in range(n):
                    if ready is not None:
                        pe.wait_ge(ready[0], ready[1] + c + 1)
                    k = chunk_at + c
                    wh, wl = w_hi[:, half, c * P:(c + 1) * P], w_lo[:, half, c * P:(c + 1) * P]
                    mm(dst[:, :], wh, hi[:, k, :], start=(first and c == 0), stop=False)
                    mm(dst[:, :], wh, lo[:, k, :], start=False, stop=False)
                    step = mm(dst[:, :], wl, hi[:, k, :], start=False, stop=(last and c == n - 1))
                step.then_inc(unit_done, 1)

            def project(stage, i, ready=None, hi=a_hi, lo=a_lo):
                first, _, blocks = UNIT[stage]
                wait_bank(stage, i)
                unit_blocks(first + i, blocks, tile_bank(stage, i), 0, hi, lo, True, True, ready=ready)

            def fill(stage, pieces):
                for t, c0, c1 in pieces:
                    u, dst = UNIT[stage][0] + t, tile_bank(stage, t)
                    if c0 == 0:
                        wait_bank(stage, t)
                        pe.wait_ge(unit_split, u + 1)
                    for c in range(c0, c1):
                        cols = slice(c * P, (c + 1) * P)
                        wh, wl = w_hi[:, u % SPLIT_SLOTS, cols], w_lo[:, u % SPLIT_SLOTS, cols]
                        mm(dst[:, :], wh, a_hi[:, c, :], start=(c == 0), stop=False)
                        mm(dst[:, :], wh, a_lo[:, c, :], start=False, stop=False)
                        step = mm(dst[:, :], wl, a_hi[:, c, :], start=False, stop=(c == DC - 1))
                    if c1 == DC:
                        step.then_inc(unit_done, 1)

            def aux_wait(*name):
                n = AUX[name]
                if n >= AUX_BANKS:
                    pe.wait_ge(aux_free[n % AUX_BANKS], n // AUX_BANKS)
                return bank[BANKS + n % AUX_BANKS]

            def total(name, source, waits):
                n = STAT[name]
                for s, v in waits:
                    pe.wait_ge(s, v)
                if n:
                    pe.wait_ge(root_ready, n)
                mm(stat_bank[:, :], ones[:, :], source, start=True, stop=True).then_inc(total_ready, 1)

            def total_x(name):
                total(name, sum_sq[:, :], [(sum_added, SQUARE[name] + DC)])

            def hidden(stage, split=None):
                first, n, blocks = UNIT[stage]
                ready = (act_ready, SPLIT[split])
                project(stage, 0, ready)
                for j in range(1, 4):
                    project(stage, j)
                with pe.Fori(0, n // 4 - 1) as it:
                    for j in range(4, 8):
                        wait_bank(stage, j, it)
                        unit_blocks(first + j, blocks, tile_bank(stage, j), 0, a_hi, a_lo, True, True, it, 4)

            def down(stage, turn):
                first = UNIT[stage][0]
                pe.wait_ge(hidden_ready, FC * (turn + 1))
                with pe.Fori(0, DC // 4) as it:
                    for j in range(4):
                        wait_bank(stage, j, it)
                        for half in range(2):
                            unit_blocks(first + 2 * j + half, DOWN_CHUNKS, tile_bank(stage, j),
                                        half * DOWN_CHUNKS, h_hi, h_lo, half == 0, half == 1, it, 8)

            pe.wait_ge(const_loaded, 48)
            total_x("norm1")
            pe.wait_ge(const1_loaded, 16 * 7)

            def aux1(t):
                name = aux_of_tile1(t)
                dst = aux_wait(*name)
                wait(tile_read("proj1", t))
                if name[0] == "rope":
                    mm(dst[:, :], rot[:, :], unrot[:, name[1] % 2, :], start=True, stop=True).then_inc(aux_ready, 1)
                else:
                    for j in range(QB):
                        step = pe.transpose(dst[:, j * P:(j + 1) * P], v1t[name[1] % 2][:, j * P:(j + 1) * P],
                                            ident[:, :])
                    step.then_inc(aux_ready, 1)

            project("proj1", 0, (act_ready, SPLIT["norm1"]))
            project("proj1", 1)
            aux1(0)
            project("proj1", 2)
            aux1(1)
            for a in range(ATT_STEPS + 2):
                if a == 0:
                    fill("proj1", FILL1[0])
                    aux1(2)
                if a < ATT_STEPS:
                    h, i = a // QB, a % QB
                    end = (i + 1) * P
                    pe.wait_ge(rope_done, 2 * h + 2)
                    for n in range(2):
                        dst = aux_wait("score", a, n)
                        rows = slice(64 * n, 64 * n + 64)
                        mm(dst[:, 0:end], q1[rows, h, i * P:end], k1[rows, h, 0:end], start=True, stop=False)
                        mm(dst[:, end - 64:end], neg_row[0:1, :], one_row[0:1, :], start=False,
                           stop=True).then_inc(aux_ready, 1)
                if 0 < a < ATT_STEPS:
                    fill("proj1", FILL1[a])
                    for t in AUX1[a]:
                        aux1(t)
                if 1 <= a <= ATT_STEPS:
                    dst = aux_wait("turn", a - 1)
                    pe.wait_ge(attn_ready, a)
                    for j in range((a - 1) % QB + 1):
                        step = pe.transpose(dst[:, j * P:(j + 1) * P], attn[:, (a - 1) % 2, j * P:(j + 1) * P],
                                            ident[:, :])
                    step.then_inc(aux_ready, 1)
                if a < ATT_STEPS:
                    dst = aux_wait("bias", a)
                    pe.wait_ge(rel_set, 1)
                    cols = slice(0, T) if a % 2 == 0 else slice(T, BIAS_COLS)
                    mm(dst[:, 0:cols.stop - cols.start], rel_wide[:, a // 2, :], onehot[:, cols], start=True,
                       stop=True).then_inc(aux_ready, 1)
                if a >= 2:
                    b = a - 2
                    h, i = b // QB, b % QB
                    if i == 0:
                        wait_bank("attn", h)
                        wait(aux_read("vtok", h))
                    wait(aux_read("turn", b))
                    dst = tile_bank("attn", h)
                    for j in range(i + 1):
                        step = mm(dst[:, i * P:(i + 1) * P], v1[:, j, h, :], attn_t[:, b % 2, j * P:(j + 1) * P],
                                  start=(j == 0), stop=(j == i))
                    if i == QB - 1:
                        step.then_inc(head_ready, 1)
                if a == ATT_STEPS:
                    for g in range(len(WINDOWS)):
                        dst = aux_wait("pool", g)
                        pe.wait_ge(pool_ready, g + 1)
                        mm(dst[:, :], pool_w[:, g, :], pool_d[:, g, :], start=True, stop=True).then_inc(aux_ready, 1)
            for h in range(HEADS):
                total(f"head{h}", sq[:, h % 2, :], [(head_sq, h + 1)])
            for i in range(DC):
                project("wo", i, (act_ready, SPLIT["mix1"]) if i == 0 else None)
            total_x("norm2")
            hidden("up1", "norm2")
            down("down1", 0)
            total_x("final1")
            total_x("pre1")
            hidden("up2", "pre1")
            down("down2", 1)
            total_x("post1")
            total_x("mixpre")
            pe.wait_ge(const2_loaded, 16 * 3)
            for n in range(LEAD2):
                project("proj2", n, (act_ready, SPLIT["mixpre"]) if n == 0 else None)
                for kind, m in AFTER2[n]:
                    if kind == "stat":
                        total(m, sq[:, STAT[m] % 2, :], [(head_sq, 5 + (m == "kidx"))])
                    elif kind == "wturn":
                        dst = aux_wait(kind, m)
                        wait(tile_read("proj2", 2))
                        for j in range(QB):
                            step = pe.transpose(dst[:, j * 8:j * 8 + 8], widx_t[0:8, j * P:(j + 1) * P],
                                                ident[0:8, 0:8])
                        step.then_inc(aux_ready, 1)
                    elif kind == "ckvtok":
                        dst = aux_wait(kind, m)
                        pe.wait_ge(norm_ready, 1)
                        for j in range(QB):
                            step = pe.transpose(dst[:, j * P:(j + 1) * P], ckv[:, j * P:(j + 1) * P], ident[:, :])
                        step.then_inc(aux_ready, 1)
                    elif kind == "qlat":
                        dst = aux_wait(kind, m)
                        wait(tile_read("proj2", 7 + m // 2))
                        rows = slice(64 * (m % 2), 64 * (m % 2) + 64)
                        mm(dst[:, :], wuk[rows, m // 2, :], qa[rows, (m // 2) % 2, :], start=True,
                           stop=True).then_inc(aux_ready, 1)
                    elif kind == "vturn":
                        dst = aux_wait(kind, m)
                        wait(tile_read("proj2", 11 + m))
                        for j in range(QB):
                            step = pe.transpose(dst[:, j * P:(j + 1) * P], i_t[:, m % 2, j * P:(j + 1) * P],
                                                ident[:, :])
                        step.then_inc(aux_ready, 1)
                    else:
                        dst = aux_wait(kind, m)
                        i, h = IDX_STEPS[m]
                        pe.wait_ge(norm_ready, 2)
                        wait(tile_read("proj2", 3 + h // 2))
                        rows = slice(64 * (h % 2), 64 * (h % 2) + 64)
                        mm(dst[:, 0:(i + 1) * P], qidx[rows, h // 2, i * P:(i + 1) * P],
                           kidx[rows, 0:(i + 1) * P], start=True, stop=True).then_inc(aux_ready, 1)
            for a in range(DSA_STEPS + 4):
                if a < DSA_STEPS:
                    h, i = a // QB, a % QB
                    end = (i + 1) * P
                    dst = aux_wait("logit", a)
                    wait(aux_read("qlat", h))
                    mm(dst[:, 0:end], qlat[:, h, i * P:end], ckv[:, 0:end], start=True,
                       stop=True).then_inc(aux_ready, 1)
                if 2 <= a < DSA_STEPS + 2:
                    b = a - 2
                    dst = aux_wait("turn2", b)
                    pe.wait_ge(attn2_ready, b + 1)
                    for j in range(b % QB + 1):
                        step = pe.transpose(dst[:, j * P:(j + 1) * P], attn2[:, b % 2, j * P:(j + 1) * P],
                                            ident[:, :])
                    step.then_inc(aux_ready, 1)
                if a < DSA_STEPS + 3:
                    fill("proj2", FILL2[a])
                if 3 <= a < DSA_STEPS + 3:
                    b = a - 3
                    h, i = b // QB, b % QB
                    if i == 0:
                        wait_bank("olat", h)
                        wait(aux_read("ckvtok", 0))
                    wait(aux_read("turn2", b))
                    dst = tile_bank("olat", h)
                    for j in range(i + 1):
                        step = mm(dst[:, i * P:(i + 1) * P], ckv_tok[:, j, :],
                                  attn2_t[:, b % 2, j * P:(j + 1) * P], start=(j == 0), stop=(j == i))
                    if i == QB - 1:
                        step.then_inc(head_ready, 1)
                if a >= 11 and a % 8 == 3:
                    t = (a - 11) // 8
                    dst = aux_wait("ya", t)
                    wait(tile_read("olat", 2 * t))
                    wait(tile_read("olat", 2 * t + 1))
                    for n in range(2):
                        step = mm(dst[64 * n:64 * n + 64, :], wuv[:, 2 * t + n, :], olat[:, n, :], start=True,
                                  stop=True)
                    step.then_inc(aux_ready, 1)
            def hgrn_out(h):
                wait_bank("hgrn", h)
                for l in (6, 7, 8):
                    wait(aux_read("pair", h, l))
                wait(aux_read("vturn", h))
                s = h % 2
                dst = tile_bank("hgrn", h)
                for i in range(QB):
                    blocks = [(i, pair_d[:, s, i * P:(i + 1) * P])]
                    if i % 2:
                        blocks.append((i - 1, pair_1[:, s, i // 2, :]))
                    if i >= 2:
                        blocks += [(j, pair_2[:, s, j, (i - 2) * P:(i - 1) * P]) for j in range(2)]
                    for n, (j, pairs) in enumerate(blocks):
                        step = mm(dst[:, i * P:(i + 1) * P], v2[:, j, h, :], pairs, start=(n == 0),
                                  stop=(n == len(blocks) - 1))
                step.then_inc(head_ready, 1)

            for h in range(HEADS):
                s = h % 2
                dst = aux_wait("pair0", h)
                pe.wait_ge(k_ready, h + 1)
                for j in range(QB):
                    cols = slice(j * P, (j + 1) * P)
                    step = mm(dst[:, cols], hk[:, s, cols], hq[:, s, cols], start=True, stop=True)
                step.then_inc(aux_ready, 1)
                for l, b in enumerate(LEVELS):
                    e = h * len(LEVELS) + l
                    dst = aux_wait("pair", h, l)
                    pe.wait_ge(qk_ready, e + 1)
                    if b <= 64:
                        pieces = [(j, j * P, P, j * P) for j in range(QB)]
                    elif b == 128:
                        pieces = [(0, P, P, 0), (2, 3 * P, P, P)]
                    else:
                        pieces = [(0, 2 * P, 2 * P, 0), (1, 2 * P, 2 * P, 2 * P)]
                    for j, q0, n, col in pieces:
                        step = mm(dst[:, col:col + n], qk[:, e % 2, j * P:(j + 1) * P], qk[:, e % 2, q0:q0 + n],
                                  start=True, stop=True)
                    step.then_inc(aux_ready, 1)
                    fill("proj2", FILL2[DSA_STEPS + 3 + e])
                    if h and l == 2:
                        hgrn_out(h - 1)
            hgrn_out(HEADS - 1)
            for h in range(HEADS):
                total(f"hgrn{h}", sq[:, h % 2, :], [(head_sq, 7 + h)])
            for i in range(2 * DC):
                first = UNIT["branch"][0]
                wait_bank("branch", i)
                chunks = 4 * (i % 2)
                unit_blocks(first + i, 4, tile_bank("branch", i), chunks, a_hi, a_lo, True, True,
                            ready=(act_ready, SPLIT["y"] + chunks) if i < 2 else None)
            for i in range(DC):
                project("out", i, (act_ready, SPLIT["merged"]) if i == 0 else None, h_hi, h_lo)
            total_x("postmix")
            total_x("pre2")
            hidden("up3", "pre2")
            down("down3", 2)
            for i in range(DC):
                dst, u = tile_bank("pproj", i), UNIT["pproj"][0] + i // 4
                wait_bank("pproj", i)
                pe.wait_ge(unit_split, u + 1)
                if i == 0:
                    pe.wait_ge(act_ready, SPLIT["p"] + 2)
                for c in range(2):
                    cols = slice((2 * (i % 4) + c) * P, (2 * (i % 4) + c + 1) * P)
                    wh, wl = w_hi[:, u % SPLIT_SLOTS, cols], w_lo[:, u % SPLIT_SLOTS, cols]
                    mm(dst[:, :], wh, a_hi[:, c, :], start=(c == 0), stop=False)
                    mm(dst[:, :], wh, a_hi[:, 2 + c, :], start=False, stop=False)
                    step = mm(dst[:, :], wl, a_hi[:, c, :], start=False, stop=(c == 1))
                step.then_inc(unit_done if i % 4 == 3 else head_ready, 1)
            total_x("post2")
            total_x("plepre")
            for i in range(DC):
                project("ple", i, (act_ready, SPLIT["plepre"]) if i == 0 else None)
            total_x("plepost")

        @block.scalar
        def _(act):
            fn = nc.scalar.activation

            def wait(pair):
                act.wait_ge(pair[0], pair[1])

            def unit_high_part(u, it=0, per_loop=0):
                if u >= LAST_UNIT:
                    return
                slot, size = u % RAW_SLOTS, BLOCKS_OF[u] * P
                act.wait_ge(raw_loaded[slot], 16 * (u // RAW_SLOTS + 1) + it * (16 * per_loop // RAW_SLOTS))
                fn(w_hi[:, u % SPLIT_SLOTS, 0:size], raw[:, slot, 0:size], ACT.Copy).then_inc(unit_high, 1)

            def units_done(v, it=0, per_loop=0):
                act.wait_ge(unit_done, v + it * per_loop)
                unit_high_part(v + 1, it, per_loop)

            def tile_finished(stage, i):
                per_tile = 2 if stage.startswith("down") else 1
                for n in range(per_tile):
                    units_done(UNIT[stage][0] + per_tile * i + n + 1)

            def square(stage, k, src, made):
                q = SQUARE[stage] + k
                wait(made)
                if q >= 2:
                    act.wait_ge(sum_added, q - 1)
                fn(sq[:, q % 2, :], src, ACT.Square).then_inc(sq_ready, 1)

            def take_root(name, width):
                n = STAT[name]
                act.wait_ge(total_ready, n + 1)
                if n:
                    act.wait_ge(rstd_ready, n)
                fn(root[:, :], stat_bank[:, :], ACT.Sqrt, bias=prm("eps"), scale=1.0 / width).then_inc(root_ready, 1)

            def high(c, dst):
                act.wait_ge(chunk_ready, c + 1)
                fn(dst, chunk[:, c % 2, :], ACT.Copy).then_inc(hi_ready, 1)

            def highs(stage, first=0, n=DC, dst=a_hi):
                for k in range(first, first + n):
                    high(SPLIT[stage] + k, dst[:, k, :])

            def keep_branch(stage, square_stage):
                for k in range(DC):
                    tile_finished(stage, k)
                    square(square_stage, k, tile_bank(stage, k)[:, :], tile_done(stage, k))
                    fn(y[:, k, :], tile_bank(stage, k)[:, :], ACT.Copy).then_inc(tile_sem(stage, k), 1)

            for dst, name in ((rot[:, :], "c_rot"), (pool_w[:, :, :], "pool_w"), (count[:, :, :], "c_count"),
                              (onehot[:, :], "c_onehot"), (rel[:, :], "rel")):
                src = ins[name].rearrange("p (g c) -> p g c", g=4) if name == "c_count" else ins[name]
                act.dma_start(dst, src).then_inc(const1_loaded, 16)
            lam_src = ins["lambdas"]
            act.dma_start(lam_in[:, :, :], bass.AP(lam_src.tensor, lam_src.offset, [[0, P], [64, 4], [1, 64]])
                          ).then_inc(const1_loaded, 16)
            pos_src = ins["positions"]
            act.dma_start(pos_i[:, :], bass.AP(pos_src.tensor, pos_src.offset, [[0, P], [1, T]])
                          ).then_inc(const1_loaded, 16)
            unit_high_part(0)
            unit_high_part(1)
            act.wait_ge(trig_in, 1)
            fn(sin[:, :], sin[:, :], ACT.Sin).then_inc(trig, 1)
            act.wait_ge(trig_in, 2)
            fn(cos[:, :], cos[:, :], ACT.Sin).then_inc(trig, 1)
            for k in range(DC):
                square("norm1", k, x[:, k, :], (x_loaded, 16 * DC))
            take_root("norm1", D)
            highs("norm1")
            def keep_tile1(t):
                tile_finished("proj1", t)
                kind, h = TILES1[t]
                if kind in "qk":
                    r = aux_of_tile1(t)[1]
                    if r >= 2:
                        wait(aux_read("rope", r - 2))
                    dst = unrot[:, r % 2, :]
                elif kind == "v":
                    if h >= 2:
                        act.wait_ge(aux_ready, AUX["vtok", h - 2] + 1)
                    dst = v1t[h % 2][:, :]
                else:
                    if h >= 2:
                        act.wait_ge(pool_ready, h - 1)
                    dst = pool_in[:, h % 2, PAD:]
                fn(dst, tile_bank("proj1", t)[:, :], ACT.Copy).then_inc(tile_sem("proj1", t), 1)

            def keep_values(h):
                act.wait_ge(aux_ready, AUX["vtok", h] + 1)
                fn(v1[:, :, h, :], aux_bank("vtok", h)[:, :].rearrange("p (j d) -> p j d", j=QB),
                   ACT.Copy).then_inc(aux_sem("vtok", h), 1)

            for t in range(LEAD1):
                keep_tile1(t)
            act.wait_ge(lam_sum, 1)
            fn(small[:, 3:5], small[:, 1:3], ACT.Exp).then_inc(lam_exp, 1)
            for a in range(ATT_STEPS + 2):
                if a < ATT_STEPS:
                    h, i = a // QB, a % QB
                    end = (i + 1) * P
                    if a == 0:
                        keep_values(0)
                    if a >= 2:
                        act.wait_ge(attn_ready, a - 1)
                    for n in range(2):
                        act.wait_ge(neg_max, 2 * a + n + 1)
                        s = 2 * (a % 2) + n
                        fn(prob[:, a % 2, n, 0:end], aux_bank("score", a, n)[:, 0:end], ACT.Exp,
                           bias=small[:, 8 + s:9 + s], scale=DIFF_SCALE,
                           accum_out=small[:, 12 + s:13 + s]).then_inc(aux_sem("score", a, n), 1)
                    for t in closed(FILL1[a]):
                        keep_tile1(t)
                    for t in AUX1[a]:
                        if a and TILES1[t][0] == "v":
                            keep_values(TILES1[t][1])
                if 1 <= a <= ATT_STEPS:
                    act.wait_ge(aux_ready, AUX["turn", a - 1] + 1)
                    n = ((a - 1) % QB + 1) * P
                    fn(attn_t[:, (a - 1) % 2, 0:n], aux_bank("turn", a - 1)[:, 0:n], ACT.Copy).then_inc(
                        aux_sem("turn", a - 1), 1)
                if a < ATT_STEPS:
                    act.wait_ge(aux_ready, AUX["bias", a] + 1)
                    h = a // 2
                    if h >= 2:
                        act.wait_ge(bias_out[h % 2], 16 * (h // 2))
                    cols = slice(0, T) if a % 2 == 0 else slice(T, BIAS_COLS)
                    fn(bias_slot[:, h % 2, cols], aux_bank("bias", a)[:, 0:cols.stop - cols.start],
                       ACT.Copy).then_inc(aux_sem("bias", a), 1)
                    if a % 2:
                        wait(aux_read("bias", a))
                        wait(aux_read("bias", a - 1))
                        act.dma_start(bias_rows[h], bias_slot[:, h % 2, :]).then_inc(bias_out[h % 2], 16)
                if a >= 2 and (a - 2) % QB == QB - 1:
                    h = (a - 2) // QB
                    act.wait_ge(head_ready, h + 1)
                    fn(o1[:, h, :], tile_bank("attn", h)[:, :], ACT.Copy).then_inc(tile_sem("attn", h), 1)
                if a == ATT_STEPS:
                    highs("mix1", 0, 4)
            for h in range(HEADS):
                wait(tile_read("attn", h))
                if h == 0:
                    act.wait_ge(sum_added, DC)
                if h >= 2:
                    act.wait_ge(total_ready, STAT[f"head{h - 2}"] + 1)
                fn(sq[:, h % 2, :], o1[:, h, :], ACT.Square).then_inc(head_sq, 1)
                take_root(f"head{h}", P)
                highs("mix1", 4 + h, 1)
            for k in range(DC):
                tile_finished("wo", k)
                square("norm2", k, x[:, k, :], tile_read("wo", k))
            take_root("norm2", D)
            highs("norm2")
            def silu_pairs(i, it=0, per_loop=0):
                first = UNIT["up1"][0]
                for j in (i, i + 1):
                    units_done(first + 2 * j + 1, it, 2 * per_loop)
                    units_done(first + 2 * j + 2, it, 2 * per_loop)
                    act.wait_ge(gate_ready, j + 1 + it * per_loop)
                    fn(silu[:, :], gate[:, :], ACT.Silu).then_inc(silu_ready, 1)

            with act.Fori(0, FC // 2 - 1) as it:
                silu_pairs(0, it, 2)
            silu_pairs(FC - 2)
            for k in range(DC):
                tile_finished("down1", k)
                square("final1", k, x[:, k, :], tile_read("down1", k))
            take_root("final1", D)
            for k in range(DC):
                square("pre1", k, x[:, k, :], (x_ready, k + 1))
            take_root("pre1", D)
            highs("pre1")

            def silus(stage, turn):
                first = UNIT[stage][0]
                slots = [gate, silu]

                def one(i, it=0, per_loop=0):
                    units_done(first + 2 * i + 1, it, 2 * per_loop)
                    if i >= 2:
                        act.wait_ge(hidden_ready, FC * turn + i - 1 + it * per_loop)
                    fn(slots[i % 2][:, :], tile_bank(stage, 2 * i)[:, :], ACT.Silu).then_inc(
                        tile_sem(stage, 2 * i), 1)
                    units_done(first + 2 * i + 2, it, 2 * per_loop)

                one(0)
                one(1)
                with act.Fori(0, FC // 2 - 2) as it:
                    one(2, it, 2)
                    one(3, it, 2)
                one(FC - 2)
                one(FC - 1)

            silus("up2", 1)
            keep_branch("down2", "post1")
            take_root("post1", D)
            act.dma_start(wuk[:, :, :], ins["wuk"]).then_inc(const2_loaded, 16)
            act.dma_start(wuv[:, :, :], ins["wuv"]).then_inc(const2_loaded, 16)
            act.dma_start(tri[:, :], ins["c_tri"]).then_inc(const2_loaded, 16)

            def load_bias(h):
                src = bias_rows[h]
                act.dma_start(t_bias[:, h % 2, :], bass.AP(src.tensor, src.offset + P - 1,
                                                           [[BIAS_COLS - 1, P], [1, T]])
                              ).then_inc(bias_in[h % 2], 16)

            for n in range(2):
                act.wait_ge(bias_out[n], 16 * (DSA_HEADS // 2))
            load_bias(0)
            load_bias(1)
            for k in range(DC):
                square("mixpre", k, x[:, k, :], (x_ready, DC + k + 1))
            take_root("mixpre", D)
            highs("mixpre")
            act.wait_ge(lam_sum, 2)
            fn(small[:, 36:40], small[:, 32:36], ACT.Sigmoid).then_inc(lam_exp, 1)
            def keep_gate(n):
                s = 12 + n - TILES2.index("gate0")
                tile_finished("proj2", n)
                act.wait_ge(spill_out[s % 2], 16 * (s // 2))
                fn(spill_slot[s % 2][:, :], tile_bank("proj2", n)[:, :], ACT.Copy).then_inc(tile_sem("proj2", n), 1)
                wait(tile_read("proj2", n))
                act.dma_start(spill[s], spill_slot[s % 2][:, :]).then_inc(spill_out[s % 2], 16)

            for n, name in enumerate(TILES2[:LEAD2]):
                src, done = tile_bank("proj2", n)[:, :], tile_sem("proj2", n)
                kind, t = name.rstrip("0123456789"), int(name[len(name.rstrip("0123456789")):] or 0)
                if kind == "gate":
                    keep_gate(n)
                    continue
                tile_finished("proj2", n)
                if kind in ("ckv", "kidx"):
                    if n == 0:
                        act.wait_ge(sum_added, SQUARE["mixpre"] + DC)
                    fn(sq[:, n, :], src, ACT.Square).then_inc(head_sq, 1)
                    fn((ckv_raw, kidx_raw)[n][:, :], src, ACT.Copy).then_inc(done, 1)
                elif kind == "widx":
                    fn(widx_t[:, :], src, ACT.Copy).then_inc(done, 1)
                elif kind == "qi":
                    fn(qidx[:, t, :], src, ACT.Copy).then_inc(done, 1)
                elif kind == "qa":
                    if t >= 2:
                        act.wait_ge(aux_ready, AUX["qlat", 2 * t - 3] + 1)
                    fn(qa[:, t % 2, :], src, ACT.Copy).then_inc(done, 1)
                elif kind == "i":
                    if t >= 2:
                        act.wait_ge(aux_ready, AUX["vturn", t - 2] + 1)
                    fn(i_t[:, t % 2, :], src, ACT.Copy).then_inc(done, 1)
                else:
                    s = {"qh": 0, "gh": 4, "fh": 8}[kind] + t
                    if s >= 2:
                        act.wait_ge(spill_out[s % 2], 16 * (s // 2))
                    fn(spill_slot[s % 2][:, :], src, ACT.Silu if s < 8 else ACT.Sigmoid).then_inc(done, 1)
                    wait(tile_read("proj2", n))
                    act.dma_start(spill[s], spill_slot[s % 2][:, :]).then_inc(spill_out[s % 2], 16)
                for ev, m in AFTER2[n]:
                    if ev == "stat":
                        take_root(m, P)
                        continue
                    if ev == "wturn":
                        continue
                    small_out = aux_bank(ev, m)[:, :]
                    act.wait_ge(aux_ready, AUX[ev, m] + 1)
                    if ev == "ckvtok":
                        fn(ckv_tok[:, :, :], small_out.rearrange("p (j d) -> p j d", j=QB), ACT.Copy).then_inc(
                            aux_sem(ev, m), 1)
                    elif ev == "qlat":
                        fn(qlat[:, m, :], small_out, ACT.Copy, scale=ATT_SCALE).then_inc(aux_sem(ev, m), 1)
                    elif ev == "vturn":
                        fn(v2[:, :, m, :], small_out.rearrange("p (j d) -> p j d", j=QB), ACT.Copy).then_inc(
                            aux_sem(ev, m), 1)
                    else:
                        if m >= 2:
                            act.wait_ge(relu_used, m - 1)
                        w = (IDX_STEPS[m][0] + 1) * P
                        fn(relu[:, m % 2, 0:w], small_out[:, 0:w], ACT.Relu).then_inc(aux_sem(ev, m), 1)
            for a in range(DSA_STEPS + 4):
                if a < DSA_STEPS:
                    h, i = a // QB, a % QB
                    end = (i + 1) * P
                    act.wait_ge(logit_max, a + 1)
                    if a >= 2:
                        act.wait_ge(attn2_ready, a - 1)
                    fn(prob2[:, a % 2, 0:end], logit[:, a % 2, 0:end], ACT.Exp,
                       bias=small[:, 24 + a % 2:25 + a % 2],
                       accum_out=small[:, 26 + a % 2:27 + a % 2]).then_inc(exp2_done, 1)
                    if i == 1 and 1 <= h < DSA_HEADS - 1:
                        act.wait_ge(attn2_ready, QB * h)
                        load_bias(h + 1)
                if 2 <= a < DSA_STEPS + 2:
                    b = a - 2
                    act.wait_ge(aux_ready, AUX["turn2", b] + 1)
                    n = (b % QB + 1) * P
                    fn(attn2_t[:, b % 2, 0:n], aux_bank("turn2", b)[:, 0:n], ACT.Copy).then_inc(
                        aux_sem("turn2", b), 1)
                if a:
                    for t in closed(FILL2[a - 1]):
                        keep_gate(t)
                if 3 <= a < DSA_STEPS + 3 and (a - 3) % QB == QB - 1:
                    h = (a - 3) // QB
                    act.wait_ge(head_ready, HEADS + h + 1)
                    if h >= 2:
                        act.wait_ge(aux_ready, AUX["ya", (h - 2) // 2] + 1)
                    fn(olat[:, h % 2, :], tile_bank("olat", h)[:, :], ACT.Copy).then_inc(tile_sem("olat", h), 1)
            act.wait_ge(aux_ready, AUX["ya", 3] + 1)
            act.dma_start(masks[:, :, :], ins["c_masks"].rearrange("p (l t) -> p l t", l=8)).then_inc(
                const3_loaded, 16)
            act.dma_start(resets[:, :, :], ins["c_resets"].rearrange("p (l t) -> p l t", l=3)).then_inc(
                const3_loaded, 16)
            for n in range(2):
                act.wait_ge(spill_out[n], 16 * 6)

            def load_head(h):
                act.dma_start(hq[:, h % 2, :], spill[h]).then_inc(h_loaded[h % 2], 16)
                act.dma_start(hf[:, h % 2, :], spill[8 + h]).then_inc(h_loaded[h % 2], 16)

            load_head(0)
            load_head(1)
            for h in range(HEADS):
                act.dma_start(hg[:, h, :], spill[4 + h]).then_inc(hg_loaded, 16)

            def keep_head(h):
                act.wait_ge(head_ready, HEADS + DSA_HEADS + h + 1)
                fn(oh[:, h, :], tile_bank("hgrn", h)[:, :], ACT.Copy).then_inc(tile_sem("hgrn", h), 1)

            for h in range(HEADS):
                act.wait_ge(f_ready, h + 1)
                fn(logf[:, :], hf[:, h % 2, :], ACT.Ln).then_inc(logf_ready, 1)
                for l, b in enumerate(LEVELS):
                    e = h * len(LEVELS) + l
                    act.wait_ge(diff_ready, e + 1)
                    if e >= 2:
                        act.wait_ge(qk_ready, e - 1)
                    if b <= 32:
                        fn(decay[:, e % 2, :], diff[:, e % 2, :], ACT.Exp).then_inc(decay_ready, 1)
                    else:
                        split_ap = lambda ap: ap.rearrange("p (n c) -> p n c", c=2 * b)
                        to = split_ap(decay[:, e % 2, :])
                        fn(to[:, :, 0:b], split_ap(diff[:, e % 2, :])[:, :, 0:b], ACT.Exp).then_inc(decay_ready, 1)
                        fn(to[:, :, b:2 * b], split_ap(run[:, h % 2, l - 6, :])[:, :, b:2 * b],
                           ACT.Exp).then_inc(decay_ready, 1)
                    if e >= 2:
                        for t in closed(FILL2[DSA_STEPS + 3 + e - 2]):
                            keep_gate(t)
                    if h and l == 4:
                        keep_head(h - 1)
                    if l >= 8:
                        for m in (7, 8):
                            if h >= 2:
                                act.wait_ge(head_ready, HEADS + DSA_HEADS + h - 1)
                            act.wait_ge(aux_ready, AUX["pair", h, m] + 1)
                            src = aux_bank("pair", h, m)
                            if m == 7:
                                fn(pair_1[:, h % 2, :, :], src[:, 0:2 * P].rearrange("p (n t) -> p n t", n=2),
                                   ACT.Copy).then_inc(aux_sem("pair", h, m), 1)
                            else:
                                fn(pair_2[:, h % 2, :, :], src[:, :].rearrange("p (n t) -> p n t", n=2),
                                   ACT.Copy).then_inc(aux_sem("pair", h, m), 1)
                if h + 2 < HEADS:
                    wait(aux_read("pair", h, 6))
                    act.wait_ge(qk_ready, (h + 1) * len(LEVELS))
                    load_head(h + 2)
            for e in (HGRN_STEPS - 2, HGRN_STEPS - 1):
                for t in closed(FILL2[DSA_STEPS + 3 + e]):
                    keep_gate(t)
            for t in range(4):
                act.wait_ge(chunk_ready, SPLIT["y"] + t + 1)
                fn(a_hi[:, t, :], ya[:, t, :], ACT.Copy).then_inc(hi_ready, 1)
            keep_head(HEADS - 1)
            for h in range(HEADS):
                wait(tile_read("hgrn", h))
                if h >= 2:
                    act.wait_ge(total_ready, STAT[f"hgrn{h - 2}"] + 1)
                fn(sq[:, h % 2, :], oh[:, h, :], ACT.Square).then_inc(head_sq, 1)
                take_root(f"hgrn{h}", P)
                highs("y", 4 + h, 1)

            def load_gates(m):
                for n in range(2):
                    act.dma_start(gates_in[:, 2 * (m % 2) + n, :], spill[12 + 8 * n + m]).then_inc(
                        gates_loaded[m % 2], 16)

            act.wait_ge(aux_ready, len(AUX))
            def open_gates(m):
                act.wait_ge(gates_loaded[m % 2], 32 * (m // 2 + 1))
                for n in range(2):
                    slot = gates_in[:, 2 * (m % 2) + n, :]
                    fn(slot, slot, ACT.Sigmoid, bias=prm("b_gate", 8 * n + m)).then_inc(gates_open, 1)

            for n in range(2):
                act.wait_ge(spill_out[n], 16 * 14)
            load_gates(0)
            load_gates(1)
            open_gates(0)
            for m in range(DC):
                if m + 1 < DC:
                    open_gates(m + 1)
                tile_finished("branch", 2 * m)
                tile_finished("branch", 2 * m + 1)
                high(SPLIT["merged"] + m, h_hi[:, m, :])
                if m + 2 < DC:
                    load_gates(m + 2)
            keep_branch("out", "postmix")
            take_root("postmix", D)
            for k in range(DC):
                square("pre2", k, x[:, k, :], (x_ready, 2 * DC + k + 1))
            take_root("pre2", D)
            highs("pre2")
            silus("up3", 2)
            for c in range(2):
                act.dma_start(pe_in[:, c, :], ins["pt"][c]).then_inc(p_loaded, 16)
            highs("p", 0, 2)
            keep_branch("down3", "post2")
            for i in range(DC):
                if i % 4 == 3:
                    units_done(UNIT["pproj"][0] + i // 4 + 1)
                else:
                    act.wait_ge(head_ready, 2 * HEADS + DSA_HEADS + i - i // 4 + 1)
                fn(p_proj[:, i, :], tile_bank("pproj", i)[:, :], ACT.Copy).then_inc(tile_sem("pproj", i), 1)
            take_root("post2", D)
            for k in range(DC):
                square("plepre", k, x[:, k, :], (x_ready, 3 * DC + k + 1))
            take_root("plepre", D)
            highs("plepre")
            slots = [gate, silu]
            for i in range(DC + 1):
                if i < DC:
                    tile_finished("ple", i)
                    if i >= 2:
                        act.wait_ge(y_ready, i - 1)
                    fn(slots[i % 2][:, :], tile_bank("ple", i)[:, :], ACT.Sigmoid).then_inc(tile_sem("ple", i), 1)
                if i:
                    square("plepost", i - 1, p_proj[:, i - 1, :], (y_ready, i))
            take_root("plepost", D)

        @block.vector
        def _(dve):
            v = nc.vector
            steps = [0]

            def step(ins_, it=0, per_loop=0):
                steps[0] += 1
                ins_.then_inc(dve_step, 1)
                dve.wait_ge(dve_step, steps[0] + (it * per_loop if per_loop else 0))

            def wait(pair):
                dve.wait_ge(pair[0], pair[1])

            def rsqrt(name):
                n = STAT[name]
                dve.wait_ge(root_ready, n + 1)
                v.reciprocal(rstd[:, :], root[:, :]).then_inc(rstd_ready, 1)
                dve.wait_ge(rstd_ready, n + 1)

            def low(c, dst, hi):
                dve.wait_ge(hi_ready, c + 1)
                v.tensor_tensor(dst, chunk[:, c % 2, :], hi.bitcast(F32), ALU.subtract).then_inc(act_ready, 1)

            def made(c):
                dve.wait_ge(chunk_ready, c + 1)

            def slot_free(c):
                if c >= 2:
                    dve.wait_ge(act_ready, c - 1)

            def norm_to_split(name, stage, g):
                rsqrt(name)
                c0 = SPLIT[stage]
                for k in range(DC + 1):
                    if k < DC:
                        slot_free(c0 + k)
                        v.scalar_tensor_tensor(chunk[:, (c0 + k) % 2, :], x[:, k, :], prm(g, k), rstd[:, :],
                                               ALU.mult, ALU.mult).then_inc(chunk_ready, 1)
                    if k:
                        made(c0 + k - 1)
                        low(c0 + k - 1, a_lo[:, k - 1, :], a_hi[:, k - 1, :])

            def add_square(stage, k):
                q = SQUARE[stage] + k
                dve.wait_ge(sq_ready, q + 1)
                if k == 0:
                    v.tensor_copy(sum_sq[:, :], sq[:, q % 2, :]).then_inc(sum_added, 1)
                else:
                    dve.wait_ge(sum_added, q)
                    v.tensor_tensor(sum_sq[:, :], sum_sq[:, :], sq[:, q % 2, :], ALU.add).then_inc(sum_added, 1)

            def add_tiles(stage, square_stage):
                for k in range(DC + 1):
                    if k < DC:
                        wait(tile_done(stage, k))
                        v.tensor_tensor(x[:, k, :], x[:, k, :], tile_bank(stage, k)[:, :], ALU.add).then_inc(
                            tile_sem(stage, k), 1)
                    if k:
                        add_square(square_stage, k - 1)

            def add_branch(name, g, src, last_read, signal, before, square_stage=None):
                rsqrt(name)
                for k in range(DC + 1):
                    if k < DC:
                        if last_read is not None:
                            wait(last_read(k))
                        if k >= 2:
                            dve.wait_ge(signal, before + k - 1)
                        step(v.scalar_tensor_tensor(chunk[:, k % 2, :], src[:, k, :], prm(g, k), rstd[:, :],
                                                    ALU.mult, ALU.mult))
                        v.tensor_tensor(x[:, k, :], x[:, k, :], chunk[:, k % 2, :], ALU.add).then_inc(signal, 1)
                    if k and square_stage:
                        add_square(square_stage, k - 1)

            v.memset(pool_in[:, :, 0:PAD], 0.0)
            v.memset(pool_s[:, :, 0:PAD], 0.0)
            v.memset(neg_row[:, 0:64], NEG)
            v.memset(neg_row[:, 64:P], 0.0)
            step(v.memset(one_row[:, :], 1.0))
            dve.wait_ge(const_loaded, 48)
            for name, factor in (("attn_norm_g", 1.0 - LAM_INIT), ("ffn1_post_g", 0.5), ("ffn2_post_g", 0.5)):
                first, n = PARAMS[name]
                step(v.tensor_scalar(par[:, first:first + n], par[:, first:first + n], factor, None, ALU.mult))
            dve.wait_ge(const1_loaded, 16 * 7)
            v.tensor_copy(rel_wide[:, :, :], rel[:, :].rearrange("p (h o) -> p h o", o=1).broadcast_to([32, DSA_HEADS, P])).then_inc(rel_set, 1)
            step(v.tensor_copy(angle[:, :], pos_i[:, :]))
            step(v.tensor_scalar(angle[:, :], angle[:, :], prm("inv_freq"), None, ALU.mult))
            step(v.tensor_scalar(turns[:, :], angle[:, :], float(1 / (2 * np.pi)), ROUND, ALU.mult, ALU.add))
            step(v.tensor_scalar(turns[:, :], turns[:, :], ROUND, None, ALU.subtract))
            for part in TURN_PARTS:
                step(v.scalar_tensor_tensor(angle[:, :], turns[:, :], -part, angle[:, :], ALU.mult, ALU.add))
            v.tensor_scalar(sin[:, :], angle[:, :], PI_BELOW, -PI_BELOW, ALU.min, ALU.max).then_inc(trig_in, 1)
            step(v.scalar_tensor_tensor(cos[:, :], angle[:, :], -1.0, angle[:, :], ALU.mult, ALU.max))
            v.tensor_scalar(cos[:, :], cos[:, :], -1.0, float(np.pi / 2), ALU.mult, ALU.add).then_inc(trig_in, 1)
            step(v.tensor_tensor(lam_in[:, 0:3:2, :], lam_in[:, 0:3:2, :], lam_in[:, 1:4:2, :], ALU.mult))
            v.tensor_reduce(small[:, 1:3], lam_in[:, 0:3:2, :], AX_X, ALU.add).then_inc(lam_sum, 1)
            lb = PARAMS["hgrn_lb0"][0]
            v.tensor_tensor(small[:, 32:36], par[:, lb:lb + 4], par[:, lb + 4:lb + 8], ALU.subtract).then_inc(
                lam_sum, 1)

            for k in range(DC):
                add_square("norm1", k)
            norm_to_split("norm1", "norm1", "norm_mix_g")
            dve.wait_ge(trig, 2)

            def rotate(t):
                _, r = aux_of_tile1(t)
                raw_q = unrot[:, r % 2, :]
                dst = (q1, k1)[r % 2][:, r // 2, :]
                wait(tile_read("proj1", t))
                v.tensor_tensor(dst, raw_q, cos[:, :], ALU.mult)
                dve.wait_ge(aux_ready, AUX["rope", r] + 1)
                if r:
                    dve.wait_ge(rope_done, r)
                v.tensor_tensor(rope_a[:, :], aux_bank("rope", r)[:, :], sin[:, :], ALU.mult).then_inc(
                    aux_sem("rope", r), 1)
                wait(aux_read("rope", r))
                v.tensor_tensor(dst, dst, rope_a[:, :], ALU.add).then_inc(rope_done, 1)
                dve.wait_ge(rope_done, r + 1)

            def pool_difference(t):
                g = TILES1[t][1]
                w = WINDOWS[g]
                wait(tile_read("proj1", t))
                token = pool_in[:, g % 2, PAD:]
                src, shift, n = pool_in[:, g % 2, :], 1, 0
                while shift < w:
                    to = pool_s[:, n % 2, :]
                    step(v.tensor_tensor(to[:, PAD:], src[:, PAD:], src[:, PAD - shift:PAD + T - shift], ALU.add))
                    src, shift, n = to, 2 * shift, n + 1
                diff_ = pool_d[:, g, :]
                step(v.scalar_tensor_tensor(diff_, src[:, PAD:], 1.0 / w, token, ALU.mult, ALU.subtract))
                step(v.tensor_tensor(rope_a[:, 0:w], src[:, PAD:PAD + w], count[:, g, 0:w], ALU.mult))
                v.tensor_tensor(diff_[:, 0:w], rope_a[:, 0:w], token[:, 0:w], ALU.subtract).then_inc(pool_ready, 1)
                dve.wait_ge(pool_ready, g + 1)

            rotate(0)
            rotate(1)
            dve.wait_ge(lam_exp, 1)
            step(v.tensor_tensor(small[:, 5:6], small[:, 4:5], small[:, 3:4], ALU.subtract))
            step(v.tensor_scalar(small[:, 5:6], small[:, 5:6], -LAM_INIT, None, ALU.add))
            for a in range(ATT_STEPS + 1):
                if a < ATT_STEPS:
                    end = (a % QB + 1) * P
                    for n in range(2):
                        s = 2 * (a % 2) + n
                        dve.wait_ge(aux_ready, AUX["score", a, n] + 1)
                        step(v.tensor_reduce(small[:, 6:7], aux_bank("score", a, n)[:, 0:end], AX_X, ALU.max))
                        v.tensor_scalar(small[:, 8 + s:9 + s], small[:, 6:7], -DIFF_SCALE, None,
                                        ALU.mult).then_inc(neg_max, 1)
                        dve.wait_ge(neg_max, 2 * a + n + 1)
                if a:
                    b = a - 1
                    end, s = (b % QB + 1) * P, 2 * (b % 2)
                    wait(aux_read("score", b, 0))
                    wait(aux_read("score", b, 1))
                    if b >= 2:
                        dve.wait_ge(aux_ready, AUX["turn", b - 2] + 1)
                        dve.wait_ge(attn_ready, b)
                    step(v.reciprocal(small[:, 16 + s:18 + s], small[:, 12 + s:14 + s]))
                    step(v.tensor_tensor(small[:, 17 + s:18 + s], small[:, 17 + s:18 + s], small[:, 5:6], ALU.mult))
                    p0, p1 = prob[:, b % 2, 0, 0:end], prob[:, b % 2, 1, 0:end]
                    step(v.tensor_scalar(p1, p1, small[:, 17 + s:18 + s], None, ALU.mult))
                    v.scalar_tensor_tensor(attn[:, b % 2, 0:end], p0, small[:, 16 + s:17 + s], p1, ALU.mult,
                                           ALU.add).then_inc(attn_ready, 1)
                if 0 < a < ATT_STEPS:
                    for t in AUX1[a]:
                        if TILES1[t][0] in "qk":
                            rotate(t)
                if a:
                    for t in closed(FILL1[a - 1]):
                        if TILES1[t][0] == "p":
                            pool_difference(t)
            for g in range(4):
                c = SPLIT["mix1"] + g
                dve.wait_ge(aux_ready, AUX["pool", g] + 1)
                slot_free(c)
                step(v.tensor_scalar(chunk[:, c % 2, :], aux_bank("pool", g)[:, :], prm("pool_scale", g), None,
                                     ALU.mult))
                dve.sem_inc(aux_sem("pool", g), 1)
                dve.sem_inc(chunk_ready, 1)
                low(c, a_lo[:, g, :], a_hi[:, g, :])
            for h in range(HEADS):
                c = SPLIT["mix1"] + 4 + h
                rsqrt(f"head{h}")
                slot_free(c)
                v.scalar_tensor_tensor(chunk[:, c % 2, :], o1[:, h, :], prm("attn_norm_g", h), rstd[:, :],
                                       ALU.mult, ALU.mult).then_inc(chunk_ready, 1)
                made(c)
                low(c, a_lo[:, 4 + h, :], a_hi[:, 4 + h, :])
            add_tiles("wo", "norm2")
            norm_to_split("norm2", "norm2", "norm_ffn_g")

            def hidden_at(buf, it, j):
                return buf[:, bass.ds(it * 2 + j, 1), :].rearrange("p k t -> p (k t)")

            for n in range(2):
                dve.wait_ge(bias_out[n], 16 * (DSA_HEADS // 2))
            first = UNIT["up1"][0]
            per = 10
            at_loop = steps[0]
            with dve.Fori(0, FC // 2) as it:
                def tap(name, tile):
                    at = PARAMS[name][0] + tile
                    return par[:, bass.ds(it * 4 + at, 1)]

                for j in range(2):
                    for n, dst in ((0, gate), (1, val)):
                        i = 2 * j + n
                        b = tile_bank("up1", i)
                        dve.wait_ge(unit_done, first + i + 1 + it * 4)
                        step(v.tensor_scalar(dst[:, :], b[:, :], tap("conv_w2", i), tap("conv_b", i), ALU.mult,
                                             ALU.add), it, per)
                        step(v.scalar_tensor_tensor(dst[:, 1:T], b[:, 0:T - 1], tap("conv_w1", i), dst[:, 1:T],
                                                    ALU.mult, ALU.add), it, per)
                        v.scalar_tensor_tensor(dst[:, 2:T], b[:, 0:T - 2], tap("conv_w0", i), dst[:, 2:T],
                                               ALU.mult, ALU.add).then_inc(tile_sem("up1", i), 1)
                        dve.wait_ge(tile_sem("up1", i), TILE["up1", i][1] + 1 + it)
                        if n == 0:
                            dve.sem_inc(gate_ready, 1)
                    dve.wait_ge(silu_ready, it * 2 + (j + 1))
                    step(v.tensor_tensor(val[:, :], silu[:, :], val[:, :], ALU.mult), it, per)
                    v.tensor_scalar(hidden_at(h_hi, it, j), val[:, :], 1.0, None, ALU.mult).then_inc(high_done, 1)
                    dve.wait_ge(high_done, it * 2 + (j + 1))
                    v.tensor_tensor(hidden_at(h_lo, it, j), val[:, :], hidden_at(h_hi, it, j).bitcast(F32),
                                    ALU.subtract).then_inc(hidden_ready, 1)
                    dve.wait_ge(hidden_ready, it * 2 + (j + 1))
            assert steps[0] - at_loop == per
            steps[0] += per * (FC // 2 - 1)
            add_tiles("down1", "final1")
            rsqrt("final1")
            for k in range(DC + 1):
                if k < DC:
                    v.scalar_tensor_tensor(x[:, k, :], x[:, k, :], prm("norm_final_g", k), rstd[:, :], ALU.mult,
                                           ALU.mult).then_inc(x_ready, 1)
                if k:
                    add_square("pre1", k - 1)
            norm_to_split("pre1", "pre1", "ffn1_pre_g")

            def hiddens(stage, turn):
                first = UNIT[stage][0]
                slots = [gate, silu]
                with dve.Fori(0, FC // 2) as it:
                    for j in range(2):
                        (g, g_uses), (u, u_uses) = TILE[stage, 2 * j], TILE[stage, 2 * j + 1]
                        dve.wait_ge(bank_free[g], g_uses + 1 + it)
                        dve.wait_ge(unit_done, first + 2 * j + 2 + it * 4)
                        v.tensor_tensor(val[:, :], slots[j][:, :], bank[u][:, :], ALU.mult).then_inc(
                            bank_free[u], 1)
                        dve.wait_ge(bank_free[u], u_uses + 1 + it)
                        v.tensor_scalar(hidden_at(h_hi, it, j), val[:, :], 1.0, None, ALU.mult).then_inc(
                            high_done, 1)
                        dve.wait_ge(high_done, FC * turn + j + 1 + it * 2)
                        v.tensor_tensor(hidden_at(h_lo, it, j), val[:, :],
                                        hidden_at(h_hi, it, j).bitcast(F32), ALU.subtract).then_inc(
                            hidden_ready, 1)
                        dve.wait_ge(hidden_ready, FC * turn + j + 1 + it * 2)

            def branch_kept(stage, square_stage):
                for k in range(DC):
                    add_square(square_stage, k)

            hiddens("up2", 1)
            branch_kept("down2", "post1")
            add_branch("post1", "ffn1_post_g", y, lambda k: tile_read("down2", k), x_ready, DC, "mixpre")
            norm_to_split("mixpre", "mixpre", "mix_pre_g")
            rsqrt("ckv")
            wait(tile_read("proj2", 0))
            v.scalar_tensor_tensor(ckv[:, :], ckv_raw[:, :], prm("kv_norm_g"), rstd[:, :], ALU.mult,
                                   ALU.mult).then_inc(norm_ready, 1)
            dve.wait_ge(norm_ready, 1)
            rsqrt("kidx")
            wait(tile_read("proj2", 1))
            v.scalar_tensor_tensor(kidx[:, :], kidx_raw[:, :], prm("kidx_norm_g"), rstd[:, :], ALU.mult,
                                   ALU.mult).then_inc(norm_ready, 1)
            dve.wait_ge(aux_ready, AUX["wturn", 0] + 1)
            v.tensor_scalar(widx[:, :, :], aux_bank("wturn", 0)[:, 0:32].rearrange("p (j h) -> p j h", j=QB),
                            IDX_W_SCALE, None, ALU.mult).then_inc(aux_sem("wturn", 0), 1)
            wait(aux_read("wturn", 0))

            def top8(i):
                step(v.max(best[:, :], score[i][:, :]))
                step(v.match_replace(score[i][:, :], best[:, :], score[i][:, :], TAKEN))

            def selected(i):
                step(v.tensor_scalar(score[i][:, :], score[i][:, :], -2e38, NEG, ALU.is_gt, ALU.mult))

            dve.wait_ge(const2_loaded, 16 * 3)
            for s, (i, h) in enumerate(IDX_STEPS):
                w = (i + 1) * P
                wait(aux_read("idx", s))
                if h == 0:
                    v.tensor_scalar(score[i][:, :], relu[:, s % 2, 0:w], widx[:, i, h:h + 1], None,
                                    ALU.mult).then_inc(relu_used, 1)
                else:
                    v.scalar_tensor_tensor(score[i][:, :], relu[:, s % 2, 0:w], widx[:, i, h:h + 1],
                                           score[i][:, :], ALU.mult, ALU.add).then_inc(relu_used, 1)
                dve.wait_ge(relu_used, s + 1)
                if h == DSA_HEADS - 1:
                    step(v.tensor_tensor(score[i][:, i * P:], score[i][:, i * P:], tri[:, :], ALU.add))
                if i < QB - 1:
                    for _r in range(2):
                        top8(i + 1)
                    if h == DSA_HEADS - 1:
                        selected(i + 1)
            for _r in range(TOPK // 8):
                top8(1)
            selected(1)
            for a in range(DSA_STEPS + 4):
                if a < DSA_STEPS:
                    h, i = a // QB, a % QB
                    end, s = (i + 1) * P, a % 2
                    if i == 0:
                        dve.wait_ge(bias_in[h % 2], 16 * (h // 2 + 1))
                    dve.wait_ge(aux_ready, AUX["logit", a] + 1)
                    if a >= 2:
                        dve.wait_ge(exp2_done, a - 1)
                    first_col = (QB - 1 - i) * P
                    v.tensor_tensor(logit[:, s, 0:end], aux_bank("logit", a)[:, 0:end],
                                    t_bias[:, h % 2, first_col:first_col + end], ALU.add).then_inc(
                        aux_sem("logit", a), 1)
                    wait(aux_read("logit", a))
                    step(v.tensor_tensor(logit[:, s, 0:end], logit[:, s, 0:end], score[i][:, :], ALU.add))
                    step(v.tensor_reduce(small[:, 6:7], logit[:, s, 0:end], AX_X, ALU.max))
                    v.tensor_scalar(small[:, 24 + s:25 + s], small[:, 6:7], -1.0, None, ALU.mult).then_inc(
                        logit_max, 1)
                    dve.wait_ge(logit_max, a + 1)
                if 1 <= a <= 32:
                    b = a - 1
                    end, s = (b % QB + 1) * P, b % 2
                    dve.wait_ge(exp2_done, b + 1)
                    if b >= 2:
                        dve.wait_ge(aux_ready, AUX["turn2", b - 2] + 1)
                        dve.wait_ge(attn2_ready, b)
                    step(v.reciprocal(small[:, 28 + s:29 + s], small[:, 26 + s:27 + s]))
                    v.tensor_scalar(attn2[:, s, 0:end], prob2[:, s, 0:end], small[:, 28 + s:29 + s], None,
                                    ALU.mult).then_inc(attn2_ready, 1)
                if a >= 11 and a % 8 == 3:
                    t = (a - 11) // 8
                    dve.wait_ge(aux_ready, AUX["ya", t] + 1)
                    step(v.tensor_copy(ya[:, t, :], aux_bank("ya", t)[:, :]))
                    dve.sem_inc(aux_sem("ya", t), 1)
                    dve.sem_inc(chunk_ready, 1)
            dve.wait_ge(lam_exp, 2)
            step(v.tensor_scalar(small[:, 40:44], small[:, 36:40], -1.0, 1.0, ALU.mult, ALU.add))
            dve.wait_ge(const3_loaded, 32)
            step(v.memset(pair_d[:, :, :], 0.0))
            for h in range(HEADS):
                s = h % 2
                dve.wait_ge(h_loaded[s], 32 * (h // 2 + 1))
                v.tensor_scalar(hf[:, s, :], hf[:, s, :], small[:, 40 + h:41 + h], small[:, 36 + h:37 + h],
                                ALU.mult, ALU.add).then_inc(f_ready, 1)
                dve.wait_ge(f_ready, h + 1)
                v.tensor_scalar(hk[:, s, :], hf[:, s, :], -1.0, 1.0, ALU.mult, ALU.add).then_inc(k_ready, 1)
                dve.wait_ge(k_ready, h + 1)
                dve.wait_ge(logf_ready, h + 1)
                for n in range(3):
                    step(v.tensor_tensor_scan(run[:, s, n, :], resets[:, n, :], logf[:, :], 0.0, ALU.mult,
                                              ALU.add))

                def make_diff(l):
                    e, b = h * len(LEVELS) + l, LEVELS[l]
                    src = run[:, s, max(0, l - 6), :].rearrange("p (n c) -> p n c", c=2 * b)
                    to = diff[:, e % 2, :].rearrange("p (n c) -> p n c", c=2 * b)
                    mid = src[:, :, b - 1:b].broadcast_to([P, T // (2 * b), b])
                    ins_ = v.tensor_tensor(to[:, :, 0:b], mid, src[:, :, 0:b], ALU.subtract)
                    if b <= 32:
                        ins_ = v.tensor_tensor(to[:, :, b:2 * b], src[:, :, b:2 * b], mid, ALU.subtract)
                    ins_.then_inc(diff_ready, 1)

                def make_qk(l):
                    e, b = h * len(LEVELS) + l, LEVELS[l]
                    part = lambda ap: ap.rearrange("p (n c) -> p n c", c=2 * b)
                    dve.wait_ge(decay_ready, decays(h, l))
                    if e >= 2:
                        dve.wait_ge(aux_ready, AUX["pair", (e - 2) // 9, (e - 2) % 9] + 1)
                    to, d = part(qk[:, e % 2, :]), part(decay[:, e % 2, :])
                    v.tensor_tensor(to[:, :, 0:b], part(hk[:, s, :])[:, :, 0:b], d[:, :, 0:b], ALU.mult)
                    v.tensor_tensor(to[:, :, b:2 * b], part(hq[:, s, :])[:, :, b:2 * b], d[:, :, b:2 * b],
                                    ALU.mult).then_inc(qk_ready, 1)

                def keep_pairs(name, level):
                    dve.wait_ge(aux_ready, AUX[name] + 1)
                    view = lambda ap: ap.rearrange("p (n t) -> p n t", n=QB)
                    mask = masks[:, level:level + 1, :]
                    v.copy_predicated(view(pair_d[:, s, :]), mask.broadcast_to([P, QB, P]),
                                      view(aux_bank(*name)[:, :])).then_inc(aux_sem(*name), 1)
                    wait(aux_read(*name))

                if h >= 2:
                    dve.wait_ge(head_ready, HEADS + DSA_HEADS + h - 1)
                if h:
                    dve.wait_ge(decay_ready, decays(h, 0) - 1)
                make_diff(0)
                keep_pairs(("pair0", h), 0)
                for l in range(len(LEVELS)):
                    if l + 1 < len(LEVELS):
                        if l >= 1:
                            dve.wait_ge(decay_ready, decays(h, l - 1))
                        make_diff(l + 1)
                    make_qk(l)
                    if 1 <= l <= 7:
                        keep_pairs(("pair", h, l - 1), l)
            for t in range(4):
                dve.wait_ge(hi_ready, SPLIT["y"] + t + 1)
                v.tensor_tensor(a_lo[:, t, :], ya[:, t, :], a_hi[:, t, :].bitcast(F32), ALU.subtract).then_inc(
                    act_ready, 1)
            for h in range(HEADS):
                c = SPLIT["y"] + 4 + h
                if h == 0:
                    dve.wait_ge(hg_loaded, 16 * HEADS)
                rsqrt(f"hgrn{h}")
                wait(tile_read("hgrn", h))
                step(v.scalar_tensor_tensor(oh[:, h, :], oh[:, h, :], prm("hgrn_norm_g"), rstd[:, :], ALU.mult,
                                            ALU.mult))
                slot_free(c)
                v.tensor_tensor(chunk[:, c % 2, :], oh[:, h, :], hg[:, h, :], ALU.mult).then_inc(chunk_ready, 1)
                made(c)
                low(c, a_lo[:, 4 + h, :], a_hi[:, 4 + h, :])
            for m in range(DC):
                c = SPLIT["merged"] + m
                dve.wait_ge(gates_open, 2 * m + 2)
                for n in range(2):
                    wait(tile_done("branch", 2 * m + n))
                    v.tensor_tensor(gated[:, n, :], gates_in[:, 2 * (m % 2) + n, :],
                                    tile_bank("branch", 2 * m + n)[:, :], ALU.mult).then_inc(
                        tile_sem("branch", 2 * m + n), 1)
                    wait(tile_read("branch", 2 * m + n))
                slot_free(c)
                v.tensor_tensor(chunk[:, c % 2, :], gated[:, 0, :], gated[:, 1, :], ALU.add).then_inc(
                    chunk_ready, 1)
                made(c)
                low(c, h_lo[:, m, :], h_hi[:, m, :])
            branch_kept("out", "postmix")
            add_branch("postmix", "mix_post_g", y, lambda k: tile_read("out", k), x_ready, 2 * DC, "pre2")
            norm_to_split("pre2", "pre2", "ffn2_pre_g")
            hiddens("up3", 2)
            for c in range(2):
                dve.wait_ge(p_loaded, 32)
                n = SPLIT["p"] + c
                slot_free(n)
                v.tensor_copy(chunk[:, n % 2, :], pe_in[:, c, :]).then_inc(chunk_ready, 1)
                made(n)
                low(n, a_hi[:, 2 + c, :], a_hi[:, c, :])
            branch_kept("down3", "post2")
            add_branch("post2", "ffn2_post_g", y, lambda k: tile_read("down3", k), x_ready, 3 * DC, "plepre")
            norm_to_split("plepre", "plepre", "ple_pre_g")
            slots = [gate, silu]
            for k in range(DC + 1):
                if k < DC:
                    wait(tile_read("ple", k))
                    wait(tile_read("pproj", k))
                    v.tensor_tensor(p_proj[:, k, :], p_proj[:, k, :], slots[k % 2][:, :], ALU.mult).then_inc(
                        y_ready, 1)
                if k:
                    add_square("plepost", k - 1)
            add_branch("plepost", "ple_post_g", p_proj, None, out_ready, 0)


def _units(w, blocks, columns=None):
    k, n = w.shape
    tiles = w.reshape(k // P, P, n // P, P).transpose(2, 0, 1, 3)
    parts = tiles.reshape(n // P, k // P // blocks, blocks, P, P)
    return parts.transpose(0, 1, 3, 2, 4).reshape(-1, P, blocks * P)


def _interleave(a, b, blocks):
    a, b = _units(a, blocks), _units(b, blocks)
    return np.stack([a, b], axis=1).reshape(-1, P, blocks * P)


def _cols(v):
    return np.asarray(v).reshape(-1, P).T


def _layout(i):
    w2 = i["w_in_2"][0]
    at = {}
    pos = 0
    for name, n in (("qa", 512), ("ckv", 128), ("qi", 512), ("kidx", 64), ("widx", 8), ("qh", 512), ("fh", 512),
                    ("i", 512), ("gh", 512), ("gate", 2048)):
        at[name] = pos
        pos += n

    def w2_cols(tile):
        name = tile.rstrip("0123456789")
        first = at[name] + P * int(tile[len(name):] or 0)
        if name == "kidx":
            return np.concatenate([w2[:, first:first + 64]] * 2, axis=1)
        return w2[:, first:first + P]

    w1 = i["w_in"][0]
    first1 = {"p": 0, "q": 512, "k": 1024, "v": 1536}
    proj1 = np.concatenate([w1[:, first1[kind] + h * P:first1[kind] + (h + 1) * P] for kind, h in TILES1], axis=1)
    up1 = i["w_up"][0]
    pproj = _units(i["w_ple_proj_2"][0], 2)
    arrays = {
        "w_proj1": _units(proj1, DC),
        "w_wo": _units(i["w_o"][0], DC),
        "w_up1": _interleave(up1[:, :FF], up1[:, FF:], DC),
        "w_down1": _units(i["w_down"][0], DOWN_CHUNKS),
        "w_up2": _interleave(i["ffn1_w_gate_2"][0], i["ffn1_w_up_2"][0], DC),
        "w_down2": _units(i["ffn1_w_down_2"][0], DOWN_CHUNKS),
        "w_proj2": _units(np.concatenate([w2_cols(t) for t in TILES2], axis=1), DC),
        "w_branch": _interleave(i["w_br_a_2"][0], i["w_br_b_2"][0], 4),
        "w_out": _units(i["w_out_2"][0], DC),
        "w_up3": _interleave(i["ffn2_w_gate_2"][0], i["ffn2_w_up_2"][0], DC),
        "w_down3": _units(i["ffn2_w_down_2"][0], DOWN_CHUNKS),
        "w_pproj": pproj.reshape(2, 4, P, 2 * P).transpose(0, 2, 1, 3).reshape(2, P, 8 * P),
        "w_ple": _units(i["w_ple_gate_2"][0], DC),
    }
    conv = i["conv_w"][0]
    inter = lambda v: np.stack([_cols(v[:FF]), _cols(v[FF:])], axis=2).reshape(P, -1)
    i_freq = (np.float32(10000.0) ** (-np.arange(0, 64, 2, dtype=np.float32) / np.float32(64))).astype(np.float32)
    par = {
        "norm_mix_g": _cols(i["norm_mix_g"]), "norm_ffn_g": _cols(i["norm_ffn_g"]),
        "norm_final_g": _cols(i["norm_final_g"]), "pool_scale": _cols(i["pool_scale"]),
        "attn_norm_g": _cols(i["attn_norm_g"]), "conv_w0": inter(conv[0]), "conv_w1": inter(conv[1]),
        "conv_w2": inter(conv[2]), "conv_b": inter(i["conv_b"][0]),
        "ffn1_pre_g": _cols(i["ffn1_pre_g_2"]), "ffn1_post_g": _cols(i["ffn1_post_g_2"]),
        "mix_pre_g": _cols(i["mix_pre_g_2"]), "mix_post_g": _cols(i["mix_post_g_2"]),
        "kv_norm_g": _cols(i["kv_norm_g_2"]),
        "kidx_norm_g": _cols(np.concatenate([i["kidx_norm_g_2"][0]] * 2)),
        "hgrn_norm_g": _cols(i["hgrn_norm_g_2"]), "b_gate": _cols(i["b_gate_2"]),
        "ffn2_pre_g": _cols(i["ffn2_pre_g_2"]), "ffn2_post_g": _cols(i["ffn2_post_g_2"]),
        "ple_pre_g": _cols(i["ple_pre_g_2"]), "ple_post_g": _cols(i["ple_post_g_2"]),
        "hgrn_lb0": _cols(i["hgrn_lb_2"][0]), "hgrn_lb1": _cols(i["hgrn_lb_2"][1]),
        "inv_freq": _cols(np.tile(i_freq, 4)), "eps": np.full((P, 1), EPS, np.float32),
    }
    arrays["par"] = np.concatenate([par[name] for name in PARAMS], axis=1)
    arrays["xt"] = i["x"][0].T.reshape(DC, P, T)
    arrays["pt"] = i["p_2"][0, 0].T.reshape(2, P, T)
    arrays["positions"] = i["positions"]
    arrays["pool_w"] = i["pool_w"][0].transpose(1, 0, 2)
    arrays["lambdas"] = np.concatenate([i[n] for n in ("lambda_q1", "lambda_k1", "lambda_q2", "lambda_k2")])
    arrays["rel"] = i["rel_bias_2"]
    arrays["wuk"] = i["w_uk_2"][0].transpose(2, 0, 1).reshape(64, 4, 2, P).transpose(2, 0, 1, 3).reshape(P, 4, P)
    arrays["wuv"] = i["w_uv_2"][0].transpose(1, 0, 2)
    arrays.update(constants())
    return {name: np.ascontiguousarray(a) for name, a in arrays.items()}


def kernel(**inputs):
    import concourse.bacc as bacc
    from concourse.bass_utils import run_bass_kernel_spmd

    nc = bacc.Bacc("TRN2", target_bir_lowering=False, num_devices=1)
    arrays = _layout({name: np.asarray(a) for name, a in inputs.items()})
    ins = {name: nc.dram_tensor(f"in_{name}", a.shape, mybir.dt.from_np(a.dtype), kind="ExternalInput").ap()
           for name, a in arrays.items()}
    spill = nc.dram_tensor("spill", (28, P, T), F32, kind="Internal").ap()
    bias_rows = nc.dram_tensor("bias_rows", (DSA_HEADS, P, BIAS_COLS), F32, kind="Internal").ap()
    out = nc.dram_tensor("out_t", (DC, P, T), F32, kind="ExternalOutput").ap()
    two_blocks(nc, ins, spill, bias_rows, out)
    result = run_bass_kernel_spmd(nc, [{f"in_{name}": a for name, a in arrays.items()}], core_ids=[0])
    return np.ascontiguousarray(result.results[0]["out_t"].reshape(D, T).T)[None]
```

```python
from contextlib import ExitStack

import numpy as np

import concourse.bass as bass
from concourse import mybir

F32 = mybir.dt.float32
F32R = mybir.dt.float32r
I32 = mybir.dt.int32
ALU = mybir.AluOpType
ACT = mybir.ActivationFunctionType
AX_X = mybir.AxisListType.X

P = 128
T = 512
D = 1024
DC = D // P
FF = 2816
FC = FF // P
QB = T // P
EPS = 1e-6
HEADS = 4
DSA_HEADS = 8
DIFF_SCALE = 64 ** -0.5
ATT_SCALE = 64 ** -0.5
IDX_W_SCALE = (8 ** -0.5) * (64 ** -0.5)
TOPK = 128
LAM_INIT = 0.2
WINDOWS = (2, 4, 8, 16)
PAD = max(WINDOWS)
NEG = -1e30
TAKEN = -3e38
LEVELS = (1, 2, 4, 8, 16, 32, 64, 128, 256)
DOWN_CHUNKS = FC // 2
SLOT = DOWN_CHUNKS * P
SLOTS = 4
BANKS = 4
AUX_BANKS = 3
BIAS_COLS = 640

PARAMS = {}
_at = 0
for _name, _n in (("norm_mix_g", 8), ("norm_ffn_g", 8), ("norm_final_g", 8), ("pool_scale", 4),
                  ("attn_norm_g", 4), ("conv_w0", 44), ("conv_w1", 44), ("conv_w2", 44), ("conv_b", 44),
                  ("ffn1_pre_g", 8), ("ffn1_post_g", 8), ("mix_pre_g", 8), ("mix_post_g", 8),
                  ("kv_norm_g", 1), ("kidx_norm_g", 1), ("hgrn_norm_g", 1), ("b_gate", 16),
                  ("ffn2_pre_g", 8), ("ffn2_post_g", 8), ("ple_pre_g", 8), ("ple_post_g", 8),
                  ("hgrn_lb0", 4), ("hgrn_lb1", 4), ("inv_freq", 1), ("eps", 1)):
    PARAMS[_name] = (_at, _n)
    _at += _n
N_PARAMS = _at

TILES2 = (["ckv", "kidx", "widx"] + [f"qi{t}" for t in range(4)] + [f"qa{t}" for t in range(4)]
          + [f"i{t}" for t in range(4)] + [f"qh{t}" for t in range(4)] + [f"gh{t}" for t in range(4)]
          + [f"fh{t}" for t in range(4)] + [f"gate{t}" for t in range(16)])
TILES1 = [(kind, h) for h in range(HEADS) for kind in "qkv"] + [("p", g) for g in range(len(WINDOWS))]
LEAD1 = 3
LEAD2 = TILES2.index("gate0") + 4
STAGES = (("proj1", 16, DC), ("wo", DC, DC), ("up1", 2 * FC, DC), ("down1", 2 * DC, DOWN_CHUNKS),
          ("up2", 2 * FC, DC), ("down2", 2 * DC, DOWN_CHUNKS), ("proj2", len(TILES2), DC),
          ("branch", 2 * DC, 4), ("out", DC, DC),
          ("up3", 2 * FC, DC), ("down3", 2 * DC, DOWN_CHUNKS), ("pproj", 2, DC), ("ple", DC, DC))
UNIT = {}
_at = 0
for _name, _n, _c in STAGES:
    UNIT[_name] = (_at, _n, _c)
    _at += _n

START_UNITS = [0, 2, 4]
EARLY = {UNIT[name][0] + 3 for name in ("proj1", "wo", "up1", "up2", "proj2", "branch", "out", "up3", "ple")}
POOL_SUMS = {"up2": "pre1", "proj2": "mixpre", "up3": "pre2", "ple": "plepre"}

BLOCKS_OF = [c for _, n, c in STAGES for _i in range(n)]



def spread(first_tile, end_tile, rates):
    steps, at, end = [], first_tile * DC, end_tile * DC
    for rate in rates:
        pieces, left = [], min(rate, end - at)
        while left:
            n = min(left, DC - at % DC)
            pieces.append((at // DC, at % DC, at % DC + n))
            at, left = at + n, left - n
        steps.append(pieces)
    assert at == end, (at, end)
    return steps


def closed(pieces):
    return [t for t, _, end in pieces if end == DC]


ATT_STEPS = 16
FILL1 = spread(LEAD1, len(TILES1), [7] * ATT_STEPS)
DSA_STEPS = DSA_HEADS * QB
HGRN_STEPS = HEADS * len(LEVELS)
GAP2 = DSA_STEPS + 3
_rates = [1 + (a % 5 == 4) for a in range(GAP2)] + [14]
_left = (len(TILES2) - LEAD2) * DC - sum(_rates)
FILL2 = spread(LEAD2, len(TILES2), _rates + [
    _left * (e + 1) // HGRN_STEPS - _left * e // HGRN_STEPS for e in range(HGRN_STEPS)])

TILE = {}
_uses = [0] * BANKS


def _tile(name, i, bank_):
    TILE[name, i] = (bank_, _uses[bank_])
    _uses[bank_] += 1


def _tiles(name, first, end, over=BANKS, start=0):
    for i in range(first, end):
        _tile(name, i, start + i % over)


_tiles("proj1", 0, 16, 3)
_tiles("attn", 0, HEADS, 1, 3)
_tiles("wo", 0, DC)
_tiles("up1", 0, 2 * FC)
_tiles("down1", 0, DC)
_tiles("up2", 0, 2 * FC)
_tiles("down2", 0, DC)
_tiles("proj2", 0, TILES2.index("gate0"))
_tiles("proj2", TILES2.index("gate0"), len(TILES2), 2)
_tiles("olat", 0, DSA_HEADS, 2, 2)
_tiles("hgrn", 0, HEADS, 2, 2)
_tiles("branch", 0, 2 * DC)
_tiles("out", 0, DC)
_tiles("up3", 0, 2 * FC)
_tiles("down3", 0, DC)
_tiles("pproj", 0, DC)
_tiles("ple", 0, DC)

AUX = {}


def _aux(*name):
    AUX[name] = len(AUX)


def aux_of_tile1(t):
    kind, h = TILES1[t]
    return {"q": ("rope", 2 * h), "k": ("rope", 2 * h + 1), "v": ("vtok", h), "p": None}[kind]


SPILLED = {"qh": 0, "gh": 4, "fh": 8, "gate": 12}
AUX1 = [[LEAD1 - 1] if a == 0 else [t for t in closed(FILL1[a - 1]) if aux_of_tile1(t)] for a in range(ATT_STEPS)]
for _t in range(LEAD1 - 1):
    _aux(*aux_of_tile1(_t))
for _a in range(ATT_STEPS + 1):
    if _a == 0:
        _aux(*aux_of_tile1(LEAD1 - 1))
    if _a < ATT_STEPS:
        _aux("score", _a, 0)
        _aux("score", _a, 1)
    if 0 < _a < ATT_STEPS:
        for _t in AUX1[_a]:
            _aux(*aux_of_tile1(_t))
    if _a:
        _aux("turn", _a - 1)
    if _a < ATT_STEPS:
        _aux("bias", _a)
for _g in range(len(WINDOWS)):
    _aux("pool", _g)
IDX_STEPS = [(i, h) for i in (3, 2, 1) for h in range(DSA_HEADS)]
AFTER2 = {n: [] for n in range(len(TILES2))}
AFTER2[3].append(("stat", "ckv"))
AFTER2[4].append(("spread", "ckv"))
AFTER2[5] += [("stat", "kidx"), ("wturn", 0)]
AFTER2[6] += [("spread", "kidx"), ("ckvtok", 0)]
for _t in range(4):
    AFTER2[8 + _t] += [("qlat", 2 * _t), ("qlat", 2 * _t + 1)]
    AFTER2[12 + _t].append(("vturn", _t))
_room = TILES2.index("gate0") - 1 - 7
for _s in range(len(IDX_STEPS)):
    AFTER2[7 + _s * _room // (len(IDX_STEPS) - 1)].append(("idx", _s))
for _n in AFTER2:
    for _ev in AFTER2[_n]:
        if _ev[0] not in ("stat", "spread"):
            _aux(*_ev)
for _a in range(DSA_STEPS + 4):
    if _a < DSA_STEPS:
        _aux("logit", _a)
    if 2 <= _a < DSA_STEPS + 2:
        _aux("turn2", _a - 2)
    if _a >= 11 and _a % 8 == 3:
        _aux("ya", (_a - 11) // 8)
for _h in range(HEADS):
    _aux("pair0", _h)
    for _l in range(len(LEVELS)):
        _aux("pair", _h, _l)

STAT = {n: i for i, n in enumerate(
    ["norm1"] + [f"head{h}" for h in range(4)] + ["norm2", "final1", "pre1", "post1", "mixpre", "ckv", "kidx"]
    + [f"hgrn{h}" for h in range(4)] + ["postmix", "pre2", "post2", "plepre", "plepost"])}
SUM = {n: i for i, n in enumerate(n for n in (m.replace("head0", "head").replace("hgrn0", "hgrn") for m in STAT)
                                  if n.rstrip("123") == n or n.rstrip("123") not in ("head", "hgrn"))}
SQUARE = {n: 8 * i for i, n in enumerate(
    ["norm1", "norm2", "final1", "pre1", "post1", "mixpre", "postmix", "pre2", "post2", "plepre", "plepost"])}
SPLIT = {}
_at = 0
for _name, _n in (("norm1", 8), ("mix1", 8), ("norm2", 8), ("pre1", 8), ("mixpre", 8), ("y", 8), ("merged", 8),
                  ("pre2", 8), ("p", 2), ("plepre", 8)):
    SPLIT[_name] = _at
    _at += _n


def bucket(dist):
    d_f = np.maximum(dist, 1).astype(np.float32)
    log_b = 16 + (np.log(d_f / np.float32(16)) / np.float32(np.log(8.0)) * np.float32(16)).astype(np.int32)
    return np.where(dist < 16, dist, np.minimum(log_b, 31))


def constants():
    i = np.arange(P)
    ident = np.eye(P, dtype=np.float32)
    rot = np.zeros((P, P), np.float32)
    for g in (0, 64):
        for j in range(32):
            rot[g + j + 32, g + j] = -1.0
            rot[g + j, g + j + 32] = 1.0
    onehot = np.zeros((P, BIAS_COLS), np.float32)
    onehot[bucket(np.maximum(T - 1 - np.arange(BIAS_COLS), 0)), np.arange(BIAS_COLS)] = 1.0
    count = np.ones((P, len(WINDOWS), PAD), np.float32)
    for g, w in enumerate(WINDOWS):
        count[:, g, :] = (1.0 / np.minimum(np.arange(PAD) + 1, w)).astype(np.float32)
    tri = np.where(i[None, :] > i[:, None], np.float32(-1e38), np.float32(0)).astype(np.float32)
    masks = np.zeros((P, 8, P), np.int32)
    masks[:, 0, :] = np.eye(P, dtype=np.int32)
    for l in range(7):
        b = LEVELS[l]
        s, t = i[:, None], i[None, :]
        masks[:, l + 1, :] = (s // (2 * b) == t // (2 * b)) & (s % (2 * b) < b) & (t % (2 * b) >= b)
    resets = np.ones((P, 3, T), np.float32)
    for n, seg in enumerate((64, 128, 256)):
        resets[:, n, ::seg] = 0.0
    return {"c_ident": ident, "c_ones": np.ones((P, P), np.float32), "c_rot": rot, "c_onehot": onehot[:32],
            "c_count": count.reshape(P, -1), "c_tri": tri, "c_masks": masks.reshape(P, -1),
            "c_resets": resets.reshape(P, -1)}

ROUND = 12582912.0
PI_BELOW = 3.1415925
TURN_PARTS = (6.28125, 8117 / 2 ** 22, float(2 * np.pi - 6.28125 - 8117 / 2 ** 22))


def decays(h, l):
    return 12 * h + (l + 1 if l < 6 else 6 + 2 * (l - 5))


LAST_UNIT = sum(n for _, n, _ in STAGES)


def two_blocks(nc, ins, spill, bias_rows, out):
    with ExitStack() as ctx:
        base = (nc.sbuf_base + 31) // 32 * 32
        arena_bytes = (nc.sbuf_usable_end - base) // 32 * 32 - 64
        ctx.enter_context(nc.sbuf_tensor("arena", [P, arena_bytes // 4], F32))
        limit = base + arena_bytes

        def placer(start, end):
            at = [start]

            def put(name, shape, dtype=F32):
                size = (int(np.prod(shape[1:])) * 4 + 31) // 32 * 32
                tensor = nc.alloc_sbuf_tensor_at(name, shape, dtype, offset=at[0])
                at[0] += size
                assert at[0] <= end, (name, at[0] - end)
                return tensor

            put.at = at
            return put

        keep = placer(base, limit)
        raw_at = keep.at[0]
        raw = keep("raw", [P, SLOTS, SLOT])
        w_lo = placer(raw_at, keep.at[0])("w_lo", [P, SLOTS, SLOT], F32R)
        w_hi = keep("w_hi", [P, SLOTS, SLOT], F32R)
        x = keep("x", [P, DC, T])
        a_hi = keep("a_hi", [P, DC, T], F32R)
        y_at = keep.at[0]
        a_lo = keep("a_lo", [P, DC, T], F32R)
        room_at = keep.at[0]
        h_hi = keep("h_hi", [P, FC, T], F32R)
        h_lo = keep("h_lo", [P, FC, T], F32R)
        room_end = keep.at[0]
        par = keep("par", [P, N_PARAMS])
        ident = keep("ident", [P, P])
        ones = keep("ones", [P, P])
        sum_sq = keep("sum_sq", [P, T])
        sq = keep("sq", [P, 2, T])
        chunk = keep("chunk", [P, 2, T])
        root = keep("root", [P, 4 * QB])
        inverse = keep("inverse", [P, 4 * QB])
        diagonal = keep("diagonal", [P, T])
        rstd = keep("rstd", [P, T])
        rstd_mix = keep("rstd_mix", [P, T])
        gate = keep("gate", [P, T])
        val = keep("val", [P, T])
        silu = keep("silu", [P, T])
        small = keep("small", [P, 64])
        lam_in = keep("lam_in", [P, 4, 64])
        y = placer(y_at, room_at)("y", [P, DC, T])
        spill_slot = [gate, val]
        logf = silu
        bias_mask = [sum_sq, diagonal]

        r1 = placer(room_at, room_end)
        rot = r1("rot", [P, P])
        pool_w = r1("pool_w", [P, 4, P])
        count = r1("count", [P, 4, PAD])
        cos = r1("cos", [P, T])
        sin = r1("sin", [P, T])
        q1 = r1("q1", [P, HEADS, T])
        k1 = r1("k1", [P, HEADS, T])
        v1 = r1("v1", [P, QB, HEADS, P])
        o1 = r1("o1", [P, HEADS, T])
        neg_row = r1("neg_row", [1, P])
        one_row = r1("one_row", [1, 64])
        onehot = r1("onehot", [32, BIAS_COLS])
        rel = r1("rel", [32, DSA_HEADS])
        rel_wide = r1("rel_wide", [32, DSA_HEADS, P])
        bias_slot = r1("bias_slot", [P, 2, BIAS_COLS])
        before_softmax = r1.at[0]
        r1_angle = placer(before_softmax, room_end)
        pos_i = r1_angle("pos_i", [P, T], I32)
        angle = r1_angle("angle", [P, T])
        turns = r1_angle("turns", [P, T])
        prob = r1("prob", [P, 2, 2, T])
        unrot = r1("unrot", [P, 2, T])
        pool_in = r1("pool_in", [P, 2, PAD + T])
        pool_s = r1("pool_s", [P, 2, PAD + T])
        pool_d = r1("pool_d", [P, 4, T])
        rope_a = silu
        v1t = [gate, val]
        attn = r1("attn", [P, 2, T])
        attn_t = r1("attn_t", [P, 2, T])

        ya_at = room_end - 4 * T * 4
        ya = placer(ya_at, room_end)("ya", [P, 4, T])
        r2 = placer(room_at, ya_at)
        v2 = r2("v2", [P, QB, HEADS, P])
        r2_split = r2.at[0]
        ckv_raw = r2("ckv_raw", [P, T])
        ckv = r2("ckv", [P, T])
        ckv_tok = r2("ckv_tok", [P, QB, P])
        kidx_raw = r2("kidx_raw", [P, T])
        kidx = r2("kidx", [P, T])
        widx_t = r2("widx_t", [P, T])
        widx = r2("widx", [P, QB, DSA_HEADS])
        wuk = r2("wuk", [P, 4, P])
        wuv = r2("wuv", [P, DSA_HEADS, 64])
        tri = r2("tri", [P, P])
        qlat = r2("qlat", [P, DSA_HEADS, T])
        score = [tri] + [r2(f"score{i}", [P, (i + 1) * P]) for i in range(1, QB)]
        best = r2("best", [P, 8])
        t_bias = r2("t_bias", [P, 2, T])
        r2_under = placer(r2.at[0], ya_at)
        qa = r2_under("qa", [P, 2, T])
        relu = r2_under("relu", [P, 2, T])
        i_t = r2_under("i_t", [P, 2, T])
        logit = r2("logit", [P, 2, T])
        prob2 = r2("prob2", [P, 2, T])
        attn2 = r2("attn2", [P, 2, T])
        attn2_t = r2("attn2_t", [P, 2, T])
        olat = r2("olat", [P, 2, T])
        qidx = r2("qidx", [P, 4, T])
        r3 = placer(r2_split, ya_at)
        masks = r3("masks", [P, 8, P], I32)
        resets = r3("resets", [P, 3, T])
        hq = r3("hq", [P, 2, T])
        hf = r3("hf", [P, 2, T])
        hk = r3("hk", [P, 2, T])
        run = r3("run", [P, 2, 3, T])
        diff = r3("diff", [P, 2, T])
        decay = r3("decay", [P, 2, T])
        qk = r3("qk", [P, 2, T])
        pair_d = r3("pair_d", [P, 2, T])
        pair_1 = r3("pair_1", [P, 2, 2, P])
        pair_2 = r3("pair_2", [P, 2, 2, 2 * P])
        oh = r3("oh", [P, HEADS, T])
        hg = r3("hg", [P, HEADS, T])
        r4 = placer(room_at + 8 * T * 4, room_at + FC * T * 4)
        gates_in = r4("gates_in", [P, 4, T])
        gated = r4("gated", [P, 2, T])
        pe_in = placer(y_at - 4 * T * 4, y_at)("pe_in", [P, 2, T])
        p_proj = placer(room_at, room_end)("p_proj", [P, DC, T])

        bank = [ctx.enter_context(nc.psum_tensor(f"bank{i}", [P, T], F32)) for i in range(8)]
        stat_bank = bank[7]

        def tile_bank(stage, i):
            return bank[TILE[stage, i][0]]

        def aux_bank(*name):
            return bank[BANKS + AUX[name] % AUX_BANKS]

        def tile_sem(stage, i):
            return bank_free[TILE[stage, i][0]]

        def tile_read(stage, i):
            return tile_sem(stage, i), TILE[stage, i][1] + 1

        def tile_done(stage, i):
            per_tile = 2 if stage.startswith("down") else 1
            return unit_done, UNIT[stage][0] + per_tile * (i + 1)

        def aux_sem(*name):
            return aux_free[AUX[name] % AUX_BANKS]

        def aux_read(*name):
            return aux_sem(*name), AUX[name] // AUX_BANKS + 1

        def prm(name, i=0, rows=P):
            return par[0:rows, PARAMS[name][0] + i:PARAMS[name][0] + i + 1]

        def sem(name):
            return ctx.enter_context(nc.semaphore(name))

        raw_loaded = [sem(f"raw_loaded{i}") for i in range(SLOTS)]
        unit_high = sem("unit_high")
        unit_split = sem("unit_split")
        unit_done = sem("unit_done")
        bank_free = [sem(f"bank_free{i}") for i in range(BANKS)]
        aux_ready = sem("aux_ready")
        aux_free = [sem(f"aux_free{i}") for i in range(AUX_BANKS)]
        head_ready = sem("head_ready")
        total_ready = sem("total_ready")
        root_ready = sem("root_ready")
        head_summed = sem("head_summed")
        diagonal_ready = sem("diagonal_ready")
        spread_ready = sem("spread_ready")
        rstd_ready = sem("rstd_ready")
        sq_ready = sem("sq_ready")
        sum_added = sem("sum_added")
        head_sq = sem("head_sq")
        chunk_ready = sem("chunk_ready")
        hi_ready = sem("hi_ready")
        act_ready = sem("act_ready")
        x_ready = sem("x_ready")
        y_ready = sem("y_ready")
        x_loaded = [sem(f"x_loaded{k}") for k in range(DC)]
        par_loaded = sem("par_loaded")
        const_loaded = sem("const_loaded")
        const1_loaded = sem("const1_loaded")
        const2_loaded = sem("const2_loaded")
        const3_loaded = sem("const3_loaded")
        p_loaded = sem("p_loaded")
        dve_step = sem("dve_step")
        trig_in = sem("trig_in")
        trig = sem("trig")
        lam_sum = sem("lam_sum")
        lam_exp = sem("lam_exp")
        rel_set = sem("rel_set")
        rope_done = sem("rope_done")
        pool_ready = sem("pool_ready")
        neg_max = sem("neg_max")
        attn_ready = sem("attn_ready")
        bias_out = [sem(f"bias_out{i}") for i in range(2)]
        high_done = sem("high_done")
        silu_ready = sem("silu_ready")
        gate_ready = sem("gate_ready")
        hidden_ready = sem("hidden_ready")
        norm_ready = sem("norm_ready")
        relu_used = sem("relu_used")
        spill_out = [sem(f"spill_out{i}") for i in range(2)]
        bias_in = [sem(f"bias_in{i}") for i in range(2)]
        logit_max = sem("logit_max")
        exp2_done = sem("exp2_done")
        attn2_ready = sem("attn2_ready")
        h_loaded = [sem(f"h_loaded{i}") for i in range(2)]
        hg_loaded = sem("hg_loaded")
        f_ready = sem("f_ready")
        logf_ready = sem("logf_ready")
        k_ready = sem("k_ready")
        diff_ready = sem("diff_ready")
        decay_ready = sem("decay_ready")
        qk_ready = sem("qk_ready")
        gates_loaded = [sem(f"gates_loaded{i}") for i in range(2)]
        cos_scaled = sem("cos_scaled")
        ple_open = sem("ple_open")
        selected_ready = sem("selected_ready")
        bias_mask_ready = sem("bias_mask_ready")
        sums_ready = sem("sums_ready")
        spill_made = sem("spill_made")
        gates_scaled = sem("gates_scaled")
        gates_open = sem("gates_open")
        out_ready = sem("out_ready")
        stored = sem("stored")

        block = ctx.enter_context(nc.Block())

        @block.sync
        def _(sp):
            def load_unit(src, u, slot, size):
                sp.dma_start(raw[:, slot, 0:size], src).then_inc(raw_loaded[slot], 16)

            def load_stage(name):
                first, n, blocks = UNIT[name]
                src = ins["w_" + name]
                size = blocks * P
                straight = max(0, SLOTS - first)
                for i in range(len(START_UNITS) if first == 0 else 0, straight):
                    load_unit(src[i], first + i, (first + i) % SLOTS, size)
                loops = (n - straight) // SLOTS
                if loops:
                    with sp.Fori(0, loops) as it:
                        for j in range(SLOTS):
                            u = first + straight + j
                            sp.wait_ge(unit_done, u - SLOTS + 1 + it * SLOTS)
                            unit = src[bass.ds(it * SLOTS + (straight + j), 1), :, :]
                            load_unit(unit.rearrange("u p m -> (u p) m"), u, u % SLOTS, size)
                for i in range(straight + loops * SLOTS, n):
                    u = first + i
                    sp.wait_ge(unit_done, u - SLOTS + 1)
                    load_unit(src[i], u, u % SLOTS, size)

            sp.dma_start(par[:, :], ins["par"]).then_inc(par_loaded, 16)
            for k in range(DC):
                if k in START_UNITS:
                    u = START_UNITS.index(k)
                    load_unit(ins["w_proj1"][u], u, u, DC * P)
                sp.dma_start(x[:, k, :], ins["xt"][k]).then_inc(x_loaded[k], 16)
            sp.dma_start(ident[:, :], ins["c_ident"]).then_inc(const_loaded, 16)
            sp.dma_start(ones[:, :], ins["c_ones"]).then_inc(const_loaded, 16)
            for name, n, _ in STAGES:
                load_stage(name)
            for k in range(DC):
                sp.wait_ge(out_ready, k + 1)
                sp.dma_start(out[k], x[:, k, :]).then_inc(stored, 16)
            sp.wait_ge(stored, 16 * DC)

        @block.gpsimd
        def _(pool):
            def split_unit(u, size, it=0, per_loop=0):
                slot, half = u % SLOTS, u % SLOTS
                hi, lo, src = w_hi[:, half, 0:size], w_lo[:, half, 0:size], raw[:, slot, 0:size]
                pool.wait_ge(unit_high, u + 1 + it * per_loop)
                pool.tensor_tensor(lo, src, hi.bitcast(F32), ALU.subtract).then_inc(unit_split, 1)

            def add_squares(stage):
                for k in range(1, DC):
                    q = SQUARE[stage] + k
                    pool.wait_ge(sq_ready, q + 1)
                    if k == 1:
                        pool.tensor_tensor(sum_sq[:, :], sq[:, 0, :], sq[:, 1, :], ALU.add).then_inc(sum_added, 2)
                    else:
                        pool.wait_ge(sum_added, q)
                        pool.tensor_tensor(sum_sq[:, :], sum_sq[:, :], sq[:, q % 2, :], ALU.add).then_inc(
                            sum_added, 1)

            def split_units(name, start, end):
                first, size = UNIT[name][0], UNIT[name][2] * P
                loops = max(0, end - start) // SLOTS
                if loops > 1:
                    with pool.Fori(0, loops) as it:
                        for j in range(SLOTS):
                            split_unit(first + start + j, size, it, SLOTS)
                    start += SLOTS * loops
                for i in range(start, end):
                    split_unit(first + i, size)

            def split_for(t):
                u = UNIT["proj2"][0] + t + 3
                split_unit(u, BLOCKS_OF[u] * P)

            def make_diff(e):
                h, l = e // len(LEVELS), e % len(LEVELS)
                b = LEVELS[l]
                if l == 0:
                    pool.wait_ge(sums_ready, h + 1)
                if e >= 2:
                    pool.wait_ge(decay_ready, decays((e - 2) // len(LEVELS), (e - 2) % len(LEVELS)))
                src = run[:, h % 2, max(0, l - 6), :].rearrange("p (n c) -> p n c", c=2 * b)
                to = diff[:, e % 2, :].rearrange("p (n c) -> p n c", c=2 * b)
                mid = src[:, :, b - 1:b].broadcast_to([P, T // (2 * b), b])
                ins_ = pool.tensor_tensor(to[:, :, 0:b], mid, src[:, :, 0:b], ALU.subtract)
                if b <= 32:
                    ins_ = pool.tensor_tensor(to[:, :, b:2 * b], src[:, :, b:2 * b], mid, ALU.subtract)
                ins_.then_inc(diff_ready, 1)

            for name, n, _ in STAGES[:6]:
                split_units(name, 0, min(n, SLOTS))
                if name in POOL_SUMS:
                    add_squares(POOL_SUMS[name])
                split_units(name, SLOTS, n)
            split_units("proj2", 0, SLOTS)
            add_squares("mixpre")
            split_units("proj2", SLOTS, LEAD2 + 3)
            pool.wait_ge(const2_loaded, 16 * 3)
            pool.wait_ge(rstd_ready, STAT["kidx"] + 1)
            for a in range(DSA_STEPS + 4):
                if a < DSA_STEPS:
                    h, i = a // QB, a % QB
                    end, first_col = (i + 1) * P, (QB - 1 - i) * P
                    if i == 0:
                        pool.wait_ge(bias_in[h % 2], 16 * (h // 2 + 1))
                    if a == 1:
                        pool.wait_ge(selected_ready, 3)
                    if a >= 2:
                        former = aux_read("logit", a - 2)
                        pool.wait_ge(former[0], former[1])
                    pool.tensor_tensor(bias_mask[a % 2][:, 0:end], t_bias[:, h % 2, first_col:first_col + end],
                                       score[i][:, :], ALU.add).then_inc(bias_mask_ready, 1)
                if a >= 3:
                    for t in closed(FILL2[a - 3]):
                        split_for(t)
            make_diff(0)
            for e in range(HGRN_STEPS):
                if e + 1 < HGRN_STEPS:
                    make_diff(e + 1)
            pool.wait_ge(unit_split, UNIT["branch"][0] + 3)
            split_units("branch", 3, 2 * DC)
            for name, n, _ in STAGES[8:]:
                split_units(name, 0, min(n, SLOTS))
                if name in POOL_SUMS:
                    add_squares(POOL_SUMS[name])
                split_units(name, SLOTS, n)

        @block.tensor
        def _(pe):
            mm = nc.tensor.matmul

            def wait(pair):
                pe.wait_ge(pair[0], pair[1])

            def wait_bank(stage, i, turn=0):
                number, former = TILE[stage, i]
                if former:
                    pe.wait_ge(bank_free[number], former + turn)

            def unit_blocks(u, n, dst, chunk_at, hi, lo, first, last, it=0, per_loop=0, ready=None,
                            units=1):
                half = u % SLOTS
                pe.wait_ge(unit_split, u + 1 + it * per_loop)
                for c in range(n):
                    if ready is not None:
                        pe.wait_ge(ready[0], ready[1] + c + 1)
                    k = chunk_at + c
                    wh, wl = w_hi[:, half, c * P:(c + 1) * P], w_lo[:, half, c * P:(c + 1) * P]
                    mm(dst[:, :], wh, hi[:, k, :], start=(first and c == 0), stop=False)
                    mm(dst[:, :], wh, lo[:, k, :], start=False, stop=False)
                    step = mm(dst[:, :], wl, hi[:, k, :], start=False, stop=(last and c == n - 1))
                if units:
                    step.then_inc(unit_done, units)

            def project(stage, i, ready=None, hi=a_hi, lo=a_lo):
                first, _, blocks = UNIT[stage]
                wait_bank(stage, i)
                unit_blocks(first + i, blocks, tile_bank(stage, i), 0, hi, lo, True, True, ready=ready)

            def fill(stage, pieces):
                for t, c0, c1 in pieces:
                    u, dst = UNIT[stage][0] + t, tile_bank(stage, t)
                    if c0 == 0:
                        wait_bank(stage, t)
                        pe.wait_ge(unit_split, u + 1)
                    for c in range(c0, c1):
                        cols = slice(c * P, (c + 1) * P)
                        wh, wl = w_hi[:, u % SLOTS, cols], w_lo[:, u % SLOTS, cols]
                        mm(dst[:, :], wh, a_hi[:, c, :], start=(c == 0), stop=False)
                        mm(dst[:, :], wh, a_lo[:, c, :], start=False, stop=False)
                        step = mm(dst[:, :], wl, a_hi[:, c, :], start=False, stop=(c == DC - 1))
                    if c1 == DC:
                        step.then_inc(unit_done, 1)

            def aux_wait(*name):
                n = AUX[name]
                if n >= AUX_BANKS:
                    pe.wait_ge(aux_free[n % AUX_BANKS], n // AUX_BANKS)
                return bank[BANKS + n % AUX_BANKS]

            def sum_columns(source, column=0):
                for j in range(QB):
                    step = mm(stat_bank[:, column + j:column + j + 1], source[:, j * P:(j + 1) * P], ones[:, 0:1],
                              start=True, stop=True)
                return step

            def stat_bank_free(name):
                if STAT[name]:
                    pe.wait_ge(rstd_ready, STAT[name])

            def sum_x(name):
                pe.wait_ge(sum_added, SQUARE[name] + DC)
                stat_bank_free(name)
                sum_columns(sum_sq).then_inc(total_ready, 1)

            def sum_head(group, h):
                pe.wait_ge(head_sq, h + {"head": 1, "hgrn": 7}[group])
                if h == 0:
                    stat_bank_free(group + "0")
                sum_columns(sq[:, h % 2, :], QB * h).then_inc(total_ready if h == HEADS - 1 else head_summed, 1)

            def spread(name):
                pe.wait_ge(diagonal_ready, STAT[name] + 1)
                stat_bank_free(name)
                mm(stat_bank[:, :], ones[:, :], diagonal[:, :], start=True, stop=True).then_inc(spread_ready, 1)

            def total_x(name):
                sum_x(name)
                spread(name)

            def first_three(stage, split, hi=a_hi, lo=a_lo, spread_after=()):
                first = UNIT[stage][0]
                for i in range(3):
                    wait_bank(stage, i)
                pe.wait_ge(unit_split, first + 3)
                for k in range(DC):
                    pe.wait_ge(act_ready, SPLIT[split] + k + 1)
                    for i in range(3):
                        dst, cols = tile_bank(stage, i), slice(k * P, (k + 1) * P)
                        wh, wl = w_hi[:, (first + i) % SLOTS, cols], w_lo[:, (first + i) % SLOTS, cols]
                        mm(dst[:, :], wh, hi[:, k, :], start=(k == 0), stop=False)
                        mm(dst[:, :], wh, lo[:, k, :], start=False, stop=False)
                        step = mm(dst[:, :], wl, hi[:, k, :], start=False, stop=(k == DC - 1))
                        if k == DC - 1:
                            step.then_inc(unit_done, 1)
                    if spread_after and k == 0:
                        sum_head("head", HEADS - 1)
                    if k in spread_after:
                        spread(f"head{spread_after.index(k)}")

            def first_tiles(stage, split, summed=False):
                if summed:
                    sum_x(split)
                first_three(stage, split)
                if not summed:
                    sum_x(split)
                fill(stage, [(3, 0, 4)])
                spread(split)
                fill(stage, [(3, 4, DC)])

            def hidden(stage, split, summed=False):
                first, n, blocks = UNIT[stage]
                first_tiles(stage, split, summed)
                with pe.Fori(0, n // 4 - 1) as it:
                    for j in range(4, 8):
                        wait_bank(stage, j, it)
                        unit_blocks(first + j, blocks, tile_bank(stage, j), 0, a_hi, a_lo, True, True, it, 4)

            def down(stage, turn):
                first = UNIT[stage][0]
                with pe.Fori(0, DC // 4) as it:
                    for j in range(4):
                        wait_bank(stage, j, it)
                        for half in range(2):
                            if j == 0:
                                pe.wait_ge(hidden_ready, FC * turn + (half + 1) * DOWN_CHUNKS)
                            unit_blocks(first + 2 * j + half, DOWN_CHUNKS, tile_bank(stage, j),
                                        half * DOWN_CHUNKS, h_hi, h_lo, half == 0, half == 1, it, 8)


            def aux1(t):
                name = aux_of_tile1(t)
                dst = aux_wait(*name)
                wait(tile_read("proj1", t))
                if name[0] == "rope":
                    mm(dst[:, :], rot[:, :], unrot[:, name[1] % 2, :], start=True, stop=True).then_inc(aux_ready, 1)
                else:
                    for j in range(QB):
                        step = pe.transpose(dst[:, j * P:(j + 1) * P], v1t[name[1] % 2][:, j * P:(j + 1) * P],
                                            ident[:, :])
                    step.then_inc(aux_ready, 1)

            first_three("proj1", "norm1")
            pe.wait_ge(const_loaded, 32)
            pe.wait_ge(const1_loaded, 16 * 7)
            sum_x("norm1")
            for a in range(ATT_STEPS + 2):
                if a == 0:
                    fill("proj1", [(3, 0, 4)])
                    spread("norm1")
                    fill("proj1", [(3, 4, 7)])
                    for t in range(LEAD1):
                        aux1(t)
                if a < ATT_STEPS:
                    h, i = a // QB, a % QB
                    end = (i + 1) * P
                    pe.wait_ge(rope_done, 2 * h + 2)
                    for n in range(2):
                        dst = aux_wait("score", a, n)
                        rows = slice(64 * n, 64 * n + 64)
                        mm(dst[:, 0:end], q1[rows, h, i * P:end], k1[rows, h, 0:end], start=True, stop=False)
                        mm(dst[:, end - 64:end], neg_row[0:1, :], one_row[0:1, :], start=False,
                           stop=True).then_inc(aux_ready, 1)
                if 0 < a < ATT_STEPS:
                    fill("proj1", FILL1[a])
                    for t in AUX1[a]:
                        aux1(t)
                if 1 <= a <= ATT_STEPS:
                    dst = aux_wait("turn", a - 1)
                    pe.wait_ge(attn_ready, a)
                    for j in range((a - 1) % QB + 1):
                        step = pe.transpose(dst[:, j * P:(j + 1) * P], attn[:, (a - 1) % 2, j * P:(j + 1) * P],
                                            ident[:, :])
                    step.then_inc(aux_ready, 1)
                if a < ATT_STEPS:
                    dst = aux_wait("bias", a)
                    pe.wait_ge(rel_set, 1)
                    cols = slice(0, T) if a % 2 == 0 else slice(T, BIAS_COLS)
                    mm(dst[:, 0:cols.stop - cols.start], rel_wide[:, a // 2, :], onehot[:, cols], start=True,
                       stop=True).then_inc(aux_ready, 1)
                if a >= 2:
                    b = a - 2
                    h, i = b // QB, b % QB
                    if i == 0:
                        wait_bank("attn", h)
                        wait(aux_read("vtok", h))
                    wait(aux_read("turn", b))
                    dst = tile_bank("attn", h)
                    for j in range(i + 1):
                        step = mm(dst[:, i * P:(i + 1) * P], v1[:, j, h, :], attn_t[:, b % 2, j * P:(j + 1) * P],
                                  start=(j == 0), stop=(j == i))
                    if i == QB - 1:
                        step.then_inc(head_ready, 1)
                if a >= 6 and a % QB == 2:
                    sum_head("head", (a - 6) // QB)
                if a == ATT_STEPS:
                    for g in range(len(WINDOWS)):
                        dst = aux_wait("pool", g)
                        pe.wait_ge(pool_ready, g + 1)
                        mm(dst[:, :], pool_w[:, g, :], pool_d[:, g, :], start=True, stop=True).then_inc(aux_ready, 1)
            first_three("wo", "mix1", spread_after=(1, 2, 3, 4))
            for i in range(3, DC):
                project("wo", i)
            hidden("up1", "norm2", summed=True)
            down("down1", 0)
            total_x("final1")
            hidden("up2", "pre1")
            down("down2", 1)
            total_x("post1")
            pe.wait_ge(const2_loaded, 16 * 3)
            for n in range(LEAD2):
                if n == 0:
                    first_tiles("proj2", "mixpre")
                if n > 3:
                    project("proj2", n)
                for kind, m in AFTER2[n]:
                    if kind == "stat":
                        pe.wait_ge(head_sq, 5 + (m == "kidx"))
                        stat_bank_free(m)
                        sum_columns(sq[:, int(m == "kidx"), :]).then_inc(total_ready, 1)
                    elif kind == "spread":
                        spread(m)
                    elif kind == "wturn":
                        dst = aux_wait(kind, m)
                        wait(tile_read("proj2", 2))
                        for j in range(QB):
                            step = pe.transpose(dst[:, j * 8:j * 8 + 8], widx_t[0:8, j * P:(j + 1) * P],
                                                ident[0:8, 0:8])
                        step.then_inc(aux_ready, 1)
                    elif kind == "ckvtok":
                        dst = aux_wait(kind, m)
                        pe.wait_ge(norm_ready, 1)
                        for j in range(QB):
                            step = pe.transpose(dst[:, j * P:(j + 1) * P], ckv[:, j * P:(j + 1) * P], ident[:, :])
                        step.then_inc(aux_ready, 1)
                    elif kind == "qlat":
                        dst = aux_wait(kind, m)
                        wait(tile_read("proj2", 7 + m // 2))
                        rows = slice(64 * (m % 2), 64 * (m % 2) + 64)
                        mm(dst[:, :], wuk[rows, m // 2, :], qa[rows, (m // 2) % 2, :], start=True,
                           stop=True).then_inc(aux_ready, 1)
                    elif kind == "vturn":
                        dst = aux_wait(kind, m)
                        wait(tile_read("proj2", 11 + m))
                        for j in range(QB):
                            step = pe.transpose(dst[:, j * P:(j + 1) * P], i_t[:, m % 2, j * P:(j + 1) * P],
                                                ident[:, :])
                        step.then_inc(aux_ready, 1)
                    else:
                        dst = aux_wait(kind, m)
                        i, h = IDX_STEPS[m]
                        pe.wait_ge(norm_ready, 2)
                        wait(tile_read("proj2", 3 + h // 2))
                        rows = slice(64 * (h % 2), 64 * (h % 2) + 64)
                        mm(dst[:, 0:(i + 1) * P], qidx[rows, h // 2, i * P:(i + 1) * P],
                           kidx[rows, 0:(i + 1) * P], start=True, stop=True).then_inc(aux_ready, 1)
            for a in range(DSA_STEPS + 4):
                if a < DSA_STEPS:
                    h, i = a // QB, a % QB
                    end = (i + 1) * P
                    dst = aux_wait("logit", a)
                    wait(aux_read("qlat", h))
                    mm(dst[:, 0:end], qlat[:, h, i * P:end], ckv[:, 0:end], start=True,
                       stop=True).then_inc(aux_ready, 1)
                if 2 <= a < DSA_STEPS + 2:
                    b = a - 2
                    dst = aux_wait("turn2", b)
                    pe.wait_ge(attn2_ready, b + 1)
                    for j in range(b % QB + 1):
                        step = pe.transpose(dst[:, j * P:(j + 1) * P], attn2[:, b % 2, j * P:(j + 1) * P],
                                            ident[:, :])
                    step.then_inc(aux_ready, 1)
                if a < DSA_STEPS + 3:
                    fill("proj2", FILL2[a])
                if 3 <= a < DSA_STEPS + 3:
                    b = a - 3
                    h, i = b // QB, b % QB
                    if i == 0:
                        wait_bank("olat", h)
                        wait(aux_read("ckvtok", 0))
                    wait(aux_read("turn2", b))
                    dst = tile_bank("olat", h)
                    for j in range(i + 1):
                        step = mm(dst[:, i * P:(i + 1) * P], ckv_tok[:, j, :],
                                  attn2_t[:, b % 2, j * P:(j + 1) * P], start=(j == 0), stop=(j == i))
                    if i == QB - 1:
                        step.then_inc(head_ready, 1)
                if a >= 11 and a % 8 == 3:
                    t = (a - 11) // 8
                    dst = aux_wait("ya", t)
                    wait(tile_read("olat", 2 * t))
                    wait(tile_read("olat", 2 * t + 1))
                    for n in range(2):
                        step = mm(dst[64 * n:64 * n + 64, :], wuv[:, 2 * t + n, :], olat[:, n, :], start=True,
                                  stop=True)
                    step.then_inc(aux_ready, 1)
            fill("proj2", FILL2[GAP2])
            def hgrn_out(h):
                wait_bank("hgrn", h)
                for l in (6, 7, 8):
                    wait(aux_read("pair", h, l))
                wait(aux_read("vturn", h))
                s = h % 2
                dst = tile_bank("hgrn", h)
                for i in range(QB):
                    blocks = [(i, pair_d[:, s, i * P:(i + 1) * P])]
                    if i % 2:
                        blocks.append((i - 1, pair_1[:, s, i // 2, :]))
                    if i >= 2:
                        blocks += [(j, pair_2[:, s, j, (i - 2) * P:(i - 1) * P]) for j in range(2)]
                    for n, (j, pairs) in enumerate(blocks):
                        step = mm(dst[:, i * P:(i + 1) * P], v2[:, j, h, :], pairs, start=(n == 0),
                                  stop=(n == len(blocks) - 1))
                step.then_inc(head_ready, 1)

            for h in range(HEADS):
                s = h % 2
                dst = aux_wait("pair0", h)
                pe.wait_ge(k_ready, h + 1)
                for j in range(QB):
                    cols = slice(j * P, (j + 1) * P)
                    step = mm(dst[:, cols], hk[:, s, cols], hq[:, s, cols], start=True, stop=True)
                step.then_inc(aux_ready, 1)
                for l, b in enumerate(LEVELS):
                    e = h * len(LEVELS) + l
                    dst = aux_wait("pair", h, l)
                    pe.wait_ge(qk_ready, e + 1)
                    if b <= 64:
                        pieces = [(j, j * P, P, j * P) for j in range(QB)]
                    elif b == 128:
                        pieces = [(0, P, P, 0), (2, 3 * P, P, P)]
                    else:
                        pieces = [(0, 2 * P, 2 * P, 0), (1, 2 * P, 2 * P, 2 * P)]
                    for j, q0, n, col in pieces:
                        step = mm(dst[:, col:col + n], qk[:, e % 2, j * P:(j + 1) * P], qk[:, e % 2, q0:q0 + n],
                                  start=True, stop=True)
                    step.then_inc(aux_ready, 1)
                    fill("proj2", FILL2[GAP2 + 1 + e])
                    if h and l == 2:
                        hgrn_out(h - 1)
                    if h and l == 6:
                        sum_head("hgrn", h - 1)
            hgrn_out(HEADS - 1)
            for i, units in [(0, 1), (2, 0), (1, 1), (3, 2)] + [(i, 1) for i in range(4, 2 * DC)]:
                first = UNIT["branch"][0]
                wait_bank("branch", i)
                chunks = 4 * (i % 2)
                unit_blocks(first + i, 4, tile_bank("branch", i), chunks, a_hi, a_lo, True, True,
                            ready=(act_ready, SPLIT["y"] + chunks) if i < 2 else None, units=units)
                if i == 0:
                    sum_head("hgrn", HEADS - 1)
                for h in range(HEADS) if i == 2 else ():
                    spread(f"hgrn{h}")
            first_three("out", "merged", h_hi, h_lo)
            for i in range(3, DC):
                project("out", i, None, h_hi, h_lo)
            total_x("postmix")
            hidden("up3", "pre2")
            down("down3", 2)
            for i in range(DC):
                dst, u = tile_bank("pproj", i), UNIT["pproj"][0] + i // 4
                wait_bank("pproj", i)
                pe.wait_ge(unit_split, u + 1)
                if i == 0:
                    pe.wait_ge(act_ready, SPLIT["p"] + 2)
                for c in range(2):
                    cols = slice((2 * (i % 4) + c) * P, (2 * (i % 4) + c + 1) * P)
                    wh, wl = w_hi[:, u % SLOTS, cols], w_lo[:, u % SLOTS, cols]
                    mm(dst[:, :], wh, a_hi[:, c, :], start=(c == 0), stop=False)
                    mm(dst[:, :], wh, a_hi[:, 2 + c, :], start=False, stop=False)
                    step = mm(dst[:, :], wl, a_hi[:, c, :], start=False, stop=(c == 1))
                step.then_inc(unit_done if i % 4 == 3 else head_ready, 1)
            total_x("post2")
            first_tiles("ple", "plepre")
            for i in range(4, DC):
                project("ple", i)
            total_x("plepost")

        @block.scalar
        def _(act):
            fn = nc.scalar.activation

            def wait(pair):
                act.wait_ge(pair[0], pair[1])

            def unit_high_part(u, it=0, per_loop=0):
                if u >= LAST_UNIT:
                    return
                slot, size = u % SLOTS, BLOCKS_OF[u] * P
                act.wait_ge(raw_loaded[slot], 16 * (u // SLOTS + 1) + it * (16 * per_loop // SLOTS))
                fn(w_hi[:, slot, 0:size], raw[:, slot, 0:size], ACT.Copy).then_inc(unit_high, 1)

            def units_done(v, it=0, per_loop=0):
                act.wait_ge(unit_done, v + it * per_loop)
                if v + 2 not in EARLY:
                    unit_high_part(v + 2, it, per_loop)

            def tile_finished(stage, i):
                per_tile = 2 if stage.startswith("down") else 1
                for n in range(per_tile):
                    units_done(UNIT[stage][0] + per_tile * i + n + 1)

            def square(stage, k, src, made):
                q = SQUARE[stage] + k
                wait(made)
                if q >= 2:
                    act.wait_ge(sum_added, q - 1)
                fn(sq[:, q % 2, :], src, ACT.Square).then_inc(sq_ready, 1)

            def take_root(name, width, columns=QB):
                act.wait_ge(total_ready, SUM[name] + 1)
                fn(root[:, 0:columns], stat_bank[:, 0:columns], ACT.Sqrt, bias=prm("eps"), scale=1.0 / width).then_inc(
                    root_ready, 1)

            def square_head(group, h, src):
                if h >= 2:
                    act.wait_ge(head_summed, h - 1 + (3 if group == "hgrn" else 0))
                fn(sq[:, h % 2, :], src[:, h, :], ACT.Square).then_inc(head_sq, 1)

            def high(c, dst):
                act.wait_ge(chunk_ready, c + 1)
                fn(dst, chunk[:, c % 2, :], ACT.Copy).then_inc(hi_ready, 1)

            def scaled_high(g, k):
                fn(a_hi[:, k, :], x[:, k, :], ACT.Copy, scale=prm(g, k)).then_inc(hi_ready, 1)

            def scaled_highs(stage, g, before, units):
                unit_high_part(UNIT[units][0] + 3)
                for k in range(DC):
                    act.wait_ge(x_ready, before + k + 1)
                    scaled_high(g, k)
                    square(stage, k, x[:, k, :], (x_ready, before + k + 1))
                take_root(stage, D)
                for n in range(2):
                    units_done(UNIT[units][0] + n + 1)

            def highs(stage, first=0, n=DC, dst=a_hi):
                for k in range(first, first + n):
                    high(SPLIT[stage] + k, dst[:, k, :])

            def keep_branch(stage, square_stage):
                for k in range(DC):
                    tile_finished(stage, k)
                    square(square_stage, k, tile_bank(stage, k)[:, :], tile_done(stage, k))
                    fn(y[:, k, :], tile_bank(stage, k)[:, :], ACT.Copy).then_inc(tile_sem(stage, k), 1)

            for dst, name in ((rot[:, :], "c_rot"), (pool_w[:, :, :], "pool_w"), (count[:, :, :], "c_count"),
                              (onehot[:, :], "c_onehot"), (rel[:, :], "rel")):
                src = ins[name].rearrange("p (g c) -> p g c", g=4) if name == "c_count" else ins[name]
                act.dma_start(dst, src).then_inc(const1_loaded, 16)
            lam_src = ins["lambdas"]
            act.dma_start(lam_in[:, :, :], bass.AP(lam_src.tensor, lam_src.offset, [[0, P], [64, 4], [1, 64]])
                          ).then_inc(const1_loaded, 16)
            pos_src = ins["positions"]
            act.dma_start(pos_i[:, :], bass.AP(pos_src.tensor, pos_src.offset, [[0, P], [1, T]])
                          ).then_inc(const1_loaded, 16)
            act.wait_ge(par_loaded, 16)
            for k in range(DC):
                if k in START_UNITS:
                    unit_high_part(START_UNITS.index(k))
                act.wait_ge(x_loaded[k], 16)
                scaled_high("norm_mix_g", k)
                square("norm1", k, x[:, k, :], (x_loaded[k], 16))
            unit_high_part(len(START_UNITS))
            act.wait_ge(trig_in, 1)
            fn(sin[:, :], sin[:, :], ACT.Sin).then_inc(trig, 1)
            act.wait_ge(trig_in, 2)
            fn(cos[:, :], cos[:, :], ACT.Sin).then_inc(trig, 1)
            take_root("norm1", D)
            def keep_tile1(t):
                tile_finished("proj1", t)
                kind, h = TILES1[t]
                if kind not in "qk":
                    return
                r = aux_of_tile1(t)[1]
                if r >= 2:
                    wait(aux_read("rope", r - 2))
                fn(unrot[:, r % 2, :], tile_bank("proj1", t)[:, :], ACT.Copy).then_inc(tile_sem("proj1", t), 1)

            def keep_values(h):
                act.wait_ge(aux_ready, AUX["vtok", h] + 1)
                fn(v1[:, :, h, :], aux_bank("vtok", h)[:, :].rearrange("p (j d) -> p j d", j=QB),
                   ACT.Copy).then_inc(aux_sem("vtok", h), 1)

            for t in range(LEAD1):
                keep_tile1(t)
            act.wait_ge(lam_sum, 1)
            fn(small[:, 3:5], small[:, 1:3], ACT.Exp).then_inc(lam_exp, 1)
            for a in range(ATT_STEPS + 2):
                if a < ATT_STEPS:
                    h, i = a // QB, a % QB
                    end = (i + 1) * P
                    if a == 0:
                        keep_values(0)
                    if a >= 2:
                        act.wait_ge(attn_ready, a - 1)
                    for n in range(2):
                        act.wait_ge(neg_max, 2 * a + n + 1)
                        s = 2 * (a % 2) + n
                        fn(prob[:, a % 2, n, 0:end], aux_bank("score", a, n)[:, 0:end], ACT.Exp,
                           bias=small[:, 8 + s:9 + s], scale=DIFF_SCALE,
                           accum_out=small[:, 12 + s:13 + s]).then_inc(aux_sem("score", a, n), 1)
                    for t in closed(FILL1[a]):
                        keep_tile1(t)
                    for t in AUX1[a]:
                        if a and TILES1[t][0] == "v":
                            keep_values(TILES1[t][1])
                if 1 <= a <= ATT_STEPS:
                    act.wait_ge(aux_ready, AUX["turn", a - 1] + 1)
                    n = ((a - 1) % QB + 1) * P
                    fn(attn_t[:, (a - 1) % 2, 0:n], aux_bank("turn", a - 1)[:, 0:n], ACT.Copy).then_inc(
                        aux_sem("turn", a - 1), 1)
                if a < ATT_STEPS:
                    act.wait_ge(aux_ready, AUX["bias", a] + 1)
                    h = a // 2
                    if h >= 2:
                        act.wait_ge(bias_out[h % 2], 16 * (h // 2))
                    cols = slice(0, T) if a % 2 == 0 else slice(T, BIAS_COLS)
                    fn(bias_slot[:, h % 2, cols], aux_bank("bias", a)[:, 0:cols.stop - cols.start],
                       ACT.Copy).then_inc(aux_sem("bias", a), 1)
                    if a % 2:
                        wait(aux_read("bias", a))
                        wait(aux_read("bias", a - 1))
                        act.dma_start(bias_rows[h], bias_slot[:, h % 2, :]).then_inc(bias_out[h % 2], 16)
                if a >= 2 and (a - 2) % QB == QB - 1:
                    h = (a - 2) // QB
                    act.wait_ge(head_ready, h + 1)
                    fn(o1[:, h, :], tile_bank("attn", h)[:, :], ACT.Copy).then_inc(tile_sem("attn", h), 1)
                    wait(tile_read("attn", h))
                    if h == 0:
                        act.wait_ge(sum_added, DC)
                    square_head("head", h, o1)
                if a == ATT_STEPS:
                    highs("mix1", 0, 4)
            unit_high_part(UNIT["wo"][0] + 3)
            take_root("head", P, HEADS * QB)
            highs("mix1", 4, 4)
            for k in range(DC):
                tile_finished("wo", k)
                square("norm2", k, x[:, k, :], tile_read("wo", k))
            unit_high_part(UNIT["up1"][0] + 3)
            for k in range(DC):
                scaled_high("norm_ffn_g", k)
            take_root("norm2", D)
            def silu_pairs(i, it=0, per_loop=0):
                first = UNIT["up1"][0]
                for j in (i, i + 1):
                    units_done(first + 2 * j + 1, it, 2 * per_loop)
                    units_done(first + 2 * j + 2, it, 2 * per_loop)
                    act.wait_ge(gate_ready, j + 1 + it * per_loop)
                    fn(silu[:, :], gate[:, :], ACT.Silu).then_inc(silu_ready, 1)

            silu_pairs(0)
            with act.Fori(0, FC // 2 - 2) as it:
                silu_pairs(2, it, 2)
            silu_pairs(FC - 2)
            for k in range(DC):
                tile_finished("down1", k)
                square("final1", k, x[:, k, :], tile_read("down1", k))
            take_root("final1", D)
            scaled_highs("pre1", "ffn1_pre_g", 0, "up2")

            def silus(stage, turn):
                first = UNIT[stage][0]
                slots = [gate, silu]

                def one(i, it=0, per_loop=0):
                    if i:
                        units_done(first + 2 * i + 1, it, 2 * per_loop)
                    act.wait_ge(tile_sem(stage, 2 * i), TILE[stage, 2 * i][1] + 1 + it * (2 * per_loop // BANKS))
                    fn(slots[i % 2][:, :], slots[i % 2][:, :], ACT.Silu).then_inc(silu_ready, 1)
                    if i:
                        units_done(first + 2 * i + 2, it, 2 * per_loop)

                one(0)
                one(1)
                with act.Fori(0, FC // 2 - 2) as it:
                    one(2, it, 2)
                    one(3, it, 2)
                one(FC - 2)
                one(FC - 1)

            silus("up2", 1)
            keep_branch("down2", "post1")
            take_root("post1", D)
            act.dma_start(wuk[:, :, :], ins["wuk"]).then_inc(const2_loaded, 16)
            act.dma_start(wuv[:, :, :], ins["wuv"]).then_inc(const2_loaded, 16)
            act.dma_start(tri[:, :], ins["c_tri"]).then_inc(const2_loaded, 16)

            def load_bias(h):
                src = bias_rows[h]
                act.dma_start(t_bias[:, h % 2, :], bass.AP(src.tensor, src.offset + P - 1,
                                                           [[BIAS_COLS - 1, P], [1, T]])
                              ).then_inc(bias_in[h % 2], 16)

            for n in range(2):
                act.wait_ge(bias_out[n], 16 * (DSA_HEADS // 2))
            load_bias(0)
            load_bias(1)
            scaled_highs("mixpre", "mix_pre_g", DC, "proj2")
            act.wait_ge(lam_sum, 2)
            fn(small[:, 36:40], small[:, 32:36], ACT.Sigmoid).then_inc(lam_exp, 1)
            def keep_gate(n):
                s = SPILLED["gate"] + n - TILES2.index("gate0")
                tile_finished("proj2", n)
                act.wait_ge(spill_out[s % 2], 16 * (s // 2))
                fn(spill_slot[s % 2][:, :], tile_bank("proj2", n)[:, :], ACT.Copy).then_inc(tile_sem("proj2", n), 1)
                wait(tile_read("proj2", n))
                act.dma_start(spill[s], spill_slot[s % 2][:, :]).then_inc(spill_out[s % 2], 16)

            for n, name in enumerate(TILES2[:LEAD2]):
                kind, t = name.rstrip("0123456789"), int(name[len(name.rstrip("0123456789")):] or 0)
                if kind == "gate":
                    keep_gate(n)
                    continue
                if n >= 2:
                    tile_finished("proj2", n)
                if kind in ("ckv", "kidx"):
                    wait(tile_read("proj2", n))
                    fn(sq[:, n, :], (ckv_raw, kidx_raw)[n][:, :], ACT.Square).then_inc(head_sq, 1)
                elif kind in SPILLED:
                    s = SPILLED[kind] + t
                    wait(tile_read("proj2", n))
                    fn(spill_slot[s % 2][:, :], spill_slot[s % 2][:, :], ACT.Silu if s < 8 else ACT.Sigmoid).then_inc(
                        spill_made, 1)
                    act.wait_ge(spill_made, 1 + [m for m in TILES2 if m[:2] in SPILLED].index(name))
                    act.dma_start(spill[s], spill_slot[s % 2][:, :]).then_inc(spill_out[s % 2], 16)
                for ev, m in AFTER2[n]:
                    if ev == "stat":
                        take_root(m, P)
                        continue
                    if ev in ("wturn", "spread"):
                        continue
                    small_out = aux_bank(ev, m)[:, :]
                    act.wait_ge(aux_ready, AUX[ev, m] + 1)
                    if ev == "ckvtok":
                        fn(ckv_tok[:, :, :], small_out.rearrange("p (j d) -> p j d", j=QB), ACT.Copy).then_inc(
                            aux_sem(ev, m), 1)
                    elif ev == "qlat":
                        fn(qlat[:, m, :], small_out, ACT.Copy, scale=ATT_SCALE).then_inc(aux_sem(ev, m), 1)
                    elif ev == "vturn":
                        fn(v2[:, :, m, :], small_out.rearrange("p (j d) -> p j d", j=QB), ACT.Copy).then_inc(
                            aux_sem(ev, m), 1)
                    else:
                        if m >= 2:
                            act.wait_ge(relu_used, m - 1)
                        w = (IDX_STEPS[m][0] + 1) * P
                        fn(relu[:, m % 2, 0:w], small_out[:, 0:w], ACT.Relu).then_inc(aux_sem(ev, m), 1)
            for a in range(DSA_STEPS + 4):
                if 2 <= a < DSA_STEPS + 2:
                    b = a - 2
                    act.wait_ge(aux_ready, AUX["turn2", b] + 1)
                    n = (b % QB + 1) * P
                    fn(attn2_t[:, b % 2, 0:n], aux_bank("turn2", b)[:, 0:n], ACT.Copy).then_inc(
                        aux_sem("turn2", b), 1)
                if a < DSA_STEPS:
                    h, i = a // QB, a % QB
                    end = (i + 1) * P
                    act.wait_ge(logit_max, a + 1)
                    if a >= 2:
                        act.wait_ge(attn2_ready, a - 1)
                    fn(prob2[:, a % 2, 0:end], logit[:, a % 2, 0:end], ACT.Exp,
                       bias=small[:, 24 + a % 2:25 + a % 2],
                       accum_out=small[:, 26 + a % 2:27 + a % 2]).then_inc(exp2_done, 1)
                    if i == 1 and 1 <= h < DSA_HEADS - 1:
                        act.wait_ge(bias_mask_ready, QB * h)
                        load_bias(h + 1)
                if a:
                    for t in closed(FILL2[a - 1]):
                        keep_gate(t)
                if 3 <= a < DSA_STEPS + 3 and (a - 3) % QB == QB - 1:
                    h = (a - 3) // QB
                    act.wait_ge(head_ready, HEADS + h + 1)
                    if h >= 2:
                        act.wait_ge(aux_ready, AUX["ya", (h - 2) // 2] + 1)
                    fn(olat[:, h % 2, :], tile_bank("olat", h)[:, :], ACT.Copy).then_inc(tile_sem("olat", h), 1)
            act.wait_ge(aux_ready, AUX["ya", 3] + 1)
            act.dma_start(masks[:, :, :], ins["c_masks"].rearrange("p (l t) -> p l t", l=8)).then_inc(
                const3_loaded, 16)
            act.dma_start(resets[:, :, :], ins["c_resets"].rearrange("p (l t) -> p l t", l=3)).then_inc(
                const3_loaded, 16)
            for n in range(2):
                act.wait_ge(spill_out[n], 16 * 6)

            def load_head(h):
                act.dma_start(hq[:, h % 2, :], spill[h]).then_inc(h_loaded[h % 2], 16)
                act.dma_start(hf[:, h % 2, :], spill[8 + h]).then_inc(h_loaded[h % 2], 16)

            load_head(0)
            load_head(1)
            for h in range(HEADS):
                act.dma_start(hg[:, h, :], spill[4 + h]).then_inc(hg_loaded, 16)

            def keep_head(h):
                act.wait_ge(head_ready, HEADS + DSA_HEADS + h + 1)
                fn(oh[:, h, :], tile_bank("hgrn", h)[:, :], ACT.Copy).then_inc(tile_sem("hgrn", h), 1)
                wait(tile_read("hgrn", h))
                square_head("hgrn", h, oh)

            def log_forget(h):
                act.wait_ge(f_ready, h + 1)
                fn(logf[:, :], hf[:, h % 2, :], ACT.Ln).then_inc(logf_ready, 1)

            log_forget(0)
            for h in range(HEADS):
                for l, b in enumerate(LEVELS):
                    e = h * len(LEVELS) + l
                    act.wait_ge(diff_ready, e + 1)
                    if e >= 2:
                        act.wait_ge(qk_ready, e - 1)
                    if b <= 32:
                        fn(decay[:, e % 2, :], diff[:, e % 2, :], ACT.Exp).then_inc(decay_ready, 1)
                    else:
                        split_ap = lambda ap: ap.rearrange("p (n c) -> p n c", c=2 * b)
                        to = split_ap(decay[:, e % 2, :])
                        fn(to[:, :, 0:b], split_ap(diff[:, e % 2, :])[:, :, 0:b], ACT.Exp).then_inc(decay_ready, 1)
                        fn(to[:, :, b:2 * b], split_ap(run[:, h % 2, l - 6, :])[:, :, b:2 * b],
                           ACT.Exp).then_inc(decay_ready, 1)
                    if e >= 1:
                        for t in closed(FILL2[GAP2 + e - 1]):
                            keep_gate(t)
                    if h and l == 4:
                        keep_head(h - 1)
                    if l == 5 and h + 1 < HEADS:
                        log_forget(h + 1)
                    if l >= 8:
                        for m in (7, 8):
                            if h >= 2:
                                act.wait_ge(head_ready, HEADS + DSA_HEADS + h - 1)
                            act.wait_ge(aux_ready, AUX["pair", h, m] + 1)
                            src = aux_bank("pair", h, m)
                            if m == 7:
                                fn(pair_1[:, h % 2, :, :], src[:, 0:2 * P].rearrange("p (n t) -> p n t", n=2),
                                   ACT.Copy).then_inc(aux_sem("pair", h, m), 1)
                            else:
                                fn(pair_2[:, h % 2, :, :], src[:, :].rearrange("p (n t) -> p n t", n=2),
                                   ACT.Copy).then_inc(aux_sem("pair", h, m), 1)
                if h + 2 < HEADS:
                    wait(aux_read("pair", h, 6))
                    act.wait_ge(qk_ready, (h + 1) * len(LEVELS))
                    load_head(h + 2)
            for e in (HGRN_STEPS - 2, HGRN_STEPS - 1):
                for t in closed(FILL2[GAP2 + 1 + e]):
                    keep_gate(t)
            def load_gates(m):
                for n in range(2):
                    s = SPILLED["gate"] + 8 * n + m
                    act.wait_ge(spill_out[s % 2], 16 * (s // 2 + 1))
                    act.dma_start(gates_in[:, 2 * (m % 2) + n, :], spill[s]).then_inc(gates_loaded[m % 2], 16)

            act.wait_ge(aux_ready, len(AUX))
            load_gates(0)
            load_gates(1)
            for t in range(4):
                act.wait_ge(chunk_ready, SPLIT["y"] + t + 1)
                fn(a_hi[:, t, :], ya[:, t, :], ACT.Copy).then_inc(hi_ready, 1)
            unit_high_part(UNIT["branch"][0] + 3)
            keep_head(HEADS - 1)
            take_root("hgrn", P, HEADS * QB)
            highs("y", 4, 4)

            def open_gates(m):
                act.wait_ge(gates_scaled, m + 1)
                for n in range(2):
                    slot = gates_in[:, 2 * (m % 2) + n, :]
                    fn(slot, slot, ACT.Sigmoid, bias=prm("b_gate", 8 * n + m)).then_inc(gates_open, 1)

            open_gates(0)
            for m in range(DC):
                tile_finished("branch", 2 * m)
                tile_finished("branch", 2 * m + 1)
                high(SPLIT["merged"] + m, h_hi[:, m, :])
                if m + 2 < DC:
                    load_gates(m + 2)
                if m + 1 < DC:
                    open_gates(m + 1)
            unit_high_part(UNIT["out"][0] + 3)
            keep_branch("out", "postmix")
            take_root("postmix", D)
            scaled_highs("pre2", "ffn2_pre_g", 2 * DC, "up3")
            silus("up3", 2)
            for c in range(2):
                act.dma_start(pe_in[:, c, :], ins["pt"][c]).then_inc(p_loaded, 16)
            highs("p", 0, 2)
            keep_branch("down3", "post2")
            for i in range(DC):
                if i % 4 == 3:
                    units_done(UNIT["pproj"][0] + i // 4 + 1)
                else:
                    act.wait_ge(head_ready, 2 * HEADS + DSA_HEADS + i - i // 4 + 1)
                fn(p_proj[:, i, :], tile_bank("pproj", i)[:, :], ACT.Copy).then_inc(tile_sem("pproj", i), 1)
            take_root("post2", D)
            scaled_highs("plepre", "ple_pre_g", 3 * DC, "ple")
            slots = [gate, silu]
            for i in range(DC + 1):
                if i < DC:
                    if i >= 2:
                        tile_finished("ple", i)
                    wait(tile_read("ple", i))
                    fn(slots[i % 2][:, :], slots[i % 2][:, :], ACT.Sigmoid).then_inc(ple_open, 1)
                if i:
                    square("plepost", i - 1, p_proj[:, i - 1, :], (y_ready, i))
            take_root("plepost", D)

        @block.vector
        def _(dve):
            v = nc.vector
            steps = [0]

            def step(ins_, it=0, per_loop=0):
                steps[0] += 1
                ins_.then_inc(dve_step, 1)
                dve.wait_ge(dve_step, steps[0] + (it * per_loop if per_loop else 0))

            def wait(pair):
                dve.wait_ge(pair[0], pair[1])

            def invert(name, columns=QB):
                dve.wait_ge(root_ready, SUM[name] + 1)
                step(v.reciprocal(inverse[:, 0:columns], root[:, 0:columns]))

            def make_diagonal(column=0):
                v.tensor_tensor(diagonal[:, :].rearrange("p (j t) -> p j t", j=QB),
                                ident[:, :].rearrange("p (o t) -> p o t", o=1).broadcast_to([P, QB, P]),
                                inverse[:, column:column + QB].rearrange("p (j o) -> p j o", o=1).broadcast_to(
                                    [P, QB, P]), ALU.mult).then_inc(diagonal_ready, 1)

            def take_rstd(name, dst=rstd):
                n = STAT[name]
                dve.wait_ge(spread_ready, n + 1)
                v.tensor_copy(dst[:, :], stat_bank[:, :]).then_inc(rstd_ready, 1)
                dve.wait_ge(rstd_ready, n + 1)

            def norm_heads(group, src, g, before):
                invert(group, HEADS * QB)
                make_diagonal()
                for h in range(HEADS):
                    c = before + h
                    take_rstd(f"{group}{h}")
                    if h + 1 < HEADS:
                        make_diagonal(QB * (h + 1))
                    if h:
                        low(c - 1, a_lo[:, 3 + h, :], a_hi[:, 3 + h, :])
                    slot_free(c)
                    if h:
                        dve.wait_ge(chunk_ready, c)
                    v.scalar_tensor_tensor(chunk[:, c % 2, :], src[:, h, :], g(h), rstd[:, :], ALU.mult,
                                           ALU.mult).then_inc(chunk_ready, 1)
                    made(c)
                low(before + HEADS - 1, a_lo[:, 3 + HEADS, :], a_hi[:, 3 + HEADS, :])

            def rsqrt(name):
                invert(name)
                make_diagonal()
                take_rstd(name)

            def low(c, dst, hi):
                dve.wait_ge(hi_ready, c + 1)
                v.tensor_tensor(dst, chunk[:, c % 2, :], hi.bitcast(F32), ALU.subtract).then_inc(act_ready, 1)

            def made(c):
                dve.wait_ge(chunk_ready, c + 1)

            def slot_free(c):
                if c >= 2:
                    dve.wait_ge(act_ready, c - 1)

            def scaled_low(stage, g, k):
                dve.wait_ge(hi_ready, SPLIT[stage] + k + 1)
                v.scalar_tensor_tensor(a_lo[:, k, :], x[:, k, :], prm(g, k), a_hi[:, k, :].bitcast(F32), ALU.mult,
                                       ALU.subtract).then_inc(act_ready, 1)

            def scaled_done(stage):
                dve.sem_inc(chunk_ready, DC)
                rsqrt(stage)

            def norm_to_split(name, stage, g):
                rsqrt(name)
                c0 = SPLIT[stage]
                for k in range(DC + 1):
                    if k < DC:
                        slot_free(c0 + k)
                        v.scalar_tensor_tensor(chunk[:, (c0 + k) % 2, :], x[:, k, :], prm(g, k), rstd[:, :],
                                               ALU.mult, ALU.mult).then_inc(chunk_ready, 1)
                    if k:
                        made(c0 + k - 1)
                        low(c0 + k - 1, a_lo[:, k - 1, :], a_hi[:, k - 1, :])

            def add_square(stage, k):
                q = SQUARE[stage] + k
                dve.wait_ge(sq_ready, q + 1)
                if k == 0:
                    v.tensor_copy(sum_sq[:, :], sq[:, q % 2, :]).then_inc(sum_added, 1)
                else:
                    dve.wait_ge(sum_added, q)
                    v.tensor_tensor(sum_sq[:, :], sum_sq[:, :], sq[:, q % 2, :], ALU.add).then_inc(sum_added, 1)

            def add_tiles(stage, square_stage):
                for k in range(DC + 1):
                    if k < DC:
                        wait(tile_done(stage, k))
                        v.tensor_tensor(x[:, k, :], x[:, k, :], tile_bank(stage, k)[:, :], ALU.add).then_inc(
                            tile_sem(stage, k), 1)
                    if k:
                        add_square(square_stage, k - 1)

            def add_branch(name, g, src, last_read, signal, before, square_stage=None, split=None):
                rsqrt(name)
                for k in range(DC + 1):
                    if k < DC:
                        if last_read is not None:
                            wait(last_read(k))
                        if k >= 2:
                            dve.wait_ge(signal, before + k - 1)
                        step(v.scalar_tensor_tensor(chunk[:, k % 2, :], src[:, k, :], prm(g, k), rstd[:, :],
                                                    ALU.mult, ALU.mult))
                        v.tensor_tensor(x[:, k, :], x[:, k, :], chunk[:, k % 2, :], ALU.add).then_inc(signal, 1)
                    if k and square_stage:
                        add_square(square_stage, k - 1)
                    if k and split:
                        scaled_low(split[0], split[1], k - 1)

            v.memset(pool_in[:, :, 0:PAD], 0.0)
            v.memset(pool_s[:, :, 0:PAD], 0.0)
            v.memset(neg_row[:, 0:64], NEG)
            v.memset(neg_row[:, 64:P], 0.0)
            step(v.memset(one_row[:, :], 1.0))
            dve.wait_ge(par_loaded, 16)
            for k in range(DC):
                scaled_low("norm1", "norm_mix_g", k)
                add_square("norm1", k)
            dve.sem_inc(chunk_ready, DC)
            for name, factor in (("attn_norm_g", 1.0 - LAM_INIT), ("ffn1_post_g", 0.5), ("ffn2_post_g", 0.5)):
                first, n = PARAMS[name]
                step(v.tensor_scalar(par[:, first:first + n], par[:, first:first + n], factor, None, ALU.mult))
            dve.wait_ge(const1_loaded, 16 * 7)
            v.tensor_copy(rel_wide[:, :, :], rel[:, :].rearrange("p (h o) -> p h o", o=1).broadcast_to(
                [32, DSA_HEADS, P])).then_inc(rel_set, 1)
            step(v.tensor_copy(angle[:, :], pos_i[:, :]))
            step(v.tensor_scalar(angle[:, :], angle[:, :], prm("inv_freq"), None, ALU.mult))
            step(v.tensor_scalar(turns[:, :], angle[:, :], float(1 / (2 * np.pi)), ROUND, ALU.mult, ALU.add))
            step(v.tensor_scalar(turns[:, :], turns[:, :], ROUND, None, ALU.subtract))
            for part in TURN_PARTS:
                step(v.scalar_tensor_tensor(angle[:, :], turns[:, :], -part, angle[:, :], ALU.mult, ALU.add))
            v.tensor_scalar(sin[:, :], angle[:, :], PI_BELOW, -PI_BELOW, ALU.min, ALU.max).then_inc(trig_in, 1)
            step(v.scalar_tensor_tensor(cos[:, :], angle[:, :], -1.0, angle[:, :], ALU.mult, ALU.max))
            v.tensor_scalar(cos[:, :], cos[:, :], -1.0, float(np.pi / 2), ALU.mult, ALU.add).then_inc(trig_in, 1)
            step(v.tensor_tensor(lam_in[:, 0:3:2, :], lam_in[:, 0:3:2, :], lam_in[:, 1:4:2, :], ALU.mult))
            v.tensor_reduce(small[:, 1:3], lam_in[:, 0:3:2, :], AX_X, ALU.add).then_inc(lam_sum, 1)
            lb = PARAMS["hgrn_lb0"][0]
            v.tensor_tensor(small[:, 32:36], par[:, lb:lb + 4], par[:, lb + 4:lb + 8], ALU.subtract).then_inc(
                lam_sum, 1)

            dve.wait_ge(const_loaded, 32)
            rsqrt("norm1")
            dve.wait_ge(trig, 2)
            v.tensor_tensor(cos[:, :], cos[:, :], rstd[:, :], ALU.mult).then_inc(cos_scaled, 1)
            v.tensor_tensor(sin[:, :], sin[:, :], rstd[:, :], ALU.mult).then_inc(cos_scaled, 1)
            dve.wait_ge(cos_scaled, 2)

            def take_tile1(t):
                kind, h = TILES1[t]
                if kind in "qk":
                    return
                wait(tile_done("proj1", t))
                if kind == "v":
                    if h >= 2:
                        dve.wait_ge(aux_ready, AUX["vtok", h - 2] + 1)
                    dst = v1t[h % 2][:, :]
                else:
                    dst = pool_in[:, h % 2, PAD:]
                v.tensor_tensor(dst, tile_bank("proj1", t)[:, :], rstd[:, :], ALU.mult).then_inc(
                    tile_sem("proj1", t), 1)

            def rotate(t):
                _, r = aux_of_tile1(t)
                raw_q = unrot[:, r % 2, :]
                dst = (q1, k1)[r % 2][:, r // 2, :]
                wait(tile_read("proj1", t))
                v.tensor_tensor(dst, raw_q, cos[:, :], ALU.mult)
                dve.wait_ge(aux_ready, AUX["rope", r] + 1)
                if r:
                    dve.wait_ge(rope_done, r)
                v.tensor_tensor(rope_a[:, :], aux_bank("rope", r)[:, :], sin[:, :], ALU.mult).then_inc(
                    aux_sem("rope", r), 1)
                wait(aux_read("rope", r))
                v.tensor_tensor(dst, dst, rope_a[:, :], ALU.add).then_inc(rope_done, 1)
                dve.wait_ge(rope_done, r + 1)

            def pool_difference(t):
                g = TILES1[t][1]
                w = WINDOWS[g]
                wait(tile_read("proj1", t))
                token = pool_in[:, g % 2, PAD:]
                src, shift, n = pool_in[:, g % 2, :], 1, 0
                while shift < w:
                    to = pool_s[:, n % 2, :]
                    step(v.tensor_tensor(to[:, PAD:], src[:, PAD:], src[:, PAD - shift:PAD + T - shift], ALU.add))
                    src, shift, n = to, 2 * shift, n + 1
                diff_ = pool_d[:, g, :]
                step(v.scalar_tensor_tensor(diff_, src[:, PAD:], 1.0 / w, token, ALU.mult, ALU.subtract))
                step(v.tensor_tensor(rope_a[:, 0:w], src[:, PAD:PAD + w], count[:, g, 0:w], ALU.mult))
                v.tensor_tensor(diff_[:, 0:w], rope_a[:, 0:w], token[:, 0:w], ALU.subtract).then_inc(pool_ready, 1)
                dve.wait_ge(pool_ready, g + 1)

            rotate(0)
            take_tile1(LEAD1 - 1)
            rotate(1)
            dve.wait_ge(lam_exp, 1)
            step(v.tensor_tensor(small[:, 5:6], small[:, 4:5], small[:, 3:4], ALU.subtract))
            step(v.tensor_scalar(small[:, 5:6], small[:, 5:6], -LAM_INIT, None, ALU.add))
            for a in range(ATT_STEPS + 1):
                if a < ATT_STEPS:
                    end = (a % QB + 1) * P
                    for n in range(2):
                        s = 2 * (a % 2) + n
                        dve.wait_ge(aux_ready, AUX["score", a, n] + 1)
                        step(v.tensor_reduce(small[:, 6:7], aux_bank("score", a, n)[:, 0:end], AX_X, ALU.max))
                        v.tensor_scalar(small[:, 8 + s:9 + s], small[:, 6:7], -DIFF_SCALE, None,
                                        ALU.mult).then_inc(neg_max, 1)
                        dve.wait_ge(neg_max, 2 * a + n + 1)
                if a:
                    b = a - 1
                    end, s = (b % QB + 1) * P, 2 * (b % 2)
                    wait(aux_read("score", b, 0))
                    wait(aux_read("score", b, 1))
                    if b >= 2:
                        dve.wait_ge(aux_ready, AUX["turn", b - 2] + 1)
                        dve.wait_ge(attn_ready, b)
                    step(v.reciprocal(small[:, 16 + s:18 + s], small[:, 12 + s:14 + s]))
                    step(v.tensor_tensor(small[:, 17 + s:18 + s], small[:, 17 + s:18 + s], small[:, 5:6], ALU.mult))
                    p0, p1 = prob[:, b % 2, 0, 0:end], prob[:, b % 2, 1, 0:end]
                    step(v.tensor_scalar(p1, p1, small[:, 17 + s:18 + s], None, ALU.mult))
                    v.scalar_tensor_tensor(attn[:, b % 2, 0:end], p0, small[:, 16 + s:17 + s], p1, ALU.mult,
                                           ALU.add).then_inc(attn_ready, 1)
                if a < ATT_STEPS:
                    for t in closed(FILL1[a]):
                        take_tile1(t)
                if 0 < a < ATT_STEPS:
                    for t in AUX1[a]:
                        if TILES1[t][0] in "qk":
                            rotate(t)
                if a:
                    for t in closed(FILL1[a - 1]):
                        if TILES1[t][0] == "p":
                            pool_difference(t)
            for g in range(4):
                c = SPLIT["mix1"] + g
                dve.wait_ge(aux_ready, AUX["pool", g] + 1)
                slot_free(c)
                step(v.tensor_scalar(chunk[:, c % 2, :], aux_bank("pool", g)[:, :], prm("pool_scale", g), None,
                                     ALU.mult))
                dve.sem_inc(aux_sem("pool", g), 1)
                dve.sem_inc(chunk_ready, 1)
                low(c, a_lo[:, g, :], a_hi[:, g, :])
            norm_heads("head", o1, lambda h: prm("attn_norm_g", h), SPLIT["mix1"] + 4)
            add_tiles("wo", "norm2")
            for k in range(DC):
                scaled_low("norm2", "norm_ffn_g", k)
            dve.sem_inc(chunk_ready, DC)
            rsqrt("norm2")

            def hidden_at(buf, it, j):
                return buf[:, bass.ds(it * 2 + j, 1), :].rearrange("p k t -> p (k t)")

            for n in range(2):
                dve.wait_ge(bias_out[n], 16 * (DSA_HEADS // 2))
            first = UNIT["up1"][0]
            per = 14
            b = sq[:, 0, :]
            at_loop = steps[0]
            with dve.Fori(0, FC // 2) as it:
                def tap(name, tile):
                    at = PARAMS[name][0] + tile
                    return par[:, bass.ds(it * 4 + at, 1)]

                for j in range(2):
                    for n, dst in ((0, gate), (1, val)):
                        i = 2 * j + n
                        dve.wait_ge(unit_done, first + i + 1 + it * 4)
                        v.tensor_tensor(b[:, :], tile_bank("up1", i)[:, :], rstd[:, :], ALU.mult).then_inc(
                            tile_sem("up1", i), 1)
                        dve.wait_ge(tile_sem("up1", i), TILE["up1", i][1] + 1 + it)
                        step(v.tensor_scalar(dst[:, :], b[:, :], tap("conv_w2", i), tap("conv_b", i), ALU.mult,
                                             ALU.add), it, per)
                        step(v.scalar_tensor_tensor(dst[:, 1:T], b[:, 0:T - 1], tap("conv_w1", i), dst[:, 1:T],
                                                    ALU.mult, ALU.add), it, per)
                        step(v.scalar_tensor_tensor(dst[:, 2:T], b[:, 0:T - 2], tap("conv_w0", i), dst[:, 2:T],
                                                    ALU.mult, ALU.add), it, per)
                        if n == 0:
                            dve.sem_inc(gate_ready, 1)
                    dve.wait_ge(silu_ready, it * 2 + (j + 1))
                    step(v.tensor_tensor(val[:, :], silu[:, :], val[:, :], ALU.mult), it, per)
                    v.tensor_scalar(hidden_at(h_hi, it, j), val[:, :], 1.0, None, ALU.mult).then_inc(high_done, 1)
                    dve.wait_ge(high_done, it * 2 + (j + 1))
                    v.tensor_tensor(hidden_at(h_lo, it, j), val[:, :], hidden_at(h_hi, it, j).bitcast(F32),
                                    ALU.subtract).then_inc(hidden_ready, 1)
                    dve.wait_ge(hidden_ready, it * 2 + (j + 1))
            assert steps[0] - at_loop == per
            steps[0] += per * (FC // 2 - 1)
            add_tiles("down1", "final1")
            rsqrt("final1")
            for k in range(DC + 1):
                if k < DC:
                    v.scalar_tensor_tensor(x[:, k, :], x[:, k, :], prm("norm_final_g", k), rstd[:, :], ALU.mult,
                                           ALU.mult).then_inc(x_ready, 1)
                if k:
                    scaled_low("pre1", "ffn1_pre_g", k - 1)
            scaled_done("pre1")

            def hiddens(stage, turn):
                first = UNIT[stage][0]
                slots = [gate, silu]
                with dve.Fori(0, FC // 2) as it:
                    for j in range(2):
                        (g, g_uses), (u, u_uses) = TILE[stage, 2 * j], TILE[stage, 2 * j + 1]
                        dve.wait_ge(unit_done, first + 2 * j + 1 + it * 4)
                        v.tensor_tensor(slots[j][:, :], bank[g][:, :], rstd[:, :], ALU.mult).then_inc(bank_free[g], 1)
                        dve.wait_ge(unit_done, first + 2 * j + 2 + it * 4)
                        v.tensor_tensor(val[:, :], bank[u][:, :], rstd[:, :], ALU.mult).then_inc(bank_free[u], 1)
                        dve.wait_ge(bank_free[u], u_uses + 1 + it)
                        dve.wait_ge(silu_ready, FC * turn + j + 1 + it * 2)
                        step(v.tensor_tensor(val[:, :], slots[j][:, :], val[:, :], ALU.mult), it, 2)
                        v.tensor_scalar(hidden_at(h_hi, it, j), val[:, :], 1.0, None, ALU.mult).then_inc(
                            high_done, 1)
                        dve.wait_ge(high_done, FC * turn + j + 1 + it * 2)
                        v.tensor_tensor(hidden_at(h_lo, it, j), val[:, :],
                                        hidden_at(h_hi, it, j).bitcast(F32), ALU.subtract).then_inc(
                            hidden_ready, 1)
                        dve.wait_ge(hidden_ready, FC * turn + j + 1 + it * 2)
                steps[0] += 2 * (FC // 2 - 1)

            def branch_kept(stage, square_stage):
                for k in range(DC):
                    add_square(square_stage, k)

            hiddens("up2", 1)
            branch_kept("down2", "post1")
            add_branch("post1", "ffn1_post_g", y, lambda k: tile_read("down2", k), x_ready, DC,
                       split=("mixpre", "mix_pre_g"))
            dve.sem_inc(chunk_ready, DC)
            invert("mixpre")
            make_diagonal()
            take_rstd("mixpre", rstd_mix)

            def take_tile2(n):
                name = TILES2[n]
                kind, t = name.rstrip("0123456789"), int(name[len(name.rstrip("0123456789")):] or 0)
                wait(tile_done("proj2", n))
                if kind in SPILLED:
                    s = SPILLED[kind] + t
                    if s >= 2:
                        dve.wait_ge(spill_out[s % 2], 16 * (s // 2))
                    dst = spill_slot[s % 2][:, :]
                elif kind == "qa":
                    if t >= 2:
                        dve.wait_ge(aux_ready, AUX["qlat", 2 * t - 3] + 1)
                    dst = qa[:, t % 2, :]
                elif kind == "i":
                    if t >= 2:
                        dve.wait_ge(aux_ready, AUX["vturn", t - 2] + 1)
                    dst = i_t[:, t % 2, :]
                else:
                    dst = {"ckv": ckv_raw[:, :], "kidx": kidx_raw[:, :], "widx": widx_t[:, :],
                           "qi": qidx[:, t, :]}[kind]
                v.tensor_tensor(dst, tile_bank("proj2", n)[:, :], rstd_mix[:, :], ALU.mult).then_inc(
                    tile_sem("proj2", n), 1)

            def norm_keys(name):
                n, src, dst, g = {"ckv": (0, ckv_raw, ckv, "kv_norm_g"),
                                  "kidx": (1, kidx_raw, kidx, "kidx_norm_g")}[name]
                rsqrt(name)
                wait(tile_read("proj2", n))
                v.scalar_tensor_tensor(dst[:, :], src[:, :], prm(g), rstd[:, :], ALU.mult, ALU.mult).then_inc(
                    norm_ready, 1)
                dve.wait_ge(norm_ready, n + 1)

            def top8(i):
                step(v.max(best[:, :], score[i][:, :]))
                step(v.match_replace(score[i][:, :], best[:, :], score[i][:, :], TAKEN))

            def selected(i):
                v.tensor_scalar(score[i][:, :], score[i][:, :], -2e38, NEG, ALU.is_gt, ALU.mult).then_inc(
                    selected_ready, 1)
                dve.wait_ge(selected_ready, QB - i)

            def index_step(s):
                i, h = IDX_STEPS[s]
                w = (i + 1) * P
                wait(aux_read("idx", s))
                if h == 0:
                    v.tensor_scalar(score[i][:, :], relu[:, s % 2, 0:w], widx[:, i, h:h + 1], None,
                                    ALU.mult).then_inc(relu_used, 1)
                else:
                    v.scalar_tensor_tensor(score[i][:, :], relu[:, s % 2, 0:w], widx[:, i, h:h + 1],
                                           score[i][:, :], ALU.mult, ALU.add).then_inc(relu_used, 1)
                dve.wait_ge(relu_used, s + 1)
                if h == DSA_HEADS - 1:
                    step(v.tensor_tensor(score[i][:, i * P:], score[i][:, i * P:], tri[:, :], ALU.add))
                if i < QB - 1:
                    for _r in range(2):
                        top8(i + 1)
                    if h == DSA_HEADS - 1:
                        selected(i + 1)
            dve.wait_ge(const2_loaded, 16 * 3)
            for n in range(TILES2.index("gate0")):
                take_tile2(n)
                for ev, m in AFTER2[n]:
                    if ev == "spread":
                        norm_keys(m)
                    elif ev == "wturn":
                        dve.wait_ge(aux_ready, AUX["wturn", 0] + 1)
                        v.tensor_scalar(widx[:, :, :],
                                        aux_bank("wturn", 0)[:, 0:32].rearrange("p (j h) -> p j h", j=QB),
                                        IDX_W_SCALE, None, ALU.mult).then_inc(aux_sem("wturn", 0), 1)
                        wait(aux_read("wturn", 0))
                    elif ev == "idx":
                        index_step(m)
            for _r in range(TOPK // 8):
                top8(1)
            selected(1)
            for a in range(DSA_STEPS + 4):
                if a < DSA_STEPS:
                    h, i = a // QB, a % QB
                    end, s = (i + 1) * P, a % 2
                    dve.wait_ge(bias_mask_ready, a + 1)
                    dve.wait_ge(aux_ready, AUX["logit", a] + 1)
                    if a >= 2:
                        dve.wait_ge(exp2_done, a - 1)
                    v.tensor_tensor(logit[:, s, 0:end], aux_bank("logit", a)[:, 0:end], bias_mask[s][:, 0:end],
                                    ALU.add).then_inc(aux_sem("logit", a), 1)
                if 1 <= a <= DSA_STEPS:
                    r = (a - 1) % 2
                    dve.wait_ge(exp2_done, a)
                    step(v.reciprocal(small[:, 28 + r:29 + r], small[:, 26 + r:27 + r]))
                if a < DSA_STEPS:
                    wait(aux_read("logit", a))
                    step(v.tensor_reduce(small[:, 6:7], logit[:, s, 0:end], AX_X, ALU.max))
                    v.tensor_scalar(small[:, 24 + s:25 + s], small[:, 6:7], -1.0, None, ALU.mult).then_inc(
                        logit_max, 1)
                if 1 <= a <= DSA_STEPS:
                    b = a - 1
                    end, s = (b % QB + 1) * P, b % 2
                    if b >= 2:
                        dve.wait_ge(aux_ready, AUX["turn2", b - 2] + 1)
                        dve.wait_ge(attn2_ready, b)
                    v.tensor_scalar(attn2[:, s, 0:end], prob2[:, s, 0:end], small[:, 28 + s:29 + s], None,
                                    ALU.mult).then_inc(attn2_ready, 1)
                if a < DSA_STEPS:
                    dve.wait_ge(logit_max, a + 1)
                if a >= 11 and a % 8 == 3:
                    t = (a - 11) // 8
                    dve.wait_ge(aux_ready, AUX["ya", t] + 1)
                    step(v.tensor_copy(ya[:, t, :], aux_bank("ya", t)[:, :]))
                    dve.sem_inc(aux_sem("ya", t), 1)
                    dve.sem_inc(chunk_ready, 1)
            dve.wait_ge(lam_exp, 2)
            step(v.tensor_scalar(small[:, 40:44], small[:, 36:40], -1.0, 1.0, ALU.mult, ALU.add))
            dve.wait_ge(const3_loaded, 32)
            step(v.memset(pair_d[:, :, :], 0.0))

            def make_keys(h):
                s = h % 2
                dve.wait_ge(h_loaded[s], 32 * (h // 2 + 1))
                if h:
                    dve.wait_ge(logf_ready, h)
                v.tensor_scalar(hf[:, s, :], hf[:, s, :], small[:, 40 + h:41 + h], small[:, 36 + h:37 + h],
                                ALU.mult, ALU.add).then_inc(f_ready, 1)
                dve.wait_ge(f_ready, h + 1)
                v.tensor_scalar(hk[:, s, :], hf[:, s, :], -1.0, 1.0, ALU.mult, ALU.add).then_inc(k_ready, 1)
                dve.wait_ge(k_ready, h + 1)

            def make_sums(h):
                dve.wait_ge(logf_ready, h + 1)
                for n in range(3):
                    sum_ = v.tensor_tensor_scan(run[:, h % 2, n, :], resets[:, n, :], logf[:, :], 0.0, ALU.mult,
                                                ALU.add)
                sum_.then_inc(sums_ready, 1)

            def make_qk(e):
                h, l = e // len(LEVELS), e % len(LEVELS)
                s, b = h % 2, LEVELS[l]
                part = lambda ap: ap.rearrange("p (n c) -> p n c", c=2 * b)
                dve.wait_ge(decay_ready, decays(h, l))
                if e >= 2:
                    dve.wait_ge(aux_ready, AUX["pair", (e - 2) // 9, (e - 2) % 9] + 1)
                to, d = part(qk[:, e % 2, :]), part(decay[:, e % 2, :])
                v.tensor_tensor(to[:, :, 0:b], part(hk[:, s, :])[:, :, 0:b], d[:, :, 0:b], ALU.mult)
                v.tensor_tensor(to[:, :, b:2 * b], part(hq[:, s, :])[:, :, b:2 * b], d[:, :, b:2 * b],
                                ALU.mult).then_inc(qk_ready, 1)

            def keep_pairs(name, h, level):
                dve.wait_ge(aux_ready, AUX[name] + 1)
                view = lambda ap: ap.rearrange("p (n t) -> p n t", n=QB)
                mask = masks[:, level:level + 1, :]
                v.copy_predicated(view(pair_d[:, h % 2, :]), mask.broadcast_to([P, QB, P]),
                                  view(aux_bank(*name)[:, :])).then_inc(aux_sem(*name), 1)
                wait(aux_read(*name))

            def split_for(t):
                u = UNIT["proj2"][0] + t + 3
                size = BLOCKS_OF[u] * P
                dve.wait_ge(unit_high, u + 1)
                dve.wait_ge(unit_split, u)
                v.tensor_tensor(w_lo[:, u % SLOTS, 0:size], raw[:, u % SLOTS, 0:size],
                                w_hi[:, u % SLOTS, 0:size].bitcast(F32), ALU.subtract).then_inc(unit_split, 1)

            make_keys(0)
            make_sums(0)
            for h in range(HEADS):
                if h >= 2:
                    dve.wait_ge(head_ready, HEADS + DSA_HEADS + h - 1)
                keep_pairs(("pair0", h), h, 0)
                for l in range(len(LEVELS)):
                    e = h * len(LEVELS) + l
                    make_qk(e)
                    if l >= 2:
                        keep_pairs(("pair", h, l - 2), h, l - 1)
                    if e:
                        for t in closed(FILL2[GAP2 + e - 3]):
                            split_for(t)
                    if l == 4 and h + 1 < HEADS:
                        make_keys(h + 1)
                    if l == 6 and h + 1 < HEADS:
                        make_sums(h + 1)
            for pieces in FILL2[GAP2 + HGRN_STEPS - 3:]:
                for t in closed(pieces):
                    split_for(t)
            for t in range(4):
                dve.wait_ge(hi_ready, SPLIT["y"] + t + 1)
                v.tensor_tensor(a_lo[:, t, :], ya[:, t, :], a_hi[:, t, :].bitcast(F32), ALU.subtract).then_inc(
                    act_ready, 1)
            dve.wait_ge(hg_loaded, 16 * HEADS)
            def scale_gates(m):
                dve.wait_ge(gates_loaded[m % 2], 32 * (m // 2 + 1))
                for n in range(2):
                    slot = gates_in[:, 2 * (m % 2) + n, :]
                    scaled = v.tensor_tensor(slot, slot, rstd_mix[:, :], ALU.mult)
                scaled.then_inc(gates_scaled, 1)

            for h in range(HEADS):
                if h == HEADS - 1:
                    scale_gates(0)
                dve.wait_ge(head_sq, 7 + h)
                step(v.tensor_tensor(oh[:, h, :], oh[:, h, :], hg[:, h, :], ALU.mult))
            norm_heads("hgrn", oh, lambda h: prm("hgrn_norm_g"), SPLIT["y"] + 4)
            for m in range(DC):
                c = SPLIT["merged"] + m
                dve.wait_ge(gates_open, 2 * m + 2)
                for n in range(2):
                    wait(tile_done("branch", 2 * m + n))
                    v.tensor_tensor(gated[:, n, :], gates_in[:, 2 * (m % 2) + n, :],
                                    tile_bank("branch", 2 * m + n)[:, :], ALU.mult).then_inc(
                        tile_sem("branch", 2 * m + n), 1)
                    wait(tile_read("branch", 2 * m + n))
                slot_free(c)
                v.tensor_tensor(chunk[:, c % 2, :], gated[:, 0, :], gated[:, 1, :], ALU.add).then_inc(
                    chunk_ready, 1)
                if m + 1 < DC:
                    scale_gates(m + 1)
                made(c)
                low(c, h_lo[:, m, :], h_hi[:, m, :])
            branch_kept("out", "postmix")
            add_branch("postmix", "mix_post_g", y, lambda k: tile_read("out", k), x_ready, 2 * DC,
                       split=("pre2", "ffn2_pre_g"))
            scaled_done("pre2")
            hiddens("up3", 2)
            for c in range(2):
                dve.wait_ge(p_loaded, 32)
                n = SPLIT["p"] + c
                slot_free(n)
                v.tensor_copy(chunk[:, n % 2, :], pe_in[:, c, :]).then_inc(chunk_ready, 1)
                made(n)
                low(n, a_hi[:, 2 + c, :], a_hi[:, c, :])
            branch_kept("down3", "post2")
            add_branch("post2", "ffn2_post_g", y, lambda k: tile_read("down3", k), x_ready, 3 * DC,
                       split=("plepre", "ple_pre_g"))
            scaled_done("plepre")
            slots = [gate, silu]
            for k in range(DC + 1):
                if k < DC:
                    wait(tile_done("ple", k))
                    v.tensor_tensor(slots[k % 2][:, :], tile_bank("ple", k)[:, :], rstd[:, :], ALU.mult).then_inc(
                        tile_sem("ple", k), 1)
                if k:
                    dve.wait_ge(ple_open, k)
                    wait(tile_read("pproj", k - 1))
                    v.tensor_tensor(p_proj[:, k - 1, :], p_proj[:, k - 1, :], slots[(k - 1) % 2][:, :],
                                    ALU.mult).then_inc(y_ready, 1)
                    dve.wait_ge(y_ready, k)
                if k >= 2:
                    add_square("plepost", k - 2)
            add_square("plepost", DC - 1)
            add_branch("plepost", "ple_post_g", p_proj, None, out_ready, 0)


def _units(w, blocks, columns=None):
    k, n = w.shape
    tiles = w.reshape(k // P, P, n // P, P).transpose(2, 0, 1, 3)
    parts = tiles.reshape(n // P, k // P // blocks, blocks, P, P)
    return parts.transpose(0, 1, 3, 2, 4).reshape(-1, P, blocks * P)


def _interleave(a, b, blocks):
    a, b = _units(a, blocks), _units(b, blocks)
    return np.stack([a, b], axis=1).reshape(-1, P, blocks * P)


def _cols(v):
    return np.asarray(v).reshape(-1, P).T


def _layout(i):
    w2 = i["w_in_2"][0]
    at = {}
    pos = 0
    for name, n in (("qa", 512), ("ckv", 128), ("qi", 512), ("kidx", 64), ("widx", 8), ("qh", 512), ("fh", 512),
                    ("i", 512), ("gh", 512), ("gate", 2048)):
        at[name] = pos
        pos += n

    def w2_cols(tile):
        name = tile.rstrip("0123456789")
        first = at[name] + P * int(tile[len(name):] or 0)
        if name == "kidx":
            return np.concatenate([w2[:, first:first + 64]] * 2, axis=1)
        return w2[:, first:first + P]

    w1 = i["w_in"][0]
    first1 = {"p": 0, "q": 512, "k": 1024, "v": 1536}
    proj1 = np.concatenate([w1[:, first1[kind] + h * P:first1[kind] + (h + 1) * P] for kind, h in TILES1], axis=1)
    up1 = i["w_up"][0]
    pproj = _units(i["w_ple_proj_2"][0], 2)
    arrays = {
        "w_proj1": _units(proj1, DC),
        "w_wo": _units(i["w_o"][0], DC),
        "w_up1": _interleave(up1[:, :FF], up1[:, FF:], DC),
        "w_down1": _units(i["w_down"][0], DOWN_CHUNKS),
        "w_up2": _interleave(i["ffn1_w_gate_2"][0], i["ffn1_w_up_2"][0], DC),
        "w_down2": _units(i["ffn1_w_down_2"][0], DOWN_CHUNKS),
        "w_proj2": _units(np.concatenate([w2_cols(t) for t in TILES2], axis=1), DC),
        "w_branch": _interleave(i["w_br_a_2"][0], i["w_br_b_2"][0], 4),
        "w_out": _units(i["w_out_2"][0], DC),
        "w_up3": _interleave(i["ffn2_w_gate_2"][0], i["ffn2_w_up_2"][0], DC),
        "w_down3": _units(i["ffn2_w_down_2"][0], DOWN_CHUNKS),
        "w_pproj": pproj.reshape(2, 4, P, 2 * P).transpose(0, 2, 1, 3).reshape(2, P, 8 * P),
        "w_ple": _units(i["w_ple_gate_2"][0], DC),
    }
    conv = i["conv_w"][0]
    inter = lambda v: np.stack([_cols(v[:FF]), _cols(v[FF:])], axis=2).reshape(P, -1)
    i_freq = (np.float32(10000.0) ** (-np.arange(0, 64, 2, dtype=np.float32) / np.float32(64))).astype(np.float32)
    par = {
        "norm_mix_g": _cols(i["norm_mix_g"]), "norm_ffn_g": _cols(i["norm_ffn_g"]),
        "norm_final_g": _cols(i["norm_final_g"]), "pool_scale": _cols(i["pool_scale"]),
        "attn_norm_g": _cols(i["attn_norm_g"]), "conv_w0": inter(conv[0]), "conv_w1": inter(conv[1]),
        "conv_w2": inter(conv[2]), "conv_b": inter(i["conv_b"][0]),
        "ffn1_pre_g": _cols(i["ffn1_pre_g_2"]), "ffn1_post_g": _cols(i["ffn1_post_g_2"]),
        "mix_pre_g": _cols(i["mix_pre_g_2"]), "mix_post_g": _cols(i["mix_post_g_2"]),
        "kv_norm_g": _cols(i["kv_norm_g_2"]),
        "kidx_norm_g": _cols(np.concatenate([i["kidx_norm_g_2"][0]] * 2)),
        "hgrn_norm_g": _cols(i["hgrn_norm_g_2"]), "b_gate": _cols(i["b_gate_2"]),
        "ffn2_pre_g": _cols(i["ffn2_pre_g_2"]), "ffn2_post_g": _cols(i["ffn2_post_g_2"]),
        "ple_pre_g": _cols(i["ple_pre_g_2"]), "ple_post_g": _cols(i["ple_post_g_2"]),
        "hgrn_lb0": _cols(i["hgrn_lb_2"][0]), "hgrn_lb1": _cols(i["hgrn_lb_2"][1]),
        "inv_freq": _cols(np.tile(i_freq, 4)), "eps": np.full((P, 1), EPS, np.float32),
    }
    arrays["par"] = np.concatenate([par[name] for name in PARAMS], axis=1)
    arrays["xt"] = i["x"][0].T.reshape(DC, P, T)
    arrays["pt"] = i["p_2"][0, 0].T.reshape(2, P, T)
    arrays["positions"] = i["positions"]
    arrays["pool_w"] = i["pool_w"][0].transpose(1, 0, 2)
    arrays["lambdas"] = np.concatenate([i[n] for n in ("lambda_q1", "lambda_k1", "lambda_q2", "lambda_k2")])
    arrays["rel"] = i["rel_bias_2"]
    arrays["wuk"] = i["w_uk_2"][0].transpose(2, 0, 1).reshape(64, 4, 2, P).transpose(2, 0, 1, 3).reshape(P, 4, P)
    arrays["wuv"] = i["w_uv_2"][0].transpose(1, 0, 2)
    arrays.update(constants())
    return {name: np.ascontiguousarray(a) for name, a in arrays.items()}


def kernel(**inputs):
    import concourse.bacc as bacc
    from concourse.bass_utils import run_bass_kernel_spmd

    nc = bacc.Bacc("TRN2", target_bir_lowering=False, num_devices=1)
    arrays = _layout({name: np.asarray(a) for name, a in inputs.items()})
    ins = {name: nc.dram_tensor(f"in_{name}", a.shape, mybir.dt.from_np(a.dtype), kind="ExternalInput").ap()
           for name, a in arrays.items()}
    spill = nc.dram_tensor("spill", (28, P, T), F32, kind="Internal").ap()
    bias_rows = nc.dram_tensor("bias_rows", (DSA_HEADS, P, BIAS_COLS), F32, kind="Internal").ap()
    out = nc.dram_tensor("out_t", (DC, P, T), F32, kind="ExternalOutput").ap()
    two_blocks(nc, ins, spill, bias_rows, out)
    result = run_bass_kernel_spmd(nc, [{f"in_{name}": a for name, a in arrays.items()}], core_ids=[0])
    return np.ascontiguousarray(result.results[0]["out_t"].reshape(D, T).T)[None]
```
